# Optimizing a Trainium2 kernel written in Bass

```python
import jax, jax.numpy as jnp
from jax import lax
import numpy as np

D_MODEL = 1024
BATCH = 1
SEQ = 2048
DEPTH = 1

GRID_W = 64
CTX_LEN = 256
M_HEADS = 4
M_HEAD_DIM = D_MODEL // M_HEADS
M_WIDTH = M_HEADS * M_HEAD_DIM
P_GROUPS = 4
P_WIDTH = D_MODEL // 2
P_GROUP_DIM = P_WIDTH // P_GROUPS
POOL_WINDOWS = (2, 4, 8, 16)
CHUNK = 128
N_DIR = 2
N_GATE_COLS = N_DIR * 2 * M_HEADS
N_BRANCH = 2
IN_SIZES = (M_WIDTH, M_WIDTH, M_WIDTH, M_WIDTH, M_WIDTH, N_GATE_COLS, P_WIDTH, P_WIDTH, N_BRANCH * D_MODEL)
IN_WIDTH = sum(IN_SIZES)
EPS = 1e-6
M_INIT = -1e30

kernel_name = 'hybrid_mlstm_pool_flow_block'

def _split_proj(p):
    names = ('q', 'k', 'v', 'o', 'z_m', 'gates', 'p', 'z_p', 'g_branch')
    offs = [int(o) for o in np.cumsum(IN_SIZES)[:-1]]
    return dict(zip(names, jnp.split(p, offs, axis=-1)))

def _rmsnorm(x, w):
    xf = x.astype(jnp.float32)
    y = xf * lax.rsqrt(jnp.mean(xf * xf, axis=-1, keepdims=True) + EPS)
    return (y * w.astype(jnp.float32)).astype(x.dtype)

def _adaln(cvec, w, b):
    m = jax.nn.silu(cvec) @ w + b
    return jnp.split(m, 3, axis=-1)

def _zero_state(b):
    return (jnp.zeros((b, M_HEADS, M_HEAD_DIM, M_HEAD_DIM), jnp.float32),
            jnp.zeros((b, M_HEADS, M_HEAD_DIM), jnp.float32),
            jnp.full((b, M_HEADS), M_INIT, jnp.float32))

def _mlstm_inputs(parts, gate_b):
    b, t, _ = parts['q'].shape
    def heads(a):
        return a.reshape(b, t, M_HEADS, M_HEAD_DIM).transpose(0, 2, 1, 3).astype(jnp.float32)
    q = heads(parts['q'])
    k = heads(parts['k']) * (M_HEAD_DIM ** -0.5)
    v = heads(parts['v'])
    pre = parts['gates'].astype(jnp.float32) + gate_b.astype(jnp.float32)
    pre = pre.reshape(b, t, N_DIR, 2, M_HEADS).transpose(2, 3, 0, 4, 1)
    log_i = pre[:, 0]
    log_f = jax.nn.log_sigmoid(pre[:, 1])
    return q, k, v, log_i, log_f

def _mlstm_chunk(carry, xs):
    C, n, m = carry
    q, k, v, b, li = xs
    L = q.shape[2]
    causal = jnp.tril(jnp.ones((L, L), dtype=bool))
    logw = jnp.where(causal, b[..., :, None] - b[..., None, :] + li[..., None, :], -jnp.inf)
    inter = b + m[..., None]
    m_t = jnp.maximum(inter, jnp.max(logw, axis=-1))
    w_intra = jnp.exp(logw - m_t[..., None])
    w_inter = jnp.exp(inter - m_t)
    s = jnp.einsum('bhtk,bhsk->bhts', q, k) * w_intra
    num = w_inter[..., None] * jnp.einsum('bhvk,bhtk->bhtv', C, q) + jnp.einsum('bhts,bhsv->bhtv', s, v)
    den = w_inter * jnp.einsum('bhk,bhtk->bht', n, q) + jnp.sum(s, axis=-1)
    h = num / jnp.maximum(jnp.abs(den), jnp.exp(-m_t))[..., None]
    b_end = b[..., -1]
    w_end = b_end[..., None] - b + li
    m_new = jnp.maximum(b_end + m, jnp.max(w_end, axis=-1))
    decay = jnp.exp(b_end + m - m_new)
    e = jnp.exp(w_end - m_new[..., None])
    C_new = decay[..., None, None] * C + jnp.einsum('bhs,bhsv,bhsk->bhvk', e, v, k)
    n_new = decay[..., None] * n + jnp.einsum('bhs,bhsk->bhk', e, k)
    return (C_new, n_new, m_new), h

def _mlstm_scan(q, k, v, log_i, log_f, state):
    b, h, t, d = q.shape
    nc = t // CHUNK
    def chunks(a):
        return jnp.moveaxis(a.reshape(a.shape[:2] + (nc, CHUNK) + a.shape[3:]), 2, 0)
    bcum = jnp.cumsum(chunks(log_f), axis=-1)
    state, out = lax.scan(_mlstm_chunk, state, (chunks(q), chunks(k), chunks(v), bcum, chunks(log_i)))
    return jnp.moveaxis(out, 0, 2).reshape(b, h, t, d), state

def _bi_mlstm(q, k, v, log_i, log_f, st_f, st_b):
    rev = lambda a: jnp.flip(a, axis=2)
    h_f, st_f = _mlstm_scan(q, k, v, log_i[0], log_f[0], st_f)
    h_b, st_b = _mlstm_scan(rev(q), rev(k), rev(v), rev(log_i[1]), rev(log_f[1]), st_b)
    return h_f + rev(h_b), st_f, st_b

def _mlstm_branch(h, parts, head_norm_w, branch_m_w):
    b, nh, t, d = h.shape
    hn = h * lax.rsqrt(jnp.mean(h * h, axis=-1, keepdims=True) + EPS)
    hn = hn.transpose(0, 2, 1, 3).reshape(b, t, M_WIDTH).astype(parts['o'].dtype) * head_norm_w
    y = hn * jax.nn.sigmoid(parts['o']) * jax.nn.silu(parts['z_m'])
    return y @ branch_m_w

def _box_mean(x, w, axis):
    L = x.shape[axis]
    cs = jnp.cumsum(x.astype(jnp.float32), axis=axis)
    cs = jnp.concatenate([jnp.zeros_like(lax.slice_in_dim(cs, 0, 1, axis=axis)), cs], axis=axis)
    pos = np.arange(L)
    lo = np.clip(pos - w // 2, 0, L)
    hi = np.clip(pos + w - w // 2, 0, L)
    s = jnp.take(cs, hi, axis=axis) - jnp.take(cs, lo, axis=axis)
    shape = [1] * x.ndim
    shape[axis] = L
    cnt = (hi - lo).astype(np.float32).reshape(shape)
    return (s / cnt).astype(x.dtype)

def _pool_branch(parts, grid_shape, axes, pool_w, pool_scale, branch_p_w):
    p = parts['p']
    b, t, _ = p.shape
    pg = p.reshape((b,) + grid_shape + (P_GROUPS, P_GROUP_DIM))
    groups = []
    for g, w in enumerate(POOL_WINDOWS):
        a = pg[..., g, :]
        for ax in axes:
            a = _box_mean(a, w, ax)
        groups.append(a)
    mixed = (jnp.stack(groups, axis=-2) - pg).reshape(b, t, P_GROUPS, P_GROUP_DIM)
    mixed = jnp.einsum('btgc,gcd->btgd', mixed, pool_w).reshape(b, t, P_WIDTH)
    y = mixed * pool_scale * jax.nn.silu(parts['z_p'])
    return y @ branch_p_w

def _merge(parts, y_m, y_p, out_w):
    g_m, g_p = jnp.split(parts['g_branch'], 2, axis=-1)
    return (jax.nn.sigmoid(g_m) * y_m + jax.nn.sigmoid(g_p) * y_p) @ out_w

def _hybrid_layer(x, xc, mod_x, mod_c, norm_w, in_w, gate_b, head_norm_w, pool_w, pool_scale,
                  branch_m_w, branch_p_w, out_w, update_ctx):
    b, t, _ = x.shape
    rows = t // GRID_W
    shift, scale, gate = [m[:, None, :] for m in mod_x]
    shift_c, scale_c, gate_c = mod_c
    parts_x = _split_proj((_rmsnorm(x, norm_w) * (1 + scale) + shift) @ in_w)
    parts_c = _split_proj((_rmsnorm(xc, norm_w) * (1 + scale_c) + shift_c) @ in_w)
    zero = _zero_state(b)
    qc, kc, vc, lic, lfc = _mlstm_inputs(parts_c, gate_b)
    h_c, st_f, st_b = _bi_mlstm(qc, kc, vc, lic, lfc, zero, zero)
    qx, kx, vx, lix, lfx = _mlstm_inputs(parts_x, gate_b)
    h_x, _, _ = _bi_mlstm(qx, kx, vx, lix, lfx, st_f, st_b)
    y_m = _mlstm_branch(h_x, parts_x, head_norm_w, branch_m_w)
    y_p = _pool_branch(parts_x, (rows, GRID_W), (1, 2), pool_w, pool_scale, branch_p_w)
    x = x + gate * _merge(parts_x, y_m, y_p, out_w)
    if update_ctx:
        y_mc = _mlstm_branch(h_c, parts_c, head_norm_w, branch_m_w)
        y_pc = _pool_branch(parts_c, (xc.shape[1],), (1,), pool_w, pool_scale, branch_p_w)
        xc = xc + gate_c * _merge(parts_c, y_mc, y_pc, out_w)
    return x, xc

def setup_inputs(seed: int = 0) -> dict:
    key = jax.random.key(seed)
    ks = jax.random.split(key, 20)
    def nrm(k, shape, s):
        return jax.random.normal(k, shape, jnp.float32) * s
    i_b = nrm(ks[8], (DEPTH, N_DIR, 1, M_HEADS), 0.1)
    f_b = jnp.linspace(3.0, 6.0, M_HEADS, dtype=jnp.float32) + nrm(ks[9], (DEPTH, N_DIR, 1, M_HEADS), 0.1)
    return {
        'x': nrm(ks[0], (BATCH, SEQ, D_MODEL), 1.0),
        'c': nrm(ks[1], (BATCH, D_MODEL), 1.0),
        'ctx': nrm(ks[2], (BATCH, CTX_LEN, D_MODEL), 1.0),
        'c_ctx': nrm(ks[3], (D_MODEL,), 1.0),
        'norm_w': 1.0 + nrm(ks[4], (DEPTH, D_MODEL), 0.02),
        'ada_w': nrm(ks[5], (DEPTH, D_MODEL, 3 * D_MODEL), 0.5 * D_MODEL ** -0.5),
        'ada_b': nrm(ks[6], (DEPTH, 3 * D_MODEL), 0.01),
        'in_w': nrm(ks[7], (DEPTH, D_MODEL, IN_WIDTH), D_MODEL ** -0.5),
        'gate_b': jnp.concatenate([i_b, f_b], axis=2).reshape(DEPTH, N_GATE_COLS),
        'head_norm_w': 1.0 + nrm(ks[10], (DEPTH, M_WIDTH), 0.02),
        'pool_w': nrm(ks[11], (DEPTH, P_GROUPS, P_GROUP_DIM, P_GROUP_DIM), P_GROUP_DIM ** -0.5),
        'pool_scale': 1.0 + nrm(ks[12], (DEPTH, P_WIDTH), 0.1),
        'branch_m_w': nrm(ks[13], (DEPTH, M_WIDTH, D_MODEL), M_WIDTH ** -0.5),
        'branch_p_w': nrm(ks[14], (DEPTH, P_WIDTH, D_MODEL), P_WIDTH ** -0.5),
        'out_w': nrm(ks[15], (DEPTH, D_MODEL, D_MODEL), D_MODEL ** -0.5),
        'final_norm_w': 1.0 + nrm(ks[16], (D_MODEL,), 0.02),
    }

def reference(x, c, ctx, c_ctx, norm_w, ada_w, ada_b, in_w, gate_b, head_norm_w, pool_w, pool_scale,
              branch_m_w, branch_p_w, out_w, final_norm_w):
    xc = ctx
    for l in range(DEPTH):
        mod_x = _adaln(c, ada_w[l], ada_b[l])
        mod_c = _adaln(c_ctx, ada_w[l], ada_b[l])
        x, xc = _hybrid_layer(x, xc, mod_x, mod_c, norm_w[l], in_w[l], gate_b[l], head_norm_w[l],
                              pool_w[l], pool_scale[l], branch_m_w[l], branch_p_w[l], out_w[l],
                              l < DEPTH - 1)
    return _rmsnorm(x, final_norm_w)


_drawn_inputs = setup_inputs


def setup_inputs(seed=0):
    import zlib

    import numpy as np

    out = dict(_drawn_inputs(seed))
    spreads = {}
    factors = {'ctx': 22.337,
     'c_ctx': 39.923,
     'norm_w': 8.0,
     'ada_b': 8.0,
     'head_norm_w': 64.0,
     'pool_scale': 5.643,
     'final_norm_w': 8.224}
    for name, (base, spread) in spreads.items():
        noise = np.random.default_rng([zlib.crc32(name.encode()), seed]).standard_normal(out[name].shape)
        drawn = base * np.exp(spread * noise) if base else spread * noise
        out[name] = __import__('jax').numpy.asarray(drawn.astype(out[name].dtype))
    for name, factor in factors.items():
        out[name] = (out[name] * factor).astype(out[name].dtype)
    return out
```

```python
import numpy as np
from contextlib import ExitStack

import concourse.bass as bass
from concourse import mybir
from concourse.alu_op_type import AluOpType as ALU

FP32 = mybir.dt.float32
FP32R = mybir.dt.float32r
ACT = mybir.ActivationFunctionType

P = 128
D = 1024
KT = D // P
SEQ, CTX = 2048, 256
TOK = CTX + SEQ
NX, NC = SEQ // P, CTX // P
NCH = NX + NC
GRID_W = 64
GRID_H = SEQ // GRID_W
HEADS = 4
HD = D // HEADS
HB = HD // P
PW = D // 2
PG = 4
EPS = 1e-6
M_INIT = -1e30
Q0, K0, V0, O0, Z0 = (D * n for n in range(5))
GATE0 = 5 * D
NGATE = 16
POOL0 = GATE0 + NGATE
ZP0 = POOL0 + PW
GM0 = ZP0 + PW
GP0 = GM0 + D
TQ = 512
NTQ = SEQ // TQ
VW = HD + 2
NQ = 5


def f32(ap):
    return ap.bitcast(FP32)


def hybrid_block(nc, x, c, ctx, c_ctx, norm_w, ada_w, ada_b, in_w, gate_b, head_norm_w, pool_w,
                 pool_scale, branch_m_w, branch_p_w, out_w, final_norm_w, out):
    x, ctx, out = x[0], ctx[0], out[0]

    def scratch(name, shape):
        return nc.dram_tensor(name, shape, FP32, kind="Internal").ap()

    gates_d = scratch("gates_d", (NGATE, TOK))
    qk_d = scratch("qk_d", (HEADS, 2, HB, P, NCH, 2, P))
    kt_d = scratch("kt_d", (HEADS, NCH, P, HD))
    v_d = scratch("v_d", (HEADS, NCH, P, HB, 2, P))
    ends_d = scratch("ends_d", (2, 2, HEADS * NCH))
    mprev_d = scratch("mprev_d", (2, HEADS * NCH))
    negm_d = scratch("negm_d", (2, HEADS, NCH, P))
    cols_d = scratch("cols_d", (P, 2, NCH, NQ, HEADS))
    u_d = scratch("u_d", (KT, P, SEQ))
    gm_d = scratch("gm_d", (KT, P, SEQ))
    gp_d = scratch("gp_d", (KT, P, SEQ))
    xe_d = scratch("xe_d", (2, P, KT, SEQ // 2))
    p_d = scratch("p_d", (PG, P, SEQ))
    zp_d = scratch("zp_d", (PG, P, SEQ))
    mix_d = scratch("mix_d", (PG, P, SEQ))
    h_d = scratch("h_d", (2, NX, P, D))

    in_v = in_w[0].rearrange("(j p) n -> p j n", p=P)
    ada_v = ada_w[0].rearrange("(j p) n -> p j n", p=P)

    with ExitStack() as top:
        def sem(name):
            return top.enter_context(nc.semaphore(name))

        def keep(name, shape, dt=FP32):
            return top.enter_context(nc.sbuf_tensor(name, shape, dt))

        ident = keep("ident", [P, P])
        vcol = keep("vcol", [P, 64])
        mgate = keep("mgate", [P, KT])
        bank = [top.enter_context(nc.psum_tensor(f"bank{n}", [P, TQ], FP32)) for n in range(8)]
        HALF = SEQ // 2
        late = top.enter_context(ExitStack())
        early = top.enter_context(ExitStack())
        xlate = [late.enter_context(nc.sbuf_tensor(f"xlate{n}", [P, KT, HALF], FP32R)) for n in range(2)]
        xearly = [early.enter_context(nc.sbuf_tensor(f"xearly{n}", [P, KT, CTX + HALF], FP32R)) for n in range(2)]

        def xn(part, k, t0, w):
            if t0 >= CTX + HALF:
                return xlate[part][:, k, t0 - CTX - HALF:t0 - CTX - HALF + w]
            return xearly[part][:, k, t0:t0 + w]


        VR = {"norm": 0, "ada": 8, "head": 32, "pool": 40, "c": 44, "cc": 52}
        NV = 60
        AS = 256
        NAS = 3 * D // AS
        groups = [(CTX // P, 0, 1, ctx)] + [(TQ // P, CTX + TQ * n, 0, x) for n in range(NTQ)]
        tiles = [(g, r) for g, (w, *_) in enumerate(groups) for r in range(w)]
        first = [sum(w for w, *_ in groups[:g]) for g in range(len(groups) + 1)]
        with ExitStack() as ph:
            def sb(name, shape, dt=FP32):
                return ph.enter_context(nc.sbuf_tensor(name, shape, dt))

            XS, YS = 8, 2
            vrow = sb("vrow", [NV, P])
            aw = sb("aw", [P, 2, KT, AS])
            xt = sb("xt", [P, XS, D])
            sq = sb("sq", [P, D])
            y = sb("y", [P, YS, TQ])
            ss = sb("ss", [P, NCH])
            ms = sb("ms", [P, NCH])
            rt = sb("rt", [P, NCH])
            rstd = sb("rstd", [P, NCH])
            th = sb("th", [P, 2 * KT])
            s1 = sb("s1", [P, 2 * KT])
            sc = sb("sc", [P, KT, 2])
            modA = sb("modA", [P, KT, 2])
            modB = sb("modB", [P, KT, 2])
            sc1 = sb("sc1", [P, KT, 2])

            v_loaded = sem("v_loaded"); aw_loaded = [sem(f"aw_loaded{n}") for n in range(2)]
            x_loaded = [sem(f"x_loaded{n}") for n in range(XS)]
            ident_made = sem("ident_made"); v_turned = sem("v_turned"); vcol_made = sem("vcol_made")
            c_tanh = sem("c_tanh"); c_ready = sem("c_ready"); aw_used = sem("aw_used")
            mod_dve = sem("mod_dve"); squared = sem("squared"); rooted = sem("rooted")
            norm_dve = sem("norm_dve"); x_normed = sem("x_normed"); x_turned = sem("x_turned")
            y_made = sem("y_made"); y_split = sem("y_split")
            block = ph.enter_context(nc.Block())

            @block.sync
            def _(sp):
                for key, src in (("norm", norm_w[0]), ("ada", ada_b[0]), ("head", head_norm_w[0]),
                                 ("pool", pool_scale[0]), ("c", c[0]), ("cc", c_ctx)):
                    rows = src.shape[0] // P
                    sp.dma_start(vrow[VR[key]:VR[key] + rows, :],
                                 src.rearrange("(a b) -> a b", b=P)).then_inc(v_loaded, 16)
                for n in range(NAS):
                    if n >= 2:
                        sp.wait_ge(aw_used, n - 1)
                    sp.dma_start(aw[:, n % 2], ada_v[:, :, n * AS:(n + 1) * AS]).then_inc(aw_loaded[n % 2], 16)

            @block.gpsimd
            def _(pool):
                nc.gpsimd.memset(ident[:, :], 0.0).then_inc(ident_made, 1)
                pool.wait_ge(ident_made, 1)
                nc.gpsimd.affine_select(out=ident[:, :], in_=ident[:, :], compare_op=ALU.not_equal, fill=1.0,
                                        base=0, pattern=[[-1, P]], channel_multiplier=1).then_inc(ident_made, 1)
                for n, (g, r) in enumerate(tiles):
                    if n >= XS:
                        back = tiles[n - XS][0]
                        pool.wait_ge(x_turned, KT * (back + 1))
                    src = groups[g][3]
                    row = (n - first[g]) * P + (0 if g == 0 else groups[g][1] - CTX)
                    pool.dma_start(xt[:, n % XS, :], src[row:row + P, :]).then_inc(x_loaded[n % XS], 16)

            @block.tensor
            def _(pe):
                pe.wait_ge(ident_made, 2)
                pe.wait_ge(v_loaded, 16 * 6)
                pe.transpose(bank[0][:, 0:NV], vrow[:, :], ident[0:NV, 0:NV]).then_inc(v_turned, 1)
                pe.wait_ge(c_ready, 1)

                def modulation(n):
                    pe.wait_ge(aw_loaded[n % 2], 16 * (n // 2 + 1))
                    for t in range(AS // P):
                        f = n * (AS // P) + t
                        for k in range(KT):
                            mm = pe.matmul(bank[1][:, 2 * f:2 * f + 2], aw[:, n % 2, k, t * P:(t + 1) * P],
                                           sc[:, k, :], start=(k == 0), stop=(k == KT - 1))
                    mm.then_inc(aw_used, 1)

                for n in range(NAS):
                    modulation(n)
                for g, (w, t0, kind, _) in enumerate(groups):
                    for j in range(KT):
                        m = KT * g + j
                        pe.wait_ge(x_normed, first[g + 1])
                        if m >= 2:
                            pe.wait_ge(y_made, m - 1)
                        for r in range(w):
                            n = first[g] + r
                            mm = pe.transpose(bank[2 + m % 2][:, r * P:(r + 1) * P],
                                              xt[:, n % XS, j * P:(j + 1) * P], ident[:, :])
                        mm.then_inc(x_turned, 1)

            @block.scalar
            def _(act):
                act.wait_ge(vcol_made, 1)
                act.activation(th[:, :], vcol[:, VR["c"]:VR["c"] + 2 * KT], ACT.Tanh, scale=0.5).then_inc(c_tanh, 1)

                def squares(g):
                    for n in range(first[g], first[g + 1]):
                        act.wait_ge(x_loaded[n % XS], 16 * (n // XS + 1))
                        if n >= 1:
                            act.wait_ge(squared, n)
                        act.activation(sq[:, :], xt[:, n % XS, :], ACT.Square,
                                       accum_out=ss[:, n:n + 1]).then_inc(squared, 1)

                def root(g):
                    act.wait_ge(norm_dve, 2 * g + 1)
                    a, b = first[g], first[g + 1]
                    act.activation(rt[:, a:b], ms[:, a:b], ACT.Sqrt).then_inc(rooted, 1)

                squares(0)
                root(0)
                for g, (w, t0, kind, _) in enumerate(groups):
                    if g + 1 < len(groups):
                        squares(g + 1)
                        root(g + 1)
                    for j in range(KT):
                        m = KT * g + j
                        act.wait_ge(x_turned, m + 1)
                        if g == 0 and j == 0:
                            act.wait_ge(mod_dve, 4)
                        if m >= YS:
                            act.wait_ge(y_split, 2 * (m - YS + 1))
                        act.activation(y[:, m % YS, 0:w * P], bank[2 + m % 2][:, 0:w * P], ACT.Identity,
                                       bias=modB[:, j, kind:kind + 1], scale=modA[:, j, kind:kind + 1]).then_inc(y_made, 1)

            @block.vector
            def _(dve):
                dve.wait_ge(v_turned, 1)
                dve.tensor_copy(vcol[:, 0:NV], bank[0][:, 0:NV]).then_inc(vcol_made, 1)
                dve.wait_ge(vcol_made, 1)
                dve.wait_ge(c_tanh, 1)
                dve.scalar_tensor_tensor(out=s1[:, :], in0=th[:, :], scalar=1.0,
                                         in1=vcol[:, VR["c"]:VR["c"] + 2 * KT], op0=ALU.add,
                                         op1=ALU.mult).then_inc(vcol_made, 1)
                dve.wait_ge(vcol_made, 2)
                dve.tensor_scalar(sc[:, :, :], s1[:, :].rearrange("p (a j) -> p j a", a=2), 0.5, None,
                                  ALU.mult).then_inc(c_ready, 1)

                def scales(g):
                    a, b = first[g], first[g + 1]
                    dve.wait_ge(squared, b)
                    dve.tensor_scalar(ms[:, a:b], ss[:, a:b], 1.0 / D, EPS, ALU.mult, ALU.add).then_inc(norm_dve, 1)
                    dve.wait_ge(rooted, g + 1)
                    dve.reciprocal(rstd[:, a:b], rt[:, a:b]).then_inc(norm_dve, 1)
                    dve.wait_ge(norm_dve, 2 * g + 2)
                    for n in range(a, b):
                        dve.tensor_scalar(xt[:, n % XS, :], xt[:, n % XS, :], rstd[:, n:n + 1], None,
                                          ALU.mult).then_inc(x_normed, 1)

                scales(0)
                dve.wait_ge(aw_used, NAS)
                mod = bank[1][:, 0:6 * KT].rearrange("p (f a) -> p f a", a=2)
                for a in range(2):
                    dve.tensor_tensor(modB[:, :, a], mod[:, 0:KT, a], vcol[:, VR["ada"]:VR["ada"] + KT],
                                      ALU.add)
                    last = dve.tensor_tensor(sc1[:, :, a], mod[:, KT:2 * KT, a],
                                             vcol[:, VR["ada"] + KT:VR["ada"] + 2 * KT], ALU.add)
                last.then_inc(mod_dve, 1)
                dve.tensor_tensor(mgate[:, :], mod[:, 2 * KT:3 * KT, 0],
                                  vcol[:, VR["ada"] + 2 * KT:VR["ada"] + 3 * KT], ALU.add).then_inc(mod_dve, 1)
                dve.wait_ge(mod_dve, 2)
                for a in range(2):
                    dve.scalar_tensor_tensor(out=modA[:, :, a], in0=sc1[:, :, a], scalar=1.0,
                                             in1=vcol[:, VR["norm"]:VR["norm"] + KT], op0=ALU.add,
                                             op1=ALU.mult).then_inc(mod_dve, 1)
                dve.tensor_scalar(mgate[:, :], mgate[:, :], 0.5, None, ALU.mult).then_inc(mod_dve, 1)
                for g, (w, t0, kind, _) in enumerate(groups):
                    if g + 1 < len(groups):
                        scales(g + 1)
                    for j in range(KT):
                        m = KT * g + j
                        dve.wait_ge(y_made, m + 1)
                        n = w * P
                        dve.tensor_copy(xn(0, j, t0, n), y[:, m % YS, 0:n]).then_inc(y_split, 1)
                        dve.wait_ge(y_split, 2 * m + 1)
                        dve.tensor_tensor(xn(1, j, t0, n), y[:, m % YS, 0:n], f32(xn(0, j, t0, n)),
                                          ALU.subtract).then_inc(y_split, 1)
                dve.tensor_scalar(vcol[:, VR["pool"]:VR["pool"] + PG], vcol[:, VR["pool"]:VR["pool"] + PG],
                                  0.5, None, ALU.mult)


        HC = HEADS * NCH
        with ExitStack() as ph:
            def sb(name, shape, dt=FP32):
                return ph.enter_context(nc.sbuf_tensor(name, shape, dt))

            wg = sb("wg", [P, KT, NGATE])
            wgh = sb("wgh", [P, KT, NGATE], FP32R)
            wgl = sb("wgl", [P, KT, NGATE], FP32R)
            gbias = sb("gbias", [NGATE, 1])
            grow = sb("grow", [NGATE, TQ])
            gi = [sb(f"gi{d}", [HC, P]) for d in range(2)]
            gf = [sb(f"gf{d}", [HC, P]) for d in range(2)]
            gb = [sb(f"gb{d}", [HC, P]) for d in range(2)]
            gt = [sb(f"gt{d}", [HC, P]) for d in range(2)]
            gm = [sb(f"gm{d}", [HC, P]) for d in range(2)]
            gq = [sb(f"gq{d}", [HC, NQ, P]) for d in range(2)]
            ones = sb("ones", [HC, P])
            zeros = sb("zeros", [HC, P])
            ce = [sb(f"ce{d}", [HEADS, 2, NCH]) for d in range(2)]
            cm = [sb(f"cm{d}", [HEADS, NCH]) for d in range(2)]
            mprev = [sb(f"mprev{d}", [HC, 1]) for d in range(2)]
            nmend = [sb(f"nmend{d}", [HC, 1]) for d in range(2)]
            colst = sb("colst", [P, 2, NCH, NQ, HEADS])
            mpb = [sb(f"mpb{d}", [HC, P]) for d in range(2)]
            R_LF, R_CUM, R_A, R_ENDS = 4, 6, 8, 10
            R_CARRY = R_ENDS + 6
            R_M = R_CARRY + 4
            R_NEGM = R_M + 4
            R_QUANT = R_NEGM + 6
            

            g_loaded = sem("g_loaded"); g_hi = sem("g_hi"); g_lo = sem("g_lo"); g_done = sem("g_done")
            g_row = sem("g_row"); g_stored = sem("g_stored"); g_back = sem("g_back"); r_act = sem("r_act")
            r_dve = sem("r_dve"); ends_st = sem("ends_st"); ends_ld = sem("ends_ld"); mp_st = sem("mp_st")
            mp_ld = sem("mp_ld"); negm_st = sem("negm_st"); q_turned = sem("q_turned"); q_cols = sem("q_cols")
            cols_st = sem("cols_st")
            block = ph.enter_context(nc.Block())
            pieces = [(0, CTX)] + [(CTX + TQ * n, TQ) for n in range(NTQ)]

            @block.sync
            def _(sp):
                sp.dma_start(wg[:, :, :], in_v[:, :, GATE0:GATE0 + NGATE]).then_inc(g_loaded, 16)
                sp.dma_start(gbias[:, :], gate_b[0].rearrange("(a b) -> a b", b=1)).then_inc(g_loaded, 16)
                for n, (t0, w) in enumerate(pieces):
                    sp.wait_ge(g_row, n + 1)
                    sp.dma_start(gates_d[:, t0:t0 + w], grow[:, 0:w]).then_inc(g_stored, 16)
                sp.wait_ge(g_stored, 16 * len(pieces))
                for d in range(2):
                    for k, dst in ((0, gi[d]), (1, gf[d])):
                        r = 2 * HEADS * d + HEADS * k
                        sp.dma_start(dst[:, :], gates_d[r:r + HEADS, :].rearrange("h (c t) -> (h c) t", t=P))\
                            .then_inc(g_back, 16)
                sp.wait_ge(r_dve, R_ENDS)
                for d in range(2):
                    e = P - 1 if d == 0 else 0
                    sp.dma_start(ends_d[d, 0].rearrange("(a b) -> a b", b=1), gm[d][:, e:e + 1]).then_inc(ends_st, 16)
                    sp.dma_start(ends_d[d, 1].rearrange("(a b) -> a b", b=1), gb[d][:, e:e + 1]).then_inc(ends_st, 16)
                sp.wait_ge(ends_st, 64)
                for d in range(2):
                    sp.dma_start(ce[d][:, :, :], ends_d[d].rearrange("q (h c) -> h q c", h=HEADS)).then_inc(ends_ld, 16)
                sp.wait_ge(r_dve, R_CARRY)
                for d in range(2):
                    sp.dma_start(mprev_d[d].rearrange("(h c) -> h c", h=HEADS), cm[d][:, :]).then_inc(mp_st, 16)
                sp.wait_ge(mp_st, 32)
                for d in range(2):
                    sp.dma_start(mprev[d][:, :], mprev_d[d].rearrange("(a b) -> a b", b=1)).then_inc(mp_ld, 16)
                sp.wait_ge(r_dve, R_NEGM)
                for d in range(2):
                    sp.dma_start(negm_d[d].rearrange("h c t -> (h c) t"), gt[d][:, :]).then_inc(negm_st, 16)
                sp.wait_ge(q_cols, 2 * NQ)
                sp.dma_start(cols_d, colst[:, :, :, :, :]).then_inc(cols_st, 16)
                sp.wait_ge(negm_st, 32)
                sp.wait_ge(cols_st, 16)

            @block.scalar
            def _(act):
                act.wait_ge(g_loaded, 32)
                act.activation(wgh[:, :, :], wg[:, :, :], ACT.Copy).then_inc(g_hi, 1)
                for n, (t0, w) in enumerate(pieces):
                    act.wait_ge(g_done, n + 1)
                    if n >= 1:
                        act.wait_ge(g_stored, 16 * n)
                    act.activation(grow[:, 0:w], bank[n % 2][0:NGATE, 0:w], ACT.Identity,
                                   bias=gbias[:, 0:1]).then_inc(g_row, 1)
                act.wait_ge(g_back, 64)
                for d in range(2):
                    act.activation(gt[d][:, :], gf[d][:, :], ACT.Abs).then_inc(r_act, 1)
                act.wait_ge(r_act, 2)
                for d in range(2):
                    act.activation(gm[d][:, :], gt[d][:, :], ACT.Exp, scale=-1.0).then_inc(r_act, 1)
                act.wait_ge(r_act, 4)
                for d in range(2):
                    act.activation(gb[d][:, :], gm[d][:, :], ACT.Ln, bias=1.0).then_inc(r_act, 1)
                act.wait_ge(r_dve, R_QUANT)
                for d in range(2):
                    act.activation(gq[d][:, 1, :], gm[d][:, :], ACT.Exp, bias=mprev[d][:, 0:1], scale=-1.0)
                    act.activation(gq[d][:, 2, :], gf[d][:, :], ACT.Exp, scale=-1.0)
                    act.activation(gq[d][:, 3, :], gi[d][:, :], ACT.Exp, bias=nmend[d][:, 0:1])
                    act.activation(gq[d][:, 4, :], mpb[d][:, :], ACT.Exp, bias=nmend[d][:, 0:1]).then_inc(r_act, 1)

            @block.vector
            def _(dve):
                dve.wait_ge(g_hi, 1)
                dve.tensor_tensor(wgl[:, :, :], wg[:, :, :], f32(wgh[:, :, :]), ALU.subtract).then_inc(g_lo, 1)
                dve.memset(ones[:, :], 1.0).then_inc(r_dve, 1)
                dve.memset(zeros[:, :], 0.0).then_inc(r_dve, 1)
                dve.wait_ge(r_dve, 2)
                dve.wait_ge(r_act, 6)
                for d in range(2):
                    dve.scalar_tensor_tensor(out=gf[d][:, :], in0=gf[d][:, :], scalar=0.0, in1=gb[d][:, :],
                                             op0=ALU.min, op1=ALU.subtract).then_inc(r_dve, 1)
                dve.wait_ge(r_dve, R_LF)
                fwd = [slice(None), slice(None, None, -1)]
                for d in range(2):
                    s = fwd[d]
                    dve.tensor_tensor_scan(gb[d][:, s], ones[:, :], gf[d][:, s], 0.0, ALU.mult,
                                           ALU.add).then_inc(r_dve, 1)
                dve.wait_ge(r_dve, R_CUM)
                for d in range(2):
                    dve.tensor_tensor(gi[d][:, :], gi[d][:, :], gb[d][:, :], ALU.subtract).then_inc(r_dve, 1)
                dve.wait_ge(r_dve, R_A)
                for d in range(2):
                    s = fwd[d]
                    dve.tensor_tensor_scan(gm[d][:, s], zeros[:, :], gi[d][:, s], -3e38, ALU.add,
                                           ALU.max).then_inc(r_dve, 1)
                dve.wait_ge(ends_ld, 32)
                for d in range(2):
                    order = list(range(NCH)) if d == 0 else list(range(NC - 1, -1, -1)) + list(range(NCH - 1, NC - 1, -1))
                    dve.memset(cm[d][:, order[0]:order[0] + 1], M_INIT).then_inc(r_dve, 1)
                    if d == 0:
                        dve.wait_ge(r_dve, R_ENDS + 1)
                        dve.tensor_tensor_scan(cm[0][:, 1:NCH], ce[0][:, 0, 0:NCH - 1], ce[0][:, 1, 0:NCH - 1],
                                               M_INIT, ALU.max, ALU.add).then_inc(r_dve, 1)
                    else:
                        dve.wait_ge(r_dve, R_ENDS + 3)
                        dve.tensor_tensor_scan(cm[1][:, 0:1], ce[1][:, 0, 1:2], ce[1][:, 1, 1:2],
                                               M_INIT, ALU.max, ALU.add).then_inc(r_dve, 1)
                        dve.wait_ge(r_dve, R_ENDS + 4)
                        dve.tensor_tensor_scan(cm[1][:, NCH - 1:NCH], ce[1][:, 0, 0:1], ce[1][:, 1, 0:1],
                                               cm[1][:, 0:1], ALU.max, ALU.add).then_inc(r_dve, 1)
                        dve.wait_ge(r_dve, R_ENDS + 5)
                        dve.tensor_tensor_scan(cm[1][:, NCH - 2:NC - 1:-1], ce[1][:, 0, NCH - 1:NC:-1],
                                               ce[1][:, 1, NCH - 1:NC:-1], cm[1][:, NCH - 1:NCH],
                                               ALU.max, ALU.add).then_inc(r_dve, 1)
                dve.wait_ge(mp_ld, 32)
                for d in range(2):
                    dve.tensor_scalar(gm[d][:, :], gm[d][:, :], mprev[d][:, 0:1], None, ALU.max).then_inc(r_dve, 1)
                    dve.tensor_scalar(mpb[d][:, :], zeros[:, :], mprev[d][:, 0:1], None, ALU.add).then_inc(r_dve, 1)
                dve.wait_ge(r_dve, R_M)
                for d in range(2):
                    e = P - 1 if d == 0 else 0
                    dve.tensor_scalar(gt[d][:, :], gm[d][:, :], -1.0, None, ALU.mult).then_inc(r_dve, 1)
                    dve.tensor_scalar(nmend[d][:, :], gm[d][:, e:e + 1], -1.0, None, ALU.mult).then_inc(r_dve, 1)
                for d in range(2):
                    dve.tensor_tensor(gf[d][:, :], gb[d][:, :], gm[d][:, :], ALU.add).then_inc(r_dve, 1)
                    dve.tensor_copy(gq[d][:, 0, :], gi[d][:, :]).then_inc(r_dve, 1)
                dve.wait_ge(r_dve, R_NEGM + 4)
                for d in range(2):
                    dve.tensor_scalar(gf[d][:, :], gf[d][:, :], -88.0, None, ALU.max).then_inc(r_dve, 1)
                for n in range(2 * NQ):
                    d, q = n // NQ, n % NQ
                    dve.wait_ge(q_turned, n + 1)
                    dve.tensor_copy(colst[:, d, :, q, :],
                                    bank[2 + n % 2][:, 0:HC].rearrange("p (h c) -> p c h", h=HEADS)).then_inc(q_cols, 1)

            @block.tensor
            def _(pe):
                pe.wait_ge(g_lo, 1)
                for n, (t0, w) in enumerate(pieces):
                    if n >= 2:
                        pe.wait_ge(g_row, n - 1)
                    for k in range(KT):
                        for n3, (a, b) in enumerate(((wgh, 0), (wgh, 1), (wgl, 0))):
                            mm = pe.matmul(bank[n % 2][0:NGATE, 0:w], a[:, k, :], xn(b, k, t0, w),
                                           start=(k == 0 and n3 == 0), stop=(k == KT - 1 and n3 == 2))
                    mm.then_inc(g_done, 1)
                pe.wait_ge(r_act, 8)
                for n in range(2 * NQ):
                    d, q = n // NQ, n % NQ
                    if n >= 2:
                        pe.wait_ge(q_cols, n - 1)
                    pe.transpose(bank[2 + n % 2][:, 0:HC], gq[d][:, q, :], ident[0:HC, 0:HC]).then_inc(q_turned, 1)

        with ExitStack() as ph:
            def sb(name, shape, dt=FP32):
                return ph.enter_context(nc.sbuf_tensor(name, shape, dt))

            wraw = sb("wraw", [P, 2, KT, P])
            wh = sb("wh", [P, 2, KT, P], FP32R)
            wl = sb("wl", [P, 2, KT, P], FP32R)
            qks = sb("qks", [P, 2, 4, 2, P], FP32R)
            ymaj = sb("ymaj", [P, 2, TQ])
            kts = sb("kts", [P, 2, 4, P])
            vs = sb("vs", [P, 2, 4, 2, P], FP32R)
            pzs = sb("pzs", [P, 2, TQ])
            tz = sb("tz", [P, TQ])

            w_loaded = [sem(f"w_loaded{n}") for n in range(2)]
            w_hi = sem("w_hi"); w_lo = sem("w_lo")
            piece_done = sem("piece_done"); piece_read = sem("piece_read")
            qk_hi = sem("qk_hi"); qk_stored = [sem(f"qk_stored{n}") for n in range(2)]
            y_copied = sem("y_copied"); turned = sem("turned")
            turned_read = sem("turned_read"); v_hi = sem("v_hi")
            kt_stored = [sem(f"kt_stored{n}") for n in range(2)]
            v_stored = [sem(f"v_stored{n}") for n in range(2)]
            pz_stored = [sem(f"pz_stored{n}") for n in range(2)]
            tz_made = sem("tz_made"); xe_stored = sem("xe_stored")

            UNITS = [(t, kind) for t in range(HB) for kind in "qkv"] + [(0, "p"), (0, "s")]
            OFF = {"q": (Q0, HD), "k": (K0, HD), "v": (V0, HD), "p": (POOL0, P), "s": (ZP0, P)}
            cpiece, xpieces = (0, CTX), [(CTX + TQ * n, TQ) for n in range(NTQ)]
            PIECES = [(u, t, kind, t0, w) for u, (t, kind) in enumerate(UNITS)
                      for t0, w in ([cpiece] if kind in "kv" else []) + xpieces]
            NU, NPC = len(UNITS), len(PIECES)
            nqk = [sum(p[2] in "qk" for p in PIECES[:m]) for m in range(NPC + 1)]
            ntr = [sum(p[2] in "kv" for p in PIECES[:m]) for m in range(NPC + 1)]
            nk = [sum(p[2] == "k" for p in PIECES[:m]) for m in range(NPC + 1)]
            nv = [sum(p[2] == "v" for p in PIECES[:m]) for m in range(NPC + 1)]
            def unit_end(u):
                return NPC + 1 + max(m for m in range(NPC) if PIECES[m][0] == u)

            npz = [sum(p[2] in "ps" for p in PIECES[:m]) for m in range(NPC + 1)]
            assert NU % 2 == 0 and NPC % 4 == 0 and nqk[-1] % 2 == 0 and ntr[-1] % 2 == 0 and nk[-1] % 2 == 0
            block = ph.enter_context(nc.Block())

            def heads(eng, body):
                with eng.Fori(0, HEADS - 1) as i:
                    body(i, True)
                body(HEADS - 1, False)

            @block.sync
            def _(sp):
                def tile(i, u):
                    t, kind = UNITS[u % NU]
                    first_col, per_head = OFF[kind]
                    sp.wait_ge(w_hi, i * NU + (u + 1))
                    sp.wait_ge(w_lo, i * NU + (u + 1))
                    sp.dma_start(wraw[:, u % 2],
                                 in_v[:, :, bass.ds(i * per_head + (first_col + t * P + (u // NU) * per_head), P)])\
                        .then_inc(w_loaded[u % 2], 16)

                def store_turned(i, m):
                    u, t, kind, t0, w = PIECES[m]
                    r, cw, c0 = ntr[m], w // P, t0 // P
                    sp.wait_ge(turned_read, i * ntr[-1] + (r + 1 + 2))
                    if kind == "k":
                        sp.dma_start(kt_d[i, c0:c0 + cw, :, t * P:(t + 1) * P].rearrange("c p f -> p c f"),
                                     kts[:, nk[m] % 2, 0:cw]).then_inc(kt_stored[nk[m] % 2], 16)
                    else:
                        sp.dma_start(v_d[i, c0:c0 + cw, :, t].rearrange("c p a f -> p c (a f)"),
                                     f32(vs[:, nv[m] % 2, 0:cw]).rearrange("p c a f -> p c (a f)"))\
                            .then_inc(v_stored[nv[m] % 2], 16)

                def body(i, ahead):
                    for m, (u, t, kind, t0, w) in enumerate(PIECES):
                        if (m == 0 or PIECES[m - 1][0] != u) and (u + 3 < NU or ahead):
                            tile(i, u + 3)
                        cw, c0 = w // P, t0 // P
                        if kind in "qk":
                            a = nqk[m]
                            sp.wait_ge(piece_read, i * NPC + (m + 1 + 4))
                            sp.dma_start(qk_d[i, "qk".index(kind), t, :, c0:c0 + cw].rearrange("p c a t -> p (c a t)"),
                                         f32(qks[:, a % 2, 0:cw]).rearrange("p c a t -> p (c a t)"))\
                                .then_inc(qk_stored[a % 2], 16)
                        if kind in "ps":
                            a = npz[m]
                            sp.wait_ge(piece_read, i * NPC + (m + 1 + 4))
                            sp.dma_start((p_d if kind == "p" else zp_d)[i, :, t0 - CTX:t0 - CTX + w],
                                         pzs[:, a % 2, 0:w]).then_inc(pz_stored[a % 2], 16)
                        if m >= 1 and PIECES[m - 1][2] in "kv":
                            store_turned(i, m - 1)

                for u in range(3):
                    tile(0, u)
                heads(sp, body)
                for n in range(2):
                    sp.wait_ge(pz_stored[n], 16 * HEADS * npz[-1] // 2)
                    sp.wait_ge(qk_stored[n], 16 * HEADS * nqk[-1] // 2)
                    sp.wait_ge(kt_stored[n], 16 * HEADS * nk[-1] // 2)
                    sp.wait_ge(v_stored[n], 16 * HEADS * nv[-1] // 2)

            @block.gpsimd
            def _(pool):
                for part in range(2):
                    pool.dma_start(xe_d[part], f32(xearly[part][:, :, CTX:CTX + HALF])).then_inc(xe_stored, 16)
                pool.wait_ge(xe_stored, 32)

            @block.tensor
            def _(pe):
                pe.sem_inc(piece_done, NPC)
                pe.sem_inc(turned, 2)

                def turn(i, m):
                    u, t, kind, t0, w = PIECES[m]
                    r = ntr[m]
                    if kind == "k":
                        pe.wait_ge(y_copied, i * nk[-1] + (nk[m] + 1))
                    else:
                        pe.wait_ge(piece_read, i * NPC + (m + 1 + 4))
                    pe.wait_ge(turned_read, i * ntr[-1] + (r + 1))
                    for b in range(w // P):
                        mm = pe.transpose(bank[4 + r % 2][:, b * P:(b + 1) * P],
                                          ymaj[:, r % 2, b * P:(b + 1) * P], ident[:, :])
                    mm.then_inc(turned, 1)

                with pe.Fori(0, HEADS) as i:
                    for m, (u, t, kind, t0, w) in enumerate(PIECES):
                        if m == 0 or PIECES[m - 1][0] != u:
                            pe.wait_ge(w_hi, i * NU + (u + 1 + 2))
                            pe.wait_ge(w_lo, i * NU + (u + 1 + 2))
                        pe.wait_ge(piece_read, i * NPC + (m + 1))
                        for k in range(KT):
                            for n, (a, b) in enumerate(((wh, 0), (wh, 1), (wl, 0))):
                                mm = pe.matmul(bank[m % 4][:, 0:w], a[:, u % 2, k, :], xn(b, k, t0, w),
                                               start=(k == 0 and n == 0), stop=(k == KT - 1 and n == 2))
                        mm.then_inc(piece_done, 1)
                        if m >= 1 and PIECES[m - 1][2] in "kv":
                            turn(i, m - 1)

            @block.scalar
            def _(act):
                act.sem_inc(w_hi, 2)

                def turned_hi(i, m):
                    u, t, kind, t0, w = PIECES[m]
                    if kind == "v":
                        r, a, cw = ntr[m], nv[m], w // P
                        act.wait_ge(turned, i * ntr[-1] + (r + 1 + 2))
                        act.wait_ge(v_stored[a % 2], i * (16 * nv[-1] // 2) + 16 * (a // 2))
                        act.activation(vs[:, a % 2, 0:cw, 0, :],
                                       bank[4 + r % 2][:, 0:w].rearrange("p (c t) -> p c t", t=P),
                                       ACT.Copy).then_inc(v_hi, 1)

                def split_hi(i, u):
                    act.wait_ge(w_loaded[u % 2], i * (16 * NU // 2) + 16 * (u // 2 + 1))
                    if u >= 2:
                        act.wait_ge(piece_done, i * NPC + unit_end(u - 2))
                    act.activation(wh[:, u % 2], wraw[:, u % 2], ACT.Copy).then_inc(w_hi, 1)

                split_hi(0, 0)
                split_hi(0, 1)

                def body(i, ahead):
                    for m, (u, t, kind, t0, w) in enumerate(PIECES):
                        scale = HD ** -0.5 if kind == "k" else 1.0
                        if kind in "qk":
                            a, cw = nqk[m], w // P
                            act.wait_ge(piece_done, i * NPC + (NPC + m + 1))
                            if kind == "k":
                                act.wait_ge(turned, i * ntr[-1] + (ntr[m] + 1))
                                act.activation(ymaj[:, ntr[m] % 2, 0:w], bank[m % 4][:, 0:w], ACT.Copy,
                                               scale=scale).then_inc(y_copied, 1)
                            act.wait_ge(qk_stored[a % 2], i * (16 * nqk[-1] // 2) + 16 * (a // 2))
                            act.activation(qks[:, a % 2, 0:cw, 0, :],
                                           bank[m % 4][:, 0:w].rearrange("p (c t) -> p c t", t=P),
                                           ACT.Copy, scale=scale).then_inc(qk_hi, 1)
                        if kind == "s":
                            act.wait_ge(piece_done, i * NPC + (NPC + m + 1))
                            act.wait_ge(piece_read, i * NPC + (m + 4))
                            act.activation(tz[:, 0:w], bank[m % 4][:, 0:w], ACT.Tanh, scale=0.5).then_inc(tz_made, 1)
                        if m >= 1 and PIECES[m - 1][2] in "kv":
                            turned_hi(i, m - 1)
                        if (m + 1 == NPC or PIECES[m + 1][0] != u) and (u + 2 < NU or ahead):
                            split_hi(i, u + 2)

                heads(act, body)

            @block.vector
            def _(dve):
                dve.sem_inc(w_lo, 2)
                dve.sem_inc(piece_read, 4)
                dve.sem_inc(turned_read, 2)

                def turned_lo(i, m):
                    u, t, kind, t0, w = PIECES[m]
                    r, cw = ntr[m], w // P
                    src = bank[4 + r % 2][:, 0:w].rearrange("p (c t) -> p c t", t=P)
                    if kind == "k":
                        a = nk[m]
                        dve.wait_ge(turned, i * ntr[-1] + (r + 1 + 2))
                        dve.wait_ge(kt_stored[a % 2], i * (16 * nk[-1] // 2) + 16 * (a // 2))
                        dve.tensor_copy(kts[:, a % 2, 0:cw], src).then_inc(turned_read, 1)
                    else:
                        a = nv[m]
                        dve.wait_ge(v_hi, i * nv[-1] + (a + 1))
                        dve.tensor_tensor(vs[:, a % 2, 0:cw, 1, :], src, f32(vs[:, a % 2, 0:cw, 0, :]),
                                          ALU.subtract).then_inc(turned_read, 1)

                def split_lo(i, u):
                    dve.wait_ge(w_hi, i * NU + (u + 1 + 2))
                    dve.tensor_tensor(wl[:, u % 2], wraw[:, u % 2], f32(wh[:, u % 2]), ALU.subtract).then_inc(w_lo, 1)

                split_lo(0, 0)
                split_lo(0, 1)

                def body(i, ahead):
                    for m, (u, t, kind, t0, w) in enumerate(PIECES):
                        if kind in "qk":
                            a, cw = nqk[m], w // P
                            dve.wait_ge(qk_hi, i * nqk[-1] + (a + 1))
                            dve.scalar_tensor_tensor(
                                out=qks[:, a % 2, 0:cw, 1, :],
                                in0=bank[m % 4][:, 0:w].rearrange("p (c t) -> p c t", t=P),
                                scalar=HD ** -0.5 if kind == "k" else 1.0, in1=f32(qks[:, a % 2, 0:cw, 0, :]),
                                op0=ALU.mult, op1=ALU.subtract).then_inc(piece_read, 1)
                        elif kind in "ps":
                            a = npz[m]
                            dve.wait_ge(pz_stored[a % 2], i * (16 * npz[-1] // 2) + 16 * (a // 2))
                            if kind == "p":
                                dve.wait_ge(piece_done, i * NPC + (NPC + m + 1))
                                dve.tensor_copy(pzs[:, a % 2, 0:w], bank[m % 4][:, 0:w]).then_inc(piece_read, 1)
                            else:
                                dve.wait_ge(tz_made, i * NTQ + (a - NTQ + 1))
                                dve.scalar_tensor_tensor(out=pzs[:, a % 2, 0:w], in0=tz[:, 0:w], scalar=1.0,
                                                         in1=bank[m % 4][:, 0:w], op0=ALU.add,
                                                         op1=ALU.mult).then_inc(piece_read, 1)
                        else:
                            dve.wait_ge(piece_done, i * NPC + (NPC + m + 1))
                            dve.wait_ge(turned, i * ntr[-1] + (ntr[m] + 1))
                            dve.tensor_copy(ymaj[:, ntr[m] % 2, 0:w], bank[m % 4][:, 0:w]).then_inc(piece_read, 1)
                        if m >= 1 and PIECES[m - 1][2] in "kv":
                            turned_lo(i, m - 1)
                        if (m + 1 == NPC or PIECES[m + 1][0] != u) and (u + 2 < NU or ahead):
                            split_lo(i, u + 2)

                heads(dve, body)

        early.close()
        with ExitStack() as ph:
            def sb(name, shape, dt=FP32):
                return ph.enter_context(nc.sbuf_tensor(name, shape, dt))

            wraw = sb("wraw4", [P, 2, KT, P])
            wh = sb("wh4", [P, 2, KT, P], FP32R)
            wl = sb("wl4", [P, 2, KT, P], FP32R)
            tanh_o = sb("tanh_o", [P, 2, TQ])
            tanh_z = sb("tanh_z", [P, TQ])
            zgate = sb("zgate", [P, TQ])
            ustage = sb("ustage", [P, 2, TQ])
            gstage = sb("gstage", [P, 2, TQ])
            NCHAIN = 2 * HEADS
            state = sb("state", [P, NCHAIN, HB, VW])
            state_h = sb("state_h", [P, 2, HB, VW], FP32R)
            state_l = sb("state_l", [P, 2, HB, VW], FP32R)
            qk_t = sb("qk_t", [P, 2, 2, HB, 2, P], FP32R)
            v_t = sb("v_t", [P, 2, 2, VW], FP32R)
            kt_t = sb("kt_t", [P, 2, HD])
            nm = sb("nm", [P, 2, 2, HEADS, P])
            cmask = sb("cmask", [P, 2, P])
            cols = sb("cols", [P, 2, NCH, NQ * HEADS])
            ccol = sb("ccol", [P, 2, 2, NQ, HEADS])
            wexp = sb("wexp", [P, 2, P])
            pf = sb("pf", [P, 2, P])
            p_h = sb("p_h", [P, 2, P], FP32R)
            p_l = sb("p_l", [P, 2, P], FP32R)
            ek_h = sb("ek_h", [P, 2, HD], FP32R)
            ek_l = sb("ek_l", [P, 2, HD], FP32R)
            ysb = sb("ysb", [P, 2, VW])
            num = sb("num", [P, 2, VW])
            den = sb("den", [P, 2, 3])
            hout = sb("hout", [P, 2, HD])
            PADR = GRID_H + max(2, 16)
            pool_a = sb("pool_a", [P, PADR * GRID_W])
            pool_b = sb("pool_b", [P, PADR * GRID_W])
            icnt = sb("icnt", [P, 2, GRID_W])

            w_loaded = [sem(f"w4_loaded{n}") for n in range(2)]
            w_hi = sem("w4_hi"); w_lo = sem("w4_lo"); piece_done = sem("piece4_done")
            act_read = sem("act_read"); u_made = sem("u_made"); dz = sem("dz")
            u_stored = [sem(f"u_stored{n}") for n in range(2)]
            g_stored = [sem(f"g4_stored{n}") for n in range(2)]
            qk_loaded = [sem(f"qk_loaded{n}") for n in range(2)]
            vk_loaded = [sem(f"vk_loaded{n}") for n in range(2)]
            nm_loaded = [sem(f"nm_loaded{n}") for n in range(2)]
            cols_loaded = sem("cols_loaded"); x_back = sem("x_back"); setup = sem("setup"); mask_made = sem("mask_made")
            chunk_cols = sem("chunk_cols"); s_done = sem("s_done"); w_exp = sem("w_exp"); s_hi = sem("s_hi")
            ek_hi = sem("ek_hi"); prep = sem("prep"); ek_lo = sem("ek_lo"); step_done = sem("step_done")
            y_read = sem("y_read"); nm_masked = sem("nm_masked"); zg = sem("zg"); fin = sem("fin"); state_new = sem("state_new")
            h_stored = [sem(f"h_stored{n}") for n in range(2)]
            p_loaded = sem("p_loaded"); box = sem("box"); mix_stored = sem("mix_stored")

            XBANK, YBANK, UBANK, SBANK = bank[4], bank[5], bank[6], bank[7]
            NCOL = VW + 2 * HB

            STEPS = [(cc, h, d) for cc in range(2) for h in range(HEADS) for d in range(2)]
            NS = len(STEPS)
            TILES = [(k, e) for e in range(2) for k in ("o", "z")] + [(k, e) for e in range(2) for k in ("m", "p")]
            OFF4 = {"o": O0, "z": Z0, "m": GM0, "p": GP0}
            PIECES = [(u, kind, e, tq) for u, (kind, e) in enumerate(TILES) for tq in range(2)]
            NU, NPC = len(TILES), len(PIECES)
            nz = [sum(p[1] == "z" for p in PIECES[:m]) for m in range(NPC + 1)]
            na = [sum(p[1] != "z" for p in PIECES[:m]) for m in range(NPC + 1)]
            ng = [sum(p[1] in "mp" for p in PIECES[:m]) for m in range(NPC + 1)]
            assert NPC == NS and NPC % 4 == 0 and nz[-1] % 2 == 0 and ng[-1] % 2 == 0
            NTRIP = NX // 2
            NCS = NS

            HALFTRIPS = NTRIP // 2

            def trips(eng, body, between=None):
                with eng.Fori(0, HALFTRIPS - 1) as i:
                    body(i, True)
                body(HALFTRIPS - 1, True)
                if between is not None:
                    between()
                with eng.Fori(HALFTRIPS, NTRIP - 1) as i:
                    body(i, True)
                body(NTRIP - 1, False)

            def half_of(i):
                return int((i if isinstance(i, int) else i.max_val) < HALFTRIPS)

            def row(i):
                return i if half_of(i) else i - HALFTRIPS

            def chunk(i, cc, d):
                return i * 2 + (NC + cc) if d == 0 else i * -2 + (NCH - 1 - cc)

            def ctx_chunk(cc, d):
                return cc if d == 0 else NC - 1 - cc

            def chain(h, d):
                return d * HEADS + h

            block = ph.enter_context(nc.Block())

            @block.sync
            def _(sp):
                sp.dma_start(cols[:, :, :, :], cols_d.rearrange("p d c q h -> p d c (q h)")).then_inc(cols_loaded, 16)

                def operands(s, L, h, c, latent):
                    sp.wait_ge(step_done, s + 1)
                    if latent:
                        sp.dma_start(f32(qk_t[:, L]).rearrange("p o b a t -> p (o b) (a t)"),
                                     qk_d[h, :, :, :, c].rearrange("o b p a t -> p (o b) (a t)"))\
                            .then_inc(qk_loaded[L], 16)
                    for a in range(2):
                        sp.dma_start(f32(v_t[:, L, a, 0:HD]).rearrange("p (b f) -> p b f", b=HB),
                                     v_d[h, c, :, :, a]).then_inc(vk_loaded[L], 16)
                    sp.dma_start(kt_t[:, L], kt_d[h, c]).then_inc(vk_loaded[L], 16)

                def tile(i, r, u):
                    kind, e = TILES[u]
                    sp.wait_ge(w_hi, i * NU + (u + 1))
                    sp.wait_ge(w_lo, i * NU + (u + 1))
                    sp.dma_start(wraw[:, u % 2], in_v[:, :, bass.ds(r * (2 * P) + (OFF4[kind] + e * P), P)])\
                        .then_inc(w_loaded[u % 2], 16)

                def store(i, st):
                    cc, h, d = STEPS[st]
                    u, kind, e, tq = PIECES[st]
                    r, half = row(i), half_of(i)
                    t0 = half * HALF + tq * TQ
                    if kind == "z":
                        sp.wait_ge(u_made, i * nz[-1] + (nz[-1] + nz[st] + 1))
                        sp.dma_start(u_d[r * 2 + e, :, t0:t0 + TQ], ustage[:, nz[st] % 2, :])\
                            .then_inc(u_stored[nz[st] % 2], 16)
                    elif kind in "mp":
                        sp.wait_ge(act_read, i * na[-1] + (na[-1] + na[st] + 1))
                        sp.dma_start((gm_d if kind == "m" else gp_d)[r * 2 + e, :, t0:t0 + TQ],
                                     gstage[:, ng[st] % 2, :]).then_inc(g_stored[ng[st] % 2], 16)
                    sp.wait_ge(fin, i * (5 * NS) + 5 * (st + 1))
                    sp.dma_start(h_d[d, chunk(i, cc, d) - NC, :, h * HD:(h + 1) * HD], hout[:, st % 2, :])\
                        .then_inc(h_stored[st % 2], 16)

                def body(i, ahead):
                    for st, (cc, h, d) in enumerate(STEPS):
                        if st % NCHAIN == 0:
                            sp.wait_ge(w_exp, i * NS + NCHAIN * cc)
                            for dd in range(2):
                                sp.dma_start(nm[:, cc, dd], negm_d[dd, :, chunk(i, cc, dd), :].partition_broadcast(P))\
                                    .then_inc(nm_loaded[cc], 16)
                        if st % 2 == 0:
                            u = st // 2 + 2
                            if u < NU:
                                tile(i, row(i), u)
                            elif ahead:
                                last = isinstance(i, int) and i == HALFTRIPS - 1
                                tile(i + 1, 0 if last else row(i) + 1, u - NU)
                        operands(i * NS + (NCS + st), st % 2, h, chunk(i, cc, d), True)
                        if st >= 2:
                            store(i, st - 2)
                    store(i, NS - 2)
                    store(i, NS - 1)

                tile(0, 0, 0)
                tile(0, 0, 1)
                for st, (cc, h, d) in enumerate(STEPS):
                    operands(st, st % 2, h, ctx_chunk(cc, d), False)

                def early_half():
                    sp.wait_ge(piece_done, NPC + NPC * HALFTRIPS)
                    for part in range(2):
                        sp.dma_start(f32(xlate[part][:, :, :]), xe_d[part]).then_inc(x_back, 16)

                trips(sp, body, early_half)
                for n in range(2):
                    sp.wait_ge(u_stored[n], 16 * NTRIP * nz[-1] // 2)
                    sp.wait_ge(g_stored[n], 16 * NTRIP * ng[-1] // 2)
                    sp.wait_ge(h_stored[n], 16 * NTRIP * NS // 2)

            @block.tensor
            def _(pe):
                pe.sem_inc(piece_done, NPC)
                pe.sem_inc(step_done, 2)
                pe.wait_ge(setup, 3)

                def scores(l, i, st):
                    L = st % 2
                    pe.wait_ge(qk_loaded[L], i * (16 * NS // 2) + 16 * (st // 2 + 1))
                    pe.wait_ge(prep, l * 3)
                    for b in range(HB):
                        for n, (ka, qa) in enumerate(((0, 0), (0, 1), (1, 0))):
                            mm = pe.matmul(SBANK[:, 0:P], qk_t[:, L, 1, b, ka, :], qk_t[:, L, 0, b, qa, :],
                                           start=(b == 0 and n == 0), stop=(b == HB - 1 and n == 2))
                    mm.then_inc(s_done, 1)

                def step(s, l, L, vk):
                    pe.wait_ge(state_new, s + NCHAIN)
                    pe.wait_ge(vk_loaded[L], vk)
                    if l is not None:
                        pe.wait_ge(s_hi, l + 1)
                        pe.wait_ge(prep, l * 3 + 3)
                        for b in range(HB):
                            for n, (qa, c_) in enumerate(((0, state_h), (0, state_l), (1, state_h))):
                                pe.matmul(XBANK[:, 0:VW], qk_t[:, L, 0, b, qa, :], c_[:, L, b, :],
                                          start=(b == 0 and n == 0), stop=(b == HB - 1 and n == 2))
                        for n, (p_, va) in enumerate(((p_h, 0), (p_h, 1), (p_l, 0))):
                            pe.matmul(YBANK[:, 0:VW], p_[:, L, :], v_t[:, L, va, :], start=(n == 0), stop=(n == 2))
                    pe.wait_ge(ek_hi, s + 1)
                    pe.wait_ge(ek_lo, s + 1)
                    for b in range(HB):
                        for n, e_ in enumerate((ek_h, ek_l)):
                            pe.matmul(YBANK[:, VW + 2 * b:VW + 2 * b + 2], e_[:, L, b * P:(b + 1) * P],
                                      v_t[:, L, 0, HD:VW], start=(n == 0), stop=(n == 1))
                    for b in range(HB):
                        for n, (e_, va) in enumerate(((ek_h, 0), (ek_h, 1), (ek_l, 0))):
                            mm = pe.matmul(UBANK[:, b * HD:(b + 1) * HD], e_[:, L, b * P:(b + 1) * P],
                                           v_t[:, L, va, 0:HD], start=(n == 0), stop=(n == 2))
                    mm.then_inc(step_done, 1)

                def piece(i, m):
                    u, kind, e, tq = PIECES[m]
                    if tq == 0:
                        pe.wait_ge(w_hi, i * NU + (u + 1 + 2))
                        pe.wait_ge(w_lo, i * NU + (u + 1 + 2))
                    pm, trip = (m - 4) % NPC, (1 if m >= 4 else 0)
                    if PIECES[pm][1] == "z":
                        pe.wait_ge(u_made, i * nz[-1] + (nz[-1] * trip + nz[pm] + 1))
                    else:
                        pe.wait_ge(act_read, i * na[-1] + (na[-1] * trip + na[pm] + 1))
                    for k in range(KT):
                        for n, (a, part) in enumerate(((wh, 0), (wh, 1), (wl, 0))):
                            mm = pe.matmul(bank[m % 4][:, :], a[:, u % 2, k, :],
                                           xlate[part][:, k, tq * TQ:(tq + 1) * TQ],
                                           start=(k == 0 and n == 0), stop=(k == KT - 1 and n == 2))
                    mm.then_inc(piece_done, 1)

                for st in range(NCS):
                    step(st, None, st % 2, 48 * (st // 2 + 1))

                def body(i):
                    for st in range(NS):
                        l = i * NS + st
                        scores(l, i, st)
                        piece(i, st)
                        step(l + NCS, l, st % 2, i * (48 * NS // 2) + 48 * (NCS // 2 + st // 2 + 1))

                with pe.Fori(0, NTRIP // 2) as i:
                    body(i)
                pe.wait_ge(x_back, 32)
                with pe.Fori(NTRIP // 2, NTRIP) as i:
                    body(i)

            @block.scalar
            def _(act):
                act.sem_inc(w_hi, 2)
                act.sem_inc(act_read, na[-1])
                act.sem_inc(w_exp, NCHAIN)

                def keys(s, L, cc, h, d, vk):
                    act.wait_ge(vk_loaded[L], vk)
                    act.wait_ge(step_done, s + 1)
                    act.activation(ek_h[:, L, :], kt_t[:, L, :], ACT.Copy,
                                   scale=ccol[:, cc, d, 3, h:h + 1]).then_inc(ek_hi, 1)

                def split_hi(i, u):
                    act.wait_ge(w_loaded[u % 2], i * (16 * NU // 2) + 16 * (u // 2 + 1))
                    act.wait_ge(piece_done, i * NPC + (NPC + 2 * u - 2))
                    act.activation(wh[:, u % 2], wraw[:, u % 2], ACT.Copy).then_inc(w_hi, 1)

                def evacuate(i, m):
                    u, kind, e, tq = PIECES[m]
                    act.wait_ge(piece_done, i * NPC + (NPC + m + 1))
                    if kind == "o":
                        act.wait_ge(u_made, i * nz[-1] + (nz[-1] + nz[m]))
                        act.activation(tanh_o[:, tq, :], bank[m % 4][:, :], ACT.Tanh, scale=0.5).then_inc(act_read, 1)
                    elif kind == "z":
                        act.wait_ge(u_made, i * nz[-1] + (nz[-1] + nz[m]))
                        act.activation(tanh_z[:, :], bank[m % 4][:, :], ACT.Tanh, scale=0.5).then_inc(dz, 1)
                    else:
                        a = ng[m]
                        act.wait_ge(g_stored[a % 2], i * (16 * ng[-1] // 2) + 16 * (a // 2))
                        act.activation(gstage[:, a % 2, :], bank[m % 4][:, :], ACT.Tanh, scale=0.5).then_inc(act_read, 1)

                split_hi(0, 0)
                split_hi(0, 1)
                for st, (cc, h, d) in enumerate(STEPS):
                    act.wait_ge(chunk_cols, 2 * cc + 2)
                    keys(st, st % 2, cc, h, d, 48 * (st // 2 + 1))

                def body(i, ahead):
                    for st, (cc, h, d) in enumerate(STEPS):
                        L, l = st % 2, i * NS + st
                        s = l + NCS
                        act.wait_ge(chunk_cols, i * 4 + (2 * cc + 6))
                        keys(s, L, cc, h, d, i * (48 * NS // 2) + 48 * (NCS // 2 + st // 2 + 1))
                        act.wait_ge(nm_masked, i * 4 + (2 * cc + 2))
                        act.activation(wexp[:, L, :], nm[:, cc, d, h, :], ACT.Exp,
                                       bias=ccol[:, cc, d, 0, h:h + 1]).then_inc(w_exp, 1)
                        act.wait_ge(state_new, s + 1)
                        act.activation(state_h[:, L], state[:, chain(h, d)], ACT.Copy).then_inc(s_hi, 1)
                        evacuate(i, st)
                        act.wait_ge(step_done, s + 3)
                        act.activation(ysb[:, L, :], YBANK[:, 0:VW], ACT.Copy).then_inc(y_read, 1)
                        if st % 2 == 1 and (st // 2 + 2 < NU or ahead):
                            split_hi(i, st // 2 + 2)

                trips(act, body)

            @block.vector
            def _(dve):
                dve.sem_inc(w_lo, 2)
                dve.sem_inc(u_made, nz[-1])
                dve.sem_inc(state_new, NCHAIN)
                dve.memset(state[:, :, :, :], 0.0).then_inc(setup, 1)
                dve.memset(f32(v_t[:, :, :, HD:VW]), 0.0).then_inc(setup, 1)
                dve.wait_ge(setup, 2)
                dve.memset(f32(v_t[:, :, 0, HD:HD + 1]), 1.0).then_inc(setup, 1)
                dve.wait_ge(cols_loaded, 16)

                def keys(s, L, cc, h, d):
                    dve.wait_ge(ek_hi, s + 1)
                    dve.scalar_tensor_tensor(out=ek_l[:, L, :], in0=kt_t[:, L, :], scalar=ccol[:, cc, d, 3, h:h + 1],
                                             in1=f32(ek_h[:, L, :]), op0=ALU.mult, op1=ALU.subtract).then_inc(ek_lo, 1)

                def update(s, cc, h, d, y_wait):
                    ch, decay = chain(h, d), ccol[:, cc, d, 4, h:h + 1]
                    dve.wait_ge(step_done, s + 3)
                    dve.wait_ge(state_new, s + 1)
                    dve.scalar_tensor_tensor(out=state[:, ch, :, 0:HD], in0=state[:, ch, :, 0:HD], scalar=decay,
                                             in1=UBANK[:, :].rearrange("p (b f) -> p b f", b=HB),
                                             op0=ALU.mult, op1=ALU.add)
                    if y_wait is not None:
                        dve.wait_ge(y_read, y_wait)
                    dve.scalar_tensor_tensor(out=state[:, ch, :, HD:VW], in0=state[:, ch, :, HD:VW], scalar=decay,
                                             in1=YBANK[:, VW:NCOL].rearrange("p (b f) -> p b f", b=HB),
                                             op0=ALU.mult, op1=ALU.add).then_inc(state_new, 1)

                def split_lo(i, u):
                    dve.wait_ge(w_hi, i * NU + (u + 1 + 2))
                    dve.tensor_tensor(wl[:, u % 2], wraw[:, u % 2], f32(wh[:, u % 2]), ALU.subtract).then_inc(w_lo, 1)

                split_lo(0, 0)
                split_lo(0, 1)
                for st, (cc, h, d) in enumerate(STEPS):
                    if st % NCHAIN == 0:
                        for dd in range(2):
                            dve.tensor_copy(ccol[:, cc, dd], cols[:, dd, ctx_chunk(cc, dd), :]
                                            .rearrange("p (q h) -> p q h", h=HEADS)).then_inc(chunk_cols, 1)
                        dve.wait_ge(chunk_cols, 2 * cc + 2)
                    keys(st, st % 2, cc, h, d)
                    update(st, cc, h, d, None)

                def evacuate(i, m):
                    u, kind, e, tq = PIECES[m]
                    if kind != "z":
                        return
                    a = nz[m]
                    dve.wait_ge(dz, i * nz[-1] + (a + 1))
                    dve.scalar_tensor_tensor(out=zgate[:, :], in0=tanh_z[:, :], scalar=1.0, in1=bank[m % 4][:, :],
                                             op0=ALU.add, op1=ALU.mult).then_inc(zg, 1)
                    dve.wait_ge(u_stored[a % 2], i * (16 * nz[-1] // 2) + 16 * (a // 2))
                    dve.wait_ge(zg, i * nz[-1] + (a + 1))
                    dve.scalar_tensor_tensor(out=ustage[:, a % 2, :], in0=tanh_o[:, tq, :], scalar=1.0,
                                             in1=zgate[:, :], op0=ALU.add, op1=ALU.mult).then_inc(u_made, 1)

                def body(i, ahead):
                    for st, (cc, h, d) in enumerate(STEPS):
                        L, l = st % 2, i * NS + st
                        s = l + NCS
                        if st % NCHAIN == 0:
                            dve.wait_ge(step_done, s - (NCHAIN - 2))
                            for dd in range(2):
                                dve.tensor_copy(ccol[:, cc, dd], cols[:, dd, bass.ds(chunk(i, cc, dd), 1), :]
                                                .rearrange("p c (q h) -> p (c q) h", h=HEADS)).then_inc(chunk_cols, 1)
                            dve.wait_ge(nm_loaded[cc], i * 32 + 32)
                            for dd in range(2):
                                dve.tensor_tensor(nm[:, cc, dd], nm[:, cc, dd],
                                                  cmask[:, dd].unsqueeze(1).broadcast_to([P, HEADS, P]),
                                                  ALU.add).then_inc(nm_masked, 1)
                            dve.wait_ge(chunk_cols, i * 4 + (2 * cc + 6))
                        keys(s, L, cc, h, d)
                        dve.wait_ge(s_done, l + 1)
                        dve.wait_ge(w_exp, l + (1 + NCHAIN))
                        dve.tensor_tensor(pf[:, L, :], SBANK[:, 0:P], wexp[:, L, :], ALU.mult).then_inc(prep, 1)
                        dve.wait_ge(s_hi, l + 1)
                        dve.tensor_tensor(state_l[:, L], state[:, chain(h, d)], f32(state_h[:, L]), ALU.subtract)
                        dve.wait_ge(prep, l * 3 + 1)
                        dve.tensor_copy(p_h[:, L, :], pf[:, L, :]).then_inc(prep, 1)
                        dve.wait_ge(prep, l * 3 + 2)
                        dve.tensor_tensor(p_l[:, L, :], pf[:, L, :], f32(p_h[:, L, :]), ALU.subtract).then_inc(prep, 1)
                        evacuate(i, st)
                        update(s, cc, h, d, l + 1)
                        dve.scalar_tensor_tensor(out=num[:, L, :], in0=XBANK[:, 0:VW], scalar=ccol[:, cc, d, 1, h:h + 1],
                                                 in1=ysb[:, L, :], op0=ALU.mult, op1=ALU.add).then_inc(fin, 1)
                        dve.wait_ge(fin, l * 5 + 1)
                        dve.tensor_scalar(den[:, L, 0:1], num[:, L, HD:HD + 1], -1.0, ccol[:, cc, d, 2, h:h + 1],
                                          ALU.mult, ALU.max).then_inc(fin, 1)
                        dve.wait_ge(fin, l * 5 + 2)
                        dve.tensor_tensor(den[:, L, 1:2], den[:, L, 0:1], num[:, L, HD:HD + 1], ALU.max).then_inc(fin, 1)
                        dve.wait_ge(fin, l * 5 + 3)
                        dve.reciprocal(den[:, L, 2:3], den[:, L, 1:2]).then_inc(fin, 1)
                        dve.wait_ge(h_stored[L], i * (16 * NS // 2) + 16 * (st // 2))
                        dve.wait_ge(fin, l * 5 + 4)
                        dve.tensor_scalar(hout[:, L, :], num[:, L, 0:HD], den[:, L, 2:3], None,
                                          ALU.mult).then_inc(fin, 1)
                        if st % 2 == 1 and (st // 2 + 2 < NU or ahead):
                            split_lo(i, st // 2 + 2)

                dve.wait_ge(mask_made, 3)
                trips(dve, body)

            @block.gpsimd
            def _(pool):
                made = [0]

                def link(ins):
                    made[0] += 1
                    ins.then_inc(box, 1)
                    pool.wait_ge(box, made[0])

                pool.memset(cmask[:, :, :], 0.0).then_inc(mask_made, 1)
                pool.wait_ge(mask_made, 1)
                for d in range(2):
                    sign = -1 if d == 0 else 1
                    nc.gpsimd.affine_select(out=cmask[:, d], in_=cmask[:, d], compare_op=ALU.is_ge, fill=M_INIT,
                                            base=0, pattern=[[-sign, P]], channel_multiplier=sign).then_inc(mask_made, 1)

                def inverse_counts(axis, length, w):
                    cnt = [min(n + w - w // 2, length) - max(n - w // 2, 0) for n in range(length)]
                    link(pool.memset(icnt[:, axis, 0:length], 1.0 / w))
                    for n in range(length):
                        if cnt[n] != w:
                            last = pool.memset(icnt[:, axis, n:n + 1], 1.0 / cnt[n])
                    link(last)

                def window_sums(views, length, w):
                    src, dst = views
                    step = 1
                    while step < w:
                        m = length - 2 * step + 1
                        link(pool.tensor_tensor(dst(0, m), src(0, m), src(step, m), ALU.add))
                        src, dst, step = dst, src, 2 * step
                    return src, dst

                PAD = 8
                RL, CL = GRID_H + 2 * PAD, GRID_W + 2 * PAD
                for g in range(PG):
                    w = 2 << g
                    start = PAD - w // 2
                    inverse_counts(0, GRID_H, w)
                    inverse_counts(1, GRID_W, w)
                    pool.memset(pool_a[:, 0:PAD * GRID_W], 0.0)
                    link(pool.memset(pool_a[:, (PAD + GRID_H) * GRID_W:RL * GRID_W], 0.0))
                    pool.dma_start(pool_a[:, PAD * GRID_W:(PAD + GRID_H) * GRID_W], p_d[g]).then_inc(p_loaded, 16)
                    pool.wait_ge(p_loaded, 32 * g + 16)
                    rows = [(lambda buf: lambda n, m: buf[:, n * GRID_W:(n + m) * GRID_W])(b) for b in (pool_a, pool_b)]
                    src, dst = window_sums(rows, RL, w)
                    other = pool_b if src is rows[0] else pool_a
                    this = pool_a if src is rows[0] else pool_b
                    wide = other[:, 0:GRID_H * CL].rearrange("p (r c) -> p r c", c=CL)
                    pool.memset(wide[:, :, 0:PAD], 0.0)
                    pool.memset(wide[:, :, PAD + GRID_W:CL], 0.0)
                    link(pool.tensor_tensor(wide[:, :, PAD:PAD + GRID_W],
                                            src(start, GRID_H).rearrange("p (r c) -> p r c", c=GRID_W),
                                            icnt[:, 0, 0:GRID_H].unsqueeze(2).broadcast_to([P, GRID_H, GRID_W]), ALU.mult))
                    cols_ = [(lambda buf: lambda n, m: buf[:, 0:GRID_H * CL]
                              .rearrange("p (r c) -> p r c", c=CL)[:, :, n:n + m])(b) for b in (other, this)]
                    src, dst = window_sums(cols_, CL, w)
                    end = other if src is cols_[0] else this
                    spare = this if src is cols_[0] else other
                    pool.dma_start(spare[:, 0:SEQ], p_d[g]).then_inc(p_loaded, 16)
                    res = src(start, GRID_W)
                    link(pool.tensor_tensor(res, res, icnt[:, 1, 0:GRID_W].unsqueeze(1)
                                            .broadcast_to([P, GRID_H, GRID_W]), ALU.mult))
                    pool.wait_ge(p_loaded, 32 * g + 32)
                    flat = spare[:, 0:SEQ].rearrange("p (r c) -> p r c", c=GRID_W)
                    link(pool.tensor_tensor(flat, res, flat, ALU.subtract))
                    pool.dma_start(mix_d[g], spare[:, 0:SEQ]).then_inc(mix_stored, 16)
                    pool.wait_ge(mix_stored, 16 * g + 16)

        late.close()
        with ExitStack() as ph:
            def sb(name, shape, dt=FP32):
                return ph.enter_context(nc.sbuf_tensor(name, shape, dt))

            QT = TQ // P
            wraw = sb("wraw5", [P, 2, KT, P])
            wh = sb("wh5", [P, 2, KT, P], FP32R)
            wl = sb("wl5", [P, 2, KT, P], FP32R)
            pw = sb("pw", [P, PG, P])
            pw_h = sb("pw_h", [P, PG, P], FP32R)
            pw_l = sb("pw_l", [P, PG, P], FP32R)
            hw_row = sb("hw_row", [P, D])
            fn_row = sb("fn_row", [P, D])
            hsum = sb("hsum", [P, 2, D])
            hback = sb("hback", [P, 2, D])
            ut = sb("ut", [P, 2, KT, P])
            yt = sb("yt", [P, KT, P])
            y_h = sb("y_h", [P, KT, TQ], FP32R)
            y_l = sb("y_l", [P, KT, TQ], FP32R)
            mixt = sb("mixt", [P, 2, TQ])
            mix_h = sb("mix_h", [P, 2, TQ], FP32R)
            mix_l = sb("mix_l", [P, 2, TQ], FP32R)
            zpt = sb("zpt", [P, 2, TQ])
            ypt = sb("ypt", [P, TQ])
            yp_h = sb("yp_h", [P, PG, TQ], FP32R)
            yp_l = sb("yp_l", [P, PG, TQ], FP32R)
            gmt = sb("gmt", [P, 2, TQ])
            gpt = sb("gpt", [P, 2, TQ])
            mm_ = sb("merged_m", [P, TQ])
            mp_ = sb("merged_p", [P, TQ])
            m_h = sb("m_h", [P, KT, TQ], FP32R)
            m_l = sb("m_l", [P, KT, TQ], FP32R)
            of = sb("of", [P, 2, TQ])
            xo = sb("xo", [P, QT, D])
            junk = sb("junk", [P, D], mybir.dt.bfloat16)
            hss = sb("hss", [P, 5, 2, HEADS])
            oss = sb("oss", [P, 5, QT])

            w_loaded = [sem(f"w5_loaded{n}") for n in range(2)]
            w_hi = sem("w5_hi"); w_lo = sem("w5_lo"); unit_done = sem("unit_done")
            rows_loaded = sem("rows_loaded"); rows_ready = sem("rows_ready")
            pw_hi = sem("pw_hi"); pw_lo = sem("pw_lo")
            h_loaded = [sem(f"h_loaded{n}") for n in range(2)]
            h_dve = sem("h_dve"); h_act = sem("h_act"); h_turned = sem("h_turned"); y_made = sem("y_made5")
            y_hi = sem("y_hi"); y_lo = sem("y_lo")
            mix_loaded = [sem(f"mix_loaded{n}") for n in range(2)]
            mix_hi = sem("mix_hi"); mix_lo = sem("mix_lo"); mix_done = sem("mix_done")
            yp_made = sem("yp_made"); yp_hi = sem("yp_hi"); yp_lo = sem("yp_lo")
            g_loaded = [sem(f"g5_loaded{n}") for n in range(2)]
            gated = sem("gated"); m_made = sem("m_made"); m_hi = sem("m_hi"); m_lo = sem("m_lo")
            of_made = sem("of_made"); o_turned = sem("o_turned"); x_loaded = sem("x5_loaded")
            x_added = sem("x_added"); o_act = sem("o_act"); o_dve = sem("o_dve"); o_ready = sem("o_ready")
            o_stored = sem("o_stored")

            UNITS = [(m, n, kt) for n in range(KT) for m, kt in (("m", KT), ("p", PG))] + [("o", n, KT) for n in range(KT)]
            NU = len(UNITS)
            SRC = {"m": branch_m_w[0].rearrange("(j p) n -> p j n", p=P),
                   "p": branch_p_w[0].rearrange("(j p) n -> p j n", p=P),
                   "o": out_w[0].rearrange("(j p) n -> p j n", p=P)}
            HSTEP = 7
            OSTEP = 2
            block = ph.enter_context(nc.Block())

            def quarters(eng, body):
                with eng.Fori(0, NTQ - 1) as i:
                    body(i, True)
                body(NTQ - 1, False)

            @block.sync
            def _(sp):
                sp.dma_start(pw[:, :, :], pool_w[0].rearrange("g c n -> c g n")).then_inc(rows_loaded, 16)
                sp.dma_start(hw_row[:, :], head_norm_w[0].partition_broadcast(P)).then_inc(rows_loaded, 16)
                sp.dma_start(fn_row[:, :], final_norm_w.partition_broadcast(P)).then_inc(rows_loaded, 16)

                def tile(i, u):
                    m, n, kt = UNITS[u % NU]
                    sp.wait_ge(w_hi, i * NU + (u + 1))
                    sp.wait_ge(w_lo, i * NU + (u + 1))
                    sp.dma_start(wraw[:, u % 2, 0:kt], SRC[m][:, :, n * P:(n + 1) * P]).then_inc(w_loaded[u % 2], 16)

                def hidden(i, q):
                    c_ = i * QT + q
                    sp.wait_ge(y_made, i * QT + (q + 1))
                    sp.dma_start(hsum[:, q % 2], h_d[0, c_]).then_inc(h_loaded[q % 2], 16)
                    sp.dma_start(hback[:, q % 2], h_d[1, c_]).then_inc(h_loaded[q % 2], 16)
                    sp.dma_start(ut[:, q % 2], u_d[:, :, bass.ds(i * TQ + q * P, P)].rearrange("j p t -> p j t"))\
                        .then_inc(h_loaded[q % 2], 16)

                def pooled(i, g):
                    if g >= 2:
                        sp.wait_ge(yp_made, i * PG + (g - 1))
                    sp.dma_start(mixt[:, g % 2], mix_d[g, :, bass.ds(i * TQ, TQ)]).then_inc(mix_loaded[g % 2], 16)
                    sp.dma_start(zpt[:, g % 2], zp_d[g, :, bass.ds(i * TQ, TQ)]).then_inc(mix_loaded[g % 2], 16)

                def gates(i, n):
                    sp.wait_ge(gated, i * (2 * KT) + 2 * max(n - 1, 0))
                    sp.dma_start(gmt[:, n % 2], gm_d[n, :, bass.ds(i * TQ, TQ)]).then_inc(g_loaded[n % 2], 16)
                    sp.dma_start(gpt[:, n % 2], gp_d[n, :, bass.ds(i * TQ, TQ)]).then_inc(g_loaded[n % 2], 16)

                for u in range(2):
                    tile(0, u)
                for q in range(QT):
                    hidden(0, q)
                for g in range(2):
                    pooled(0, g)

                def body(i, ahead):
                    gates(i, 0)
                    gates(i, 1)
                    for g in range(2, PG):
                        pooled(i, g)
                    for n in range(KT):
                        tile(i, 2 * n + 2)
                        tile(i, 2 * n + 3)
                        if n + 2 < KT:
                            gates(i, n + 2)
                    sp.wait_ge(o_stored, i * 16)
                    sp.dma_start(xo[:, :, :], x[bass.ds(i * TQ, TQ), :].rearrange("(q p) n -> p q n", p=P))\
                        .then_inc(x_loaded, 16)
                    for n in range(KT):
                        if ahead and n % 2 == 0:
                            hidden(i + 1, n // 2)
                        if 2 * KT + n + 2 < NU or ahead:
                            tile(i, 2 * KT + n + 2)
                    if ahead:
                        for g in range(2):
                            pooled(i + 1, g)
                    sp.wait_ge(o_ready, i * QT + QT)
                    sp.dma_start(out[bass.ds(i * TQ, TQ), :].rearrange("(q p) n -> p q n", p=P), xo[:, :, :])\
                        .then_inc(o_stored, 16)

                quarters(sp, body)
                sp.wait_ge(o_stored, 16 * NTQ)

            @block.tensor
            def _(pe):
                pe.sem_inc(unit_done, 2)

                def turn_hidden(i, q):
                    t = i * QT + q
                    pe.wait_ge(h_dve, t * HSTEP + HSTEP)
                    pe.wait_ge(y_made, t + 2)
                    for j in range(KT):
                        mm = pe.transpose(bank[4 + j // 4][:, (j % 4) * P:(j % 4 + 1) * P],
                                          hsum[:, q % 2, j * P:(j + 1) * P], ident[:, :])
                    mm.then_inc(h_turned, 1)

                def groups_(i):
                    for g in range(PG):
                        pe.wait_ge(mix_hi, i * PG + (g + 1))
                        pe.wait_ge(mix_lo, i * PG + (g + 1))
                        if g == 0:
                            pe.wait_ge(x_added, i * KT)
                        if g >= 2:
                            pe.wait_ge(yp_made, i * PG + (g - 1))
                        for n, (a, b) in enumerate(((pw_h, mix_h), (pw_h, mix_l), (pw_l, mix_h))):
                            mm = pe.matmul(bank[6 + g % 2][:, :], a[:, g, :], b[:, g % 2, :], start=(n == 0), stop=(n == 2))
                        mm.then_inc(mix_done, 1)

                def unit(i, u):
                    m, n, kt = UNITS[u]
                    pe.wait_ge(w_hi, i * NU + (u + 3))
                    pe.wait_ge(w_lo, i * NU + (u + 3))
                    if m == "m":
                        dst, (bh, bl) = bank[n % 2], (y_h, y_l)
                        if n == 0:
                            pe.wait_ge(y_hi, i * QT + QT)
                            pe.wait_ge(y_lo, i * QT + QT)
                        pe.wait_ge(of_made, i * KT) if n < 2 else pe.wait_ge(gated, i * (2 * KT) + 2 * (n - 1))
                    elif m == "p":
                        dst, (bh, bl) = bank[2 + n % 2], (yp_h, yp_l)
                        if n == 0:
                            pe.wait_ge(yp_hi, i * PG + PG)
                            pe.wait_ge(yp_lo, i * PG + PG)
                        pe.wait_ge(gated, i * (2 * KT) + 2 * max(n - 1, 0))
                    else:
                        dst, (bh, bl) = bank[n % 2], (m_h, m_l)
                        if n == 0:
                            pe.wait_ge(m_hi, i * KT + KT)
                            pe.wait_ge(m_lo, i * KT + KT)
                        pe.wait_ge(gated, i * (2 * KT) + 2 * KT) if n < 2 else pe.wait_ge(of_made, i * KT + (n - 1))
                    for k in range(kt):
                        for r, (a, b) in enumerate(((wh, bh), (wh, bl), (wl, bh))):
                            mm = pe.matmul(dst[:, :], a[:, u % 2, k, :], b[:, k, :],
                                           start=(k == 0 and r == 0), stop=(k == kt - 1 and r == 2))
                    mm.then_inc(unit_done, 1)

                def turn_output(i, n):
                    pe.wait_ge(of_made, i * KT + (n + 1))
                    pe.wait_ge(yp_made, i * PG + PG) if n < 2 else pe.wait_ge(x_added, i * KT + (n - 1))
                    for q in range(QT):
                        mm = pe.transpose(bank[6 + n % 2][:, q * P:(q + 1) * P], of[:, n % 2, q * P:(q + 1) * P], ident[:, :])
                    mm.then_inc(o_turned, 1)

                for q in range(QT):
                    turn_hidden(0, q)
                pe.wait_ge(pw_lo, 1)

                def body(i, ahead):
                    groups_(i)
                    for u in range(2 * KT):
                        unit(i, u)
                    for n in range(KT):
                        unit(i, 2 * KT + n)
                        if n >= 1:
                            turn_output(i, n - 1)
                        if ahead and n % 2 == 1:
                            turn_hidden(i + 1, n // 2)
                    turn_output(i, KT - 1)

                quarters(pe, body)

            @block.scalar
            def _(act):
                act.sem_inc(w_hi, 2)

                def split_hi(i, u):
                    m, n, kt = UNITS[u % NU]
                    act.wait_ge(w_loaded[u % 2], i * (16 * NU // 2) + 16 * (u // 2 + 1))
                    act.wait_ge(unit_done, i * NU + (u + 1))
                    act.activation(wh[:, u % 2, 0:kt], wraw[:, u % 2, 0:kt], ACT.Copy).then_inc(w_hi, 1)

                def squares(i, q):
                    t = i * QT + q
                    act.wait_ge(h_dve, t * HSTEP + 1)
                    for h in range(HEADS):
                        if h == 0:
                            act.wait_ge(h_act, t * (HEADS + 1))
                        else:
                            act.wait_ge(h_act, t * (HEADS + 1) + h)
                        act.activation(junk[:, 0:HD], hsum[:, q % 2, h * HD:(h + 1) * HD], ACT.Square,
                                       accum_out=hss[:, 0, q % 2, h:h + 1]).then_inc(h_act, 1)
                    act.wait_ge(h_dve, t * HSTEP + 2)
                    act.activation(hss[:, 2, q % 2], hss[:, 1, q % 2], ACT.Sqrt).then_inc(h_act, 1)

                def hidden_hi(i, q):
                    t = i * QT + q
                    act.wait_ge(y_made, t + 3)
                    act.wait_ge(unit_done, i * NU - (NU - 2 * KT - 2)) if not (isinstance(i, int) and i == 0) else None
                    act.activation(y_h[:, :, q * P:(q + 1) * P], yt[:, :, :], ACT.Copy).then_inc(y_hi, 1)

                def pooled_hi(i, g):
                    act.wait_ge(mix_loaded[g % 2], i * 64 + 32 * (g // 2 + 1))
                    act.wait_ge(mix_done, i * PG + (g - 1)) if g >= 2 else act.wait_ge(mix_done, i * PG)
                    act.activation(mix_h[:, g % 2], mixt[:, g % 2], ACT.Copy).then_inc(mix_hi, 1)

                def branch_hi(i, g):
                    act.wait_ge(yp_made, i * PG + (g + 1))
                    act.wait_ge(unit_done, i * NU + 2)
                    act.activation(yp_h[:, g], ypt[:, :], ACT.Copy).then_inc(yp_hi, 1)

                act.wait_ge(rows_loaded, 48)
                act.activation(pw_h[:, :, :], pw[:, :, :], ACT.Copy).then_inc(pw_hi, 1)
                for u in range(2):
                    split_hi(0, u)
                for q in range(QT):
                    squares(0, q)
                    hidden_hi(0, q)

                def body(i, ahead):
                    pooled_hi(i, 0)
                    for g in range(PG):
                        if g + 1 < PG:
                            pooled_hi(i, g + 1)
                        branch_hi(i, g)
                    for n in range(KT):
                        split_hi(i, 2 * n + 2)
                        split_hi(i, 2 * n + 3)
                        act.wait_ge(m_made, i * KT + (n + 1))
                        act.activation(m_h[:, n], mm_[:, :], ACT.Copy).then_inc(m_hi, 1)
                    for n in range(KT):
                        act.wait_ge(unit_done, i * NU + (2 * KT + n + 3))
                        act.wait_ge(o_turned, i * KT + max(n - 1, 0))
                        act.activation(of[:, n % 2], bank[n % 2][:, :], ACT.Copy,
                                       scale=mgate[:, n:n + 1]).then_inc(of_made, 1)
                        if 2 * KT + n + 2 < NU or ahead:
                            split_hi(i, 2 * KT + n + 2)
                        if ahead:
                            squares(i + 1, n // 2) if n % 2 == 0 else hidden_hi(i + 1, n // 2)
                    act.wait_ge(x_added, i * KT + KT)
                    for q in range(QT):
                        act.wait_ge(o_act, i * (QT + 1) + q)
                        act.wait_ge(h_act, (i + (2 if ahead else 1)) * QT * (HEADS + 1))
                        act.activation(junk[:, :], xo[:, q], ACT.Square, accum_out=oss[:, 0, q:q + 1]).then_inc(o_act, 1)
                    act.wait_ge(o_dve, i * OSTEP + 1)
                    act.activation(oss[:, 2], oss[:, 1], ACT.Sqrt).then_inc(o_act, 1)

                quarters(act, body)

            @block.vector
            def _(dve):
                dve.sem_inc(w_lo, 2)
                dve.sem_inc(y_made, 2)
                dve.wait_ge(rows_loaded, 48)
                dve.tensor_scalar(hw_row[:, :], hw_row[:, :], 0.25, None, ALU.mult).then_inc(rows_ready, 1)
                dve.wait_ge(pw_hi, 1)
                dve.tensor_tensor(pw_l[:, :, :], pw[:, :, :], f32(pw_h[:, :, :]), ALU.subtract).then_inc(pw_lo, 1)
                dve.wait_ge(rows_ready, 1)

                def split_lo(i, u):
                    m, n, kt = UNITS[u % NU]
                    dve.wait_ge(w_hi, i * NU + (u + 3))
                    dve.tensor_tensor(wl[:, u % 2, 0:kt], wraw[:, u % 2, 0:kt], f32(wh[:, u % 2, 0:kt]),
                                      ALU.subtract).then_inc(w_lo, 1)

                def norms(i, q):
                    t, L = i * QT + q, q % 2
                    dve.wait_ge(h_loaded[L], i * 96 + 48 * (q // 2 + 1))
                    dve.tensor_tensor(hsum[:, L], hsum[:, L], hback[:, L], ALU.add).then_inc(h_dve, 1)
                    dve.wait_ge(h_act, t * (HEADS + 1) + HEADS)
                    dve.tensor_scalar(hss[:, 1, L], hss[:, 0, L], 1.0 / HD, EPS, ALU.mult, ALU.add).then_inc(h_dve, 1)
                    dve.wait_ge(h_act, t * (HEADS + 1) + HEADS + 1)
                    dve.reciprocal(hss[:, 3, L], hss[:, 2, L]).then_inc(h_dve, 1)
                    dve.wait_ge(h_dve, t * HSTEP + 3)
                    for h in range(HEADS):
                        s = slice(h * HD, (h + 1) * HD)
                        dve.scalar_tensor_tensor(out=hsum[:, L, s], in0=hsum[:, L, s], scalar=hss[:, 3, L, h:h + 1],
                                                 in1=hw_row[:, s], op0=ALU.mult, op1=ALU.mult).then_inc(h_dve, 1)

                def gate_hidden(i, q):
                    t = i * QT + q
                    dve.wait_ge(h_turned, t + 1)
                    dve.wait_ge(y_hi, t)
                    dve.wait_ge(y_lo, t)
                    for b in range(2):
                        last = dve.tensor_tensor(yt[:, 4 * b:4 * b + 4], bank[4 + b][:, :].rearrange("p (j t) -> p j t", t=P),
                                                 ut[:, q % 2, 4 * b:4 * b + 4], ALU.mult)
                    last.then_inc(y_made, 1)

                def hidden_lo(i, q):
                    t = i * QT + q
                    dve.wait_ge(y_hi, t + 1)
                    dve.wait_ge(y_made, t + 3)
                    dve.tensor_tensor(y_l[:, :, q * P:(q + 1) * P], yt[:, :, :], f32(y_h[:, :, q * P:(q + 1) * P]),
                                      ALU.subtract).then_inc(y_lo, 1)

                def pooled_lo(i, g):
                    dve.wait_ge(mix_hi, i * PG + (g + 1))
                    dve.tensor_tensor(mix_l[:, g % 2], mixt[:, g % 2], f32(mix_h[:, g % 2]), ALU.subtract).then_inc(mix_lo, 1)

                for u in range(2):
                    split_lo(0, u)
                for q in range(QT):
                    norms(0, q)
                    gate_hidden(0, q)
                    hidden_lo(0, q)

                def body(i, ahead):
                    pooled_lo(i, 0)
                    for g in range(PG):
                        if g + 1 < PG:
                            pooled_lo(i, g + 1)
                        dve.wait_ge(mix_done, i * PG + (g + 1))
                        dve.wait_ge(yp_hi, i * PG + g)
                        dve.wait_ge(yp_lo, i * PG + g)
                        dve.scalar_tensor_tensor(out=ypt[:, :], in0=bank[6 + g % 2][:, :],
                                                 scalar=vcol[:, VR["pool"] + g:VR["pool"] + g + 1], in1=zpt[:, g % 2],
                                                 op0=ALU.mult, op1=ALU.mult).then_inc(yp_made, 1)
                        dve.wait_ge(yp_hi, i * PG + (g + 1))
                        dve.wait_ge(yp_made, i * PG + (g + 1))
                        dve.tensor_tensor(yp_l[:, g], ypt[:, :], f32(yp_h[:, g]), ALU.subtract).then_inc(yp_lo, 1)
                    for n in range(KT):
                        dve.wait_ge(g_loaded[n % 2], i * (32 * KT // 2) + 32 * (n // 2 + 1))
                        dve.wait_ge(unit_done, i * NU + (2 * n + 1 + 2))
                        dve.wait_ge(m_hi, i * KT + n)
                        dve.wait_ge(m_lo, i * KT + n)
                        dve.scalar_tensor_tensor(out=mm_[:, :], in0=gmt[:, n % 2], scalar=1.0, in1=bank[n % 2][:, :],
                                                 op0=ALU.add, op1=ALU.mult).then_inc(gated, 1)
                        split_lo(i, 2 * n + 2)
                        dve.wait_ge(unit_done, i * NU + (2 * n + 2 + 2))
                        dve.scalar_tensor_tensor(out=mp_[:, :], in0=gpt[:, n % 2], scalar=1.0, in1=bank[2 + n % 2][:, :],
                                                 op0=ALU.add, op1=ALU.mult).then_inc(gated, 1)
                        split_lo(i, 2 * n + 3)
                        dve.wait_ge(gated, i * (2 * KT) + 2 * n + 2)
                        dve.tensor_tensor(mm_[:, :], mm_[:, :], mp_[:, :], ALU.add).then_inc(m_made, 1)
                        dve.wait_ge(m_hi, i * KT + (n + 1))
                        dve.wait_ge(m_made, i * KT + (n + 1))
                        dve.tensor_tensor(m_l[:, n], mm_[:, :], f32(m_h[:, n]), ALU.subtract).then_inc(m_lo, 1)

                    def residual(n):
                        dve.wait_ge(o_turned, i * KT + (n + 1))
                        if n == 0:
                            dve.wait_ge(x_loaded, i * 16 + 16)
                        s = slice(n * P, (n + 1) * P)
                        dve.tensor_tensor(xo[:, :, s], bank[6 + n % 2][:, :].rearrange("p (q f) -> p q f", f=P),
                                          xo[:, :, s], ALU.add).then_inc(x_added, 1)

                    for n in range(KT):
                        if 2 * KT + n + 2 < NU or ahead:
                            split_lo(i, 2 * KT + n + 2)
                        if ahead:
                            norms(i + 1, n // 2) if n % 2 == 0 else gate_hidden(i + 1, n // 2)
                        if n >= 1:
                            residual(n - 1)
                        if ahead and n % 2 == 1:
                            hidden_lo(i + 1, n // 2)
                    residual(KT - 1)
                    dve.wait_ge(o_act, i * (QT + 1) + QT)
                    dve.tensor_scalar(oss[:, 1], oss[:, 0], 1.0 / D, EPS, ALU.mult, ALU.add).then_inc(o_dve, 1)
                    dve.wait_ge(o_act, i * (QT + 1) + QT + 1)
                    dve.reciprocal(oss[:, 3], oss[:, 2]).then_inc(o_dve, 1)
                    dve.wait_ge(o_dve, i * OSTEP + 2)
                    for q in range(QT):
                        dve.scalar_tensor_tensor(out=xo[:, q], in0=xo[:, q], scalar=oss[:, 3, q:q + 1], in1=fn_row[:, :],
                                                 op0=ALU.mult, op1=ALU.mult).then_inc(o_ready, 1)

                quarters(dve, body)


_INS = ['x', 'c', 'ctx', 'c_ctx', 'norm_w', 'ada_w', 'ada_b', 'in_w', 'gate_b', 'head_norm_w', 'pool_w',
        'pool_scale', 'branch_m_w', 'branch_p_w', 'out_w', 'final_norm_w']
_OUTS = [((1, SEQ, D), 'float32')]


def kernel(**inputs):
    import numpy as _np
    import concourse.bacc as _bacc
    from concourse import mybir as _mybir
    from concourse.bass_utils import run_bass_kernel_spmd as _run

    nc = _bacc.Bacc("TRN2", target_bir_lowering=False, num_devices=1)
    arrays, args = {}, []
    for name in _INS:
        a = _np.ascontiguousarray(inputs[name])
        arrays[f"in_{name}_dram"] = a
        args.append(nc.dram_tensor(f"in_{name}_dram", a.shape, _mybir.dt.from_np(a.dtype), kind="ExternalInput").ap())
    for i, (shape, dtype) in enumerate(_OUTS):
        dt = _mybir.dt.from_np(_np.dtype(dtype))
        args.append(nc.dram_tensor(f"out_{i}_dram", shape, dt, kind="ExternalOutput").ap())
    hybrid_block(nc, *args)
    r = _run(nc, [arrays], core_ids=[0])
    return r.results[0]["out_0_dram"]
```

```python
import numpy as np
from contextlib import ExitStack

import concourse.bass as bass
from concourse import mybir
from concourse.alu_op_type import AluOpType as ALU

FP32 = mybir.dt.float32
FP32R = mybir.dt.float32r
ACT = mybir.ActivationFunctionType

P = 128
D = 1024
KT = D // P
SEQ, CTX = 2048, 256
TOK = CTX + SEQ
NX, NC = SEQ // P, CTX // P
NCH = NX + NC
GRID_W = 64
GRID_H = SEQ // GRID_W
HEADS = 4
HD = D // HEADS
HB = HD // P
PW = D // 2
PG = 4
EPS = 1e-6
M_INIT = -1e30
Q0, K0, V0, O0, Z0 = (D * n for n in range(5))
GATE0 = 5 * D
NGATE = 16
POOL0 = GATE0 + NGATE
ZP0 = POOL0 + PW
GM0 = ZP0 + PW
GP0 = GM0 + D
TQ = 512
NTQ = SEQ // TQ
VW = HD + 2
NQ = 5


def f32(ap):
    return ap.bitcast(FP32)


def hybrid_block(nc, x, c, ctx, c_ctx, norm_w, ada_w, ada_b, in_w, gate_b, head_norm_w, pool_w,
                 pool_scale, branch_m_w, branch_p_w, out_w, final_norm_w, out):
    x, ctx, out = x[0], ctx[0], out[0]

    def scratch(name, shape):
        return nc.dram_tensor(name, shape, FP32, kind="Internal").ap()

    gates_d = scratch("gates_d", (NGATE, TOK))
    qk_d = scratch("qk_d", (HEADS, 2, HB, P, NCH, 2, P))
    kt_d = scratch("kt_d", (HEADS, NCH, P, HD))
    v_d = scratch("v_d", (HEADS, NCH, P, HB, 2, P))
    ends_d = scratch("ends_d", (2, 2, HEADS * NCH))
    mprev_d = scratch("mprev_d", (2, HEADS * NCH))
    negm_d = scratch("negm_d", (2, HEADS, NCH, P))
    cols_d = scratch("cols_d", (P, 2, NCH, NQ, HEADS))
    u_d = scratch("u_d", (KT, P, SEQ))
    gm_d = scratch("gm_d", (KT, P, SEQ))
    gp_d = scratch("gp_d", (KT, P, SEQ))
    xe_d = scratch("xe_d", (2, P, KT, SEQ // 2))
    p_d = scratch("p_d", (PG, P, SEQ))
    zp_d = scratch("zp_d", (PG, P, SEQ))
    mix_d = scratch("mix_d", (PG, P, SEQ))
    h_d = scratch("h_d", (NX, P, D))
    hsum_d = scratch("hsum_d", (NX, P, D))

    in_v = in_w[0].rearrange("(j p) n -> p j n", p=P)
    ada_v = ada_w[0].rearrange("(j p) n -> p j n", p=P)

    with ExitStack() as top:
        def sem(name):
            return top.enter_context(nc.semaphore(name))

        def keep(name, shape, dt=FP32):
            return top.enter_context(nc.sbuf_tensor(name, shape, dt))

        ident = keep("ident", [P, P])
        vcol = keep("vcol", [P, 64])
        mgate = keep("mgate", [P, KT])
        bank = [top.enter_context(nc.psum_tensor(f"bank{n}", [P, TQ], FP32)) for n in range(8)]
        HALF = SEQ // 2
        late = top.enter_context(ExitStack())
        early = top.enter_context(ExitStack())
        xlate = [late.enter_context(nc.sbuf_tensor(f"xlate{n}", [P, KT, HALF], FP32R)) for n in range(2)]
        xearly = [early.enter_context(nc.sbuf_tensor(f"xearly{n}", [P, KT, CTX + HALF], FP32R)) for n in range(2)]

        def xn(part, k, t0, w):
            if t0 >= CTX + HALF:
                return xlate[part][:, k, t0 - CTX - HALF:t0 - CTX - HALF + w]
            return xearly[part][:, k, t0:t0 + w]


        VR = {"norm": 0, "ada": 8, "head": 32, "pool": 40, "c": 44, "cc": 52}
        NV = 60
        AS = 256
        NAS = 3 * D // AS
        groups = [(CTX // P, 0, 1, ctx)] + [(TQ // P, CTX + TQ * n, 0, x) for n in range(NTQ)]
        tiles = [(g, r) for g, (w, *_) in enumerate(groups) for r in range(w)]
        first = [sum(w for w, *_ in groups[:g]) for g in range(len(groups) + 1)]
        with ExitStack() as ph:
            def sb(name, shape, dt=FP32):
                return ph.enter_context(nc.sbuf_tensor(name, shape, dt))

            XS, YS = 8, 2
            vrow = sb("vrow", [NV, P])
            aw = sb("aw", [P, 2, KT, AS])
            xt = sb("xt", [P, XS, D])
            sq = sb("sq", [P, D])
            y = sb("y", [P, YS, TQ])
            ss = sb("ss", [P, NCH])
            ms = sb("ms", [P, NCH])
            rt = sb("rt", [P, NCH])
            rstd = sb("rstd", [P, NCH])
            th = sb("th", [P, 2 * KT])
            s1 = sb("s1", [P, 2 * KT])
            sc = sb("sc", [P, KT, 2])
            modA = sb("modA", [P, KT, 2])
            modB = sb("modB", [P, KT, 2])
            sc1 = sb("sc1", [P, KT, 2])

            v_loaded = sem("v_loaded"); aw_loaded = [sem(f"aw_loaded{n}") for n in range(2)]
            x_loaded = [sem(f"x_loaded{n}") for n in range(XS)]
            ident_made = sem("ident_made"); v_turned = sem("v_turned"); vcol_made = sem("vcol_made")
            c_tanh = sem("c_tanh"); c_ready = sem("c_ready"); aw_used = sem("aw_used")
            mod_dve = sem("mod_dve"); squared = sem("squared"); rooted = sem("rooted")
            norm_dve = sem("norm_dve"); x_normed = sem("x_normed"); x_turned = sem("x_turned")
            y_made = sem("y_made"); y_split = sem("y_split")
            block = ph.enter_context(nc.Block())

            @block.sync
            def _(sp):
                for key, src in (("norm", norm_w[0]), ("ada", ada_b[0]), ("head", head_norm_w[0]),
                                 ("pool", pool_scale[0]), ("c", c[0]), ("cc", c_ctx)):
                    rows = src.shape[0] // P
                    sp.dma_start(vrow[VR[key]:VR[key] + rows, :],
                                 src.rearrange("(a b) -> a b", b=P)).then_inc(v_loaded, 16)
                for n in range(NAS):
                    if n >= 2:
                        sp.wait_ge(aw_used, n - 1)
                    sp.dma_start(aw[:, n % 2], ada_v[:, :, n * AS:(n + 1) * AS]).then_inc(aw_loaded[n % 2], 16)

            @block.gpsimd
            def _(pool):
                nc.gpsimd.memset(ident[:, :], 0.0).then_inc(ident_made, 1)
                pool.wait_ge(ident_made, 1)
                nc.gpsimd.affine_select(out=ident[:, :], in_=ident[:, :], compare_op=ALU.not_equal, fill=1.0,
                                        base=0, pattern=[[-1, P]], channel_multiplier=1).then_inc(ident_made, 1)
                for n, (g, r) in enumerate(tiles):
                    if n >= XS:
                        back = tiles[n - XS][0]
                        pool.wait_ge(x_turned, KT * (back + 1))
                    src = groups[g][3]
                    row = (n - first[g]) * P + (0 if g == 0 else groups[g][1] - CTX)
                    pool.dma_start(xt[:, n % XS, :], src[row:row + P, :]).then_inc(x_loaded[n % XS], 16)

            @block.tensor
            def _(pe):
                pe.wait_ge(ident_made, 2)
                pe.wait_ge(v_loaded, 16 * 6)
                pe.transpose(bank[0][:, 0:NV], vrow[:, :], ident[0:NV, 0:NV]).then_inc(v_turned, 1)
                pe.wait_ge(c_ready, 1)

                def modulation(n):
                    pe.wait_ge(aw_loaded[n % 2], 16 * (n // 2 + 1))
                    for t in range(AS // P):
                        f = n * (AS // P) + t
                        for k in range(KT):
                            mm = pe.matmul(bank[1][:, 2 * f:2 * f + 2], aw[:, n % 2, k, t * P:(t + 1) * P],
                                           sc[:, k, :], start=(k == 0), stop=(k == KT - 1))
                    mm.then_inc(aw_used, 1)

                for n in range(NAS):
                    modulation(n)
                for g, (w, t0, kind, _) in enumerate(groups):
                    for j in range(KT):
                        m = KT * g + j
                        pe.wait_ge(x_normed, first[g + 1])
                        if m >= 2:
                            pe.wait_ge(y_made, m - 1)
                        for r in range(w):
                            n = first[g] + r
                            mm = pe.transpose(bank[2 + m % 2][:, r * P:(r + 1) * P],
                                              xt[:, n % XS, j * P:(j + 1) * P], ident[:, :])
                        mm.then_inc(x_turned, 1)

            @block.scalar
            def _(act):
                act.wait_ge(vcol_made, 1)
                act.activation(th[:, :], vcol[:, VR["c"]:VR["c"] + 2 * KT], ACT.Tanh, scale=0.5).then_inc(c_tanh, 1)

                def squares(g):
                    for n in range(first[g], first[g + 1]):
                        act.wait_ge(x_loaded[n % XS], 16 * (n // XS + 1))
                        if n >= 1:
                            act.wait_ge(squared, n)
                        act.activation(sq[:, :], xt[:, n % XS, :], ACT.Square,
                                       accum_out=ss[:, n:n + 1]).then_inc(squared, 1)

                def root(g):
                    act.wait_ge(norm_dve, 2 * g + 1)
                    a, b = first[g], first[g + 1]
                    act.activation(rt[:, a:b], ms[:, a:b], ACT.Sqrt).then_inc(rooted, 1)

                squares(0)
                root(0)
                for g, (w, t0, kind, _) in enumerate(groups):
                    if g + 1 < len(groups):
                        squares(g + 1)
                        root(g + 1)
                    for j in range(KT):
                        m = KT * g + j
                        act.wait_ge(x_turned, m + 1)
                        if g == 0 and j == 0:
                            act.wait_ge(mod_dve, 4)
                        if m >= YS:
                            act.wait_ge(y_split, 2 * (m - YS + 1))
                        act.activation(y[:, m % YS, 0:w * P], bank[2 + m % 2][:, 0:w * P], ACT.Identity,
                                       bias=modB[:, j, kind:kind + 1], scale=modA[:, j, kind:kind + 1]).then_inc(y_made, 1)

            @block.vector
            def _(dve):
                dve.wait_ge(v_turned, 1)
                dve.tensor_copy(vcol[:, 0:NV], bank[0][:, 0:NV]).then_inc(vcol_made, 1)
                dve.wait_ge(vcol_made, 1)
                dve.wait_ge(c_tanh, 1)
                dve.scalar_tensor_tensor(out=s1[:, :], in0=th[:, :], scalar=1.0,
                                         in1=vcol[:, VR["c"]:VR["c"] + 2 * KT], op0=ALU.add,
                                         op1=ALU.mult).then_inc(vcol_made, 1)
                dve.wait_ge(vcol_made, 2)
                dve.tensor_scalar(sc[:, :, :], s1[:, :].rearrange("p (a j) -> p j a", a=2), 0.5, None,
                                  ALU.mult).then_inc(c_ready, 1)

                def scales(g):
                    a, b = first[g], first[g + 1]
                    dve.wait_ge(squared, b)
                    dve.tensor_scalar(ms[:, a:b], ss[:, a:b], 1.0 / D, EPS, ALU.mult, ALU.add).then_inc(norm_dve, 1)
                    dve.wait_ge(rooted, g + 1)
                    dve.reciprocal(rstd[:, a:b], rt[:, a:b]).then_inc(norm_dve, 1)
                    dve.wait_ge(norm_dve, 2 * g + 2)
                    for n in range(a, b):
                        dve.tensor_scalar(xt[:, n % XS, :], xt[:, n % XS, :], rstd[:, n:n + 1], None,
                                          ALU.mult).then_inc(x_normed, 1)

                scales(0)
                dve.wait_ge(aw_used, NAS)
                mod = bank[1][:, 0:6 * KT].rearrange("p (f a) -> p f a", a=2)
                for a in range(2):
                    dve.tensor_tensor(modB[:, :, a], mod[:, 0:KT, a], vcol[:, VR["ada"]:VR["ada"] + KT],
                                      ALU.add)
                    last = dve.tensor_tensor(sc1[:, :, a], mod[:, KT:2 * KT, a],
                                             vcol[:, VR["ada"] + KT:VR["ada"] + 2 * KT], ALU.add)
                last.then_inc(mod_dve, 1)
                dve.tensor_tensor(mgate[:, :], mod[:, 2 * KT:3 * KT, 0],
                                  vcol[:, VR["ada"] + 2 * KT:VR["ada"] + 3 * KT], ALU.add).then_inc(mod_dve, 1)
                dve.wait_ge(mod_dve, 2)
                for a in range(2):
                    dve.scalar_tensor_tensor(out=modA[:, :, a], in0=sc1[:, :, a], scalar=1.0,
                                             in1=vcol[:, VR["norm"]:VR["norm"] + KT], op0=ALU.add,
                                             op1=ALU.mult).then_inc(mod_dve, 1)
                dve.tensor_scalar(mgate[:, :], mgate[:, :], 0.5, None, ALU.mult).then_inc(mod_dve, 1)
                for g, (w, t0, kind, _) in enumerate(groups):
                    if g + 1 < len(groups):
                        scales(g + 1)
                    for j in range(KT):
                        m = KT * g + j
                        dve.wait_ge(y_made, m + 1)
                        n = w * P
                        dve.tensor_copy(xn(0, j, t0, n), y[:, m % YS, 0:n]).then_inc(y_split, 1)
                        dve.wait_ge(y_split, 2 * m + 1)
                        dve.tensor_tensor(xn(1, j, t0, n), y[:, m % YS, 0:n], f32(xn(0, j, t0, n)),
                                          ALU.subtract).then_inc(y_split, 1)
                dve.tensor_scalar(vcol[:, VR["pool"]:VR["pool"] + PG], vcol[:, VR["pool"]:VR["pool"] + PG],
                                  0.5, None, ALU.mult)


        HC = HEADS * NCH
        with ExitStack() as ph:
            def sb(name, shape, dt=FP32):
                return ph.enter_context(nc.sbuf_tensor(name, shape, dt))

            wg = sb("wg", [P, KT, NGATE])
            wgh = sb("wgh", [P, KT, NGATE], FP32R)
            wgl = sb("wgl", [P, KT, NGATE], FP32R)
            gbias = sb("gbias", [NGATE, 1])
            grow = sb("grow", [NGATE, TQ])
            gi = [sb(f"gi{d}", [HC, P]) for d in range(2)]
            gf = [sb(f"gf{d}", [HC, P]) for d in range(2)]
            gb = [sb(f"gb{d}", [HC, P]) for d in range(2)]
            gt = [sb(f"gt{d}", [HC, P]) for d in range(2)]
            gm = [sb(f"gm{d}", [HC, P]) for d in range(2)]
            gq = [sb(f"gq{d}", [HC, NQ, P]) for d in range(2)]
            ones = sb("ones", [HC, P])
            zeros = sb("zeros", [HC, P])
            ce = [sb(f"ce{d}", [HEADS, 2, NCH]) for d in range(2)]
            cm = [sb(f"cm{d}", [HEADS, NCH]) for d in range(2)]
            mprev = [sb(f"mprev{d}", [HC, 1]) for d in range(2)]
            nmend = [sb(f"nmend{d}", [HC, 1]) for d in range(2)]
            colst = sb("colst", [P, 2, NCH, NQ, HEADS])
            mpb = [sb(f"mpb{d}", [HC, P]) for d in range(2)]
            R_LF, R_CUM, R_A, R_ENDS = 4, 6, 8, 10
            R_CARRY = R_ENDS + 6
            R_M = R_CARRY + 4
            R_NEGM = R_M + 4
            R_QUANT = R_NEGM + 6
            

            g_loaded = sem("g_loaded"); g_hi = sem("g_hi"); g_lo = sem("g_lo"); g_done = sem("g_done")
            g_row = sem("g_row"); g_stored = sem("g_stored"); g_back = sem("g_back"); r_act = sem("r_act")
            r_dve = sem("r_dve"); ends_st = sem("ends_st"); ends_ld = sem("ends_ld"); mp_st = sem("mp_st")
            mp_ld = sem("mp_ld"); negm_st = sem("negm_st"); q_turned = sem("q_turned"); q_cols = sem("q_cols")
            cols_st = sem("cols_st")
            block = ph.enter_context(nc.Block())
            pieces = [(0, CTX)] + [(CTX + TQ * n, TQ) for n in range(NTQ)]

            @block.sync
            def _(sp):
                sp.dma_start(wg[:, :, :], in_v[:, :, GATE0:GATE0 + NGATE]).then_inc(g_loaded, 16)
                sp.dma_start(gbias[:, :], gate_b[0].rearrange("(a b) -> a b", b=1)).then_inc(g_loaded, 16)
                for n, (t0, w) in enumerate(pieces):
                    sp.wait_ge(g_row, n + 1)
                    sp.dma_start(gates_d[:, t0:t0 + w], grow[:, 0:w]).then_inc(g_stored, 16)
                sp.wait_ge(g_stored, 16 * len(pieces))
                for d in range(2):
                    for k, dst in ((0, gi[d]), (1, gf[d])):
                        r = 2 * HEADS * d + HEADS * k
                        sp.dma_start(dst[:, :], gates_d[r:r + HEADS, :].rearrange("h (c t) -> (h c) t", t=P))\
                            .then_inc(g_back, 16)
                sp.wait_ge(r_dve, R_ENDS)
                for d in range(2):
                    e = P - 1 if d == 0 else 0
                    sp.dma_start(ends_d[d, 0].rearrange("(a b) -> a b", b=1), gm[d][:, e:e + 1]).then_inc(ends_st, 16)
                    sp.dma_start(ends_d[d, 1].rearrange("(a b) -> a b", b=1), gb[d][:, e:e + 1]).then_inc(ends_st, 16)
                sp.wait_ge(ends_st, 64)
                for d in range(2):
                    sp.dma_start(ce[d][:, :, :], ends_d[d].rearrange("q (h c) -> h q c", h=HEADS)).then_inc(ends_ld, 16)
                sp.wait_ge(r_dve, R_CARRY)
                for d in range(2):
                    sp.dma_start(mprev_d[d].rearrange("(h c) -> h c", h=HEADS), cm[d][:, :]).then_inc(mp_st, 16)
                sp.wait_ge(mp_st, 32)
                for d in range(2):
                    sp.dma_start(mprev[d][:, :], mprev_d[d].rearrange("(a b) -> a b", b=1)).then_inc(mp_ld, 16)
                sp.wait_ge(r_dve, R_NEGM)
                for d in range(2):
                    sp.dma_start(negm_d[d].rearrange("h c t -> (h c) t"), gt[d][:, :]).then_inc(negm_st, 16)
                sp.wait_ge(q_cols, 2 * NQ)
                sp.dma_start(cols_d, colst[:, :, :, :, :]).then_inc(cols_st, 16)
                sp.wait_ge(negm_st, 32)
                sp.wait_ge(cols_st, 16)

            @block.scalar
            def _(act):
                act.wait_ge(g_loaded, 32)
                act.activation(wgh[:, :, :], wg[:, :, :], ACT.Copy).then_inc(g_hi, 1)
                for n, (t0, w) in enumerate(pieces):
                    act.wait_ge(g_done, n + 1)
                    if n >= 1:
                        act.wait_ge(g_stored, 16 * n)
                    act.activation(grow[:, 0:w], bank[n % 2][0:NGATE, 0:w], ACT.Identity,
                                   bias=gbias[:, 0:1]).then_inc(g_row, 1)
                act.wait_ge(g_back, 64)
                for d in range(2):
                    act.activation(gt[d][:, :], gf[d][:, :], ACT.Abs).then_inc(r_act, 1)
                act.wait_ge(r_act, 2)
                for d in range(2):
                    act.activation(gm[d][:, :], gt[d][:, :], ACT.Exp, scale=-1.0).then_inc(r_act, 1)
                act.wait_ge(r_act, 4)
                for d in range(2):
                    act.activation(gb[d][:, :], gm[d][:, :], ACT.Ln, bias=1.0).then_inc(r_act, 1)
                act.wait_ge(r_dve, R_QUANT)
                for d in range(2):
                    act.activation(gq[d][:, 1, :], gm[d][:, :], ACT.Exp, bias=mprev[d][:, 0:1], scale=-1.0)
                    act.activation(gq[d][:, 2, :], gf[d][:, :], ACT.Exp, scale=-1.0)
                    act.activation(gq[d][:, 3, :], gi[d][:, :], ACT.Exp, bias=nmend[d][:, 0:1])
                    act.activation(gq[d][:, 4, :], mpb[d][:, :], ACT.Exp, bias=nmend[d][:, 0:1]).then_inc(r_act, 1)

            @block.vector
            def _(dve):
                dve.wait_ge(g_hi, 1)
                dve.tensor_tensor(wgl[:, :, :], wg[:, :, :], f32(wgh[:, :, :]), ALU.subtract).then_inc(g_lo, 1)
                dve.memset(ones[:, :], 1.0).then_inc(r_dve, 1)
                dve.memset(zeros[:, :], 0.0).then_inc(r_dve, 1)
                dve.wait_ge(r_dve, 2)
                dve.wait_ge(r_act, 6)
                for d in range(2):
                    dve.scalar_tensor_tensor(out=gf[d][:, :], in0=gf[d][:, :], scalar=0.0, in1=gb[d][:, :],
                                             op0=ALU.min, op1=ALU.subtract).then_inc(r_dve, 1)
                dve.wait_ge(r_dve, R_LF)
                fwd = [slice(None), slice(None, None, -1)]
                for d in range(2):
                    s = fwd[d]
                    dve.tensor_tensor_scan(gb[d][:, s], ones[:, :], gf[d][:, s], 0.0, ALU.mult,
                                           ALU.add).then_inc(r_dve, 1)
                dve.wait_ge(r_dve, R_CUM)
                for d in range(2):
                    dve.tensor_tensor(gi[d][:, :], gi[d][:, :], gb[d][:, :], ALU.subtract).then_inc(r_dve, 1)
                dve.wait_ge(r_dve, R_A)
                for d in range(2):
                    s = fwd[d]
                    dve.tensor_tensor_scan(gm[d][:, s], zeros[:, :], gi[d][:, s], -3e38, ALU.add,
                                           ALU.max).then_inc(r_dve, 1)
                dve.wait_ge(ends_ld, 32)
                for d in range(2):
                    order = list(range(NCH)) if d == 0 else list(range(NC - 1, -1, -1)) + list(range(NCH - 1, NC - 1, -1))
                    dve.memset(cm[d][:, order[0]:order[0] + 1], M_INIT).then_inc(r_dve, 1)
                    if d == 0:
                        dve.wait_ge(r_dve, R_ENDS + 1)
                        dve.tensor_tensor_scan(cm[0][:, 1:NCH], ce[0][:, 0, 0:NCH - 1], ce[0][:, 1, 0:NCH - 1],
                                               M_INIT, ALU.max, ALU.add).then_inc(r_dve, 1)
                    else:
                        dve.wait_ge(r_dve, R_ENDS + 3)
                        dve.tensor_tensor_scan(cm[1][:, 0:1], ce[1][:, 0, 1:2], ce[1][:, 1, 1:2],
                                               M_INIT, ALU.max, ALU.add).then_inc(r_dve, 1)
                        dve.wait_ge(r_dve, R_ENDS + 4)
                        dve.tensor_tensor_scan(cm[1][:, NCH - 1:NCH], ce[1][:, 0, 0:1], ce[1][:, 1, 0:1],
                                               cm[1][:, 0:1], ALU.max, ALU.add).then_inc(r_dve, 1)
                        dve.wait_ge(r_dve, R_ENDS + 5)
                        dve.tensor_tensor_scan(cm[1][:, NCH - 2:NC - 1:-1], ce[1][:, 0, NCH - 1:NC:-1],
                                               ce[1][:, 1, NCH - 1:NC:-1], cm[1][:, NCH - 1:NCH],
                                               ALU.max, ALU.add).then_inc(r_dve, 1)
                dve.wait_ge(mp_ld, 32)
                for d in range(2):
                    dve.tensor_scalar(gm[d][:, :], gm[d][:, :], mprev[d][:, 0:1], None, ALU.max).then_inc(r_dve, 1)
                    dve.tensor_scalar(mpb[d][:, :], zeros[:, :], mprev[d][:, 0:1], None, ALU.add).then_inc(r_dve, 1)
                dve.wait_ge(r_dve, R_M)
                for d in range(2):
                    e = P - 1 if d == 0 else 0
                    dve.tensor_scalar(gt[d][:, :], gm[d][:, :], -1.0, None, ALU.mult).then_inc(r_dve, 1)
                    dve.tensor_scalar(nmend[d][:, :], gm[d][:, e:e + 1], -1.0, None, ALU.mult).then_inc(r_dve, 1)
                for d in range(2):
                    dve.tensor_tensor(gf[d][:, :], gb[d][:, :], gm[d][:, :], ALU.add).then_inc(r_dve, 1)
                    dve.tensor_copy(gq[d][:, 0, :], gi[d][:, :]).then_inc(r_dve, 1)
                dve.wait_ge(r_dve, R_NEGM + 4)
                for d in range(2):
                    dve.tensor_scalar(gf[d][:, :], gf[d][:, :], -88.0, None, ALU.max).then_inc(r_dve, 1)
                for n in range(2 * NQ):
                    d, q = n // NQ, n % NQ
                    dve.wait_ge(q_turned, n + 1)
                    dve.tensor_copy(colst[:, d, :, q, :],
                                    bank[2 + n % 2][:, 0:HC].rearrange("p (h c) -> p c h", h=HEADS)).then_inc(q_cols, 1)

            @block.tensor
            def _(pe):
                pe.wait_ge(g_lo, 1)
                for n, (t0, w) in enumerate(pieces):
                    if n >= 2:
                        pe.wait_ge(g_row, n - 1)
                    for k in range(KT):
                        for n3, (a, b) in enumerate(((wgh, 0), (wgh, 1), (wgl, 0))):
                            mm = pe.matmul(bank[n % 2][0:NGATE, 0:w], a[:, k, :], xn(b, k, t0, w),
                                           start=(k == 0 and n3 == 0), stop=(k == KT - 1 and n3 == 2))
                    mm.then_inc(g_done, 1)
                pe.wait_ge(r_act, 8)
                for n in range(2 * NQ):
                    d, q = n // NQ, n % NQ
                    if n >= 2:
                        pe.wait_ge(q_cols, n - 1)
                    pe.transpose(bank[2 + n % 2][:, 0:HC], gq[d][:, q, :], ident[0:HC, 0:HC]).then_inc(q_turned, 1)

        with ExitStack() as ph:
            def sb(name, shape, dt=FP32):
                return ph.enter_context(nc.sbuf_tensor(name, shape, dt))

            wraw = sb("wraw", [P, 2, KT, P])
            wh = sb("wh", [P, 2, KT, P], FP32R)
            wl = sb("wl", [P, 2, KT, P], FP32R)
            qks = sb("qks", [P, 2, 4, 2, P], FP32R)
            ymaj = sb("ymaj", [P, 2, TQ])
            kts = sb("kts", [P, 2, 4, P])
            vs = sb("vs", [P, 2, 4, 2, P], FP32R)
            pzs = sb("pzs", [P, 2, TQ])
            tz = sb("tz", [P, TQ])

            w_loaded = [sem(f"w_loaded{n}") for n in range(2)]
            w_hi = sem("w_hi"); w_lo = sem("w_lo")
            piece_done = sem("piece_done"); piece_read = sem("piece_read")
            qk_hi = sem("qk_hi"); qk_stored = [sem(f"qk_stored{n}") for n in range(2)]
            y_copied = sem("y_copied"); turned = sem("turned")
            turned_read = sem("turned_read"); v_hi = sem("v_hi")
            kt_stored = [sem(f"kt_stored{n}") for n in range(2)]
            v_stored = [sem(f"v_stored{n}") for n in range(2)]
            pz_stored = [sem(f"pz_stored{n}") for n in range(2)]
            tz_made = sem("tz_made"); xe_stored = sem("xe_stored")

            UNITS = [(t, kind) for t in range(HB) for kind in "qkv"] + [(0, "p"), (0, "s")]
            OFF = {"q": (Q0, HD), "k": (K0, HD), "v": (V0, HD), "p": (POOL0, P), "s": (ZP0, P)}
            cpiece, xpieces = (0, CTX), [(CTX + TQ * n, TQ) for n in range(NTQ)]
            PIECES = [(u, t, kind, t0, w) for u, (t, kind) in enumerate(UNITS)
                      for t0, w in ([cpiece] if kind in "kv" else []) + xpieces]
            NU, NPC = len(UNITS), len(PIECES)
            nqk = [sum(p[2] in "qk" for p in PIECES[:m]) for m in range(NPC + 1)]
            ntr = [sum(p[2] in "kv" for p in PIECES[:m]) for m in range(NPC + 1)]
            nk = [sum(p[2] == "k" for p in PIECES[:m]) for m in range(NPC + 1)]
            nv = [sum(p[2] == "v" for p in PIECES[:m]) for m in range(NPC + 1)]
            def unit_end(u):
                return NPC + 1 + max(m for m in range(NPC) if PIECES[m][0] == u)

            npz = [sum(p[2] in "ps" for p in PIECES[:m]) for m in range(NPC + 1)]
            assert NU % 2 == 0 and NPC % 4 == 0 and nqk[-1] % 2 == 0 and ntr[-1] % 2 == 0 and nk[-1] % 2 == 0
            block = ph.enter_context(nc.Block())

            def heads(eng, body):
                with eng.Fori(0, HEADS - 1) as i:
                    body(i, True)
                body(HEADS - 1, False)

            @block.sync
            def _(sp):
                def tile(i, u):
                    t, kind = UNITS[u % NU]
                    first_col, per_head = OFF[kind]
                    sp.wait_ge(w_hi, i * NU + (u + 1))
                    sp.wait_ge(w_lo, i * NU + (u + 1))
                    sp.dma_start(wraw[:, u % 2],
                                 in_v[:, :, bass.ds(i * per_head + (first_col + t * P + (u // NU) * per_head), P)])\
                        .then_inc(w_loaded[u % 2], 16)

                def store_turned(i, m):
                    u, t, kind, t0, w = PIECES[m]
                    r, cw, c0 = ntr[m], w // P, t0 // P
                    sp.wait_ge(turned_read, i * ntr[-1] + (r + 1 + 2))
                    if kind == "k":
                        sp.dma_start(kt_d[i, c0:c0 + cw, :, t * P:(t + 1) * P].rearrange("c p f -> p c f"),
                                     kts[:, nk[m] % 2, 0:cw]).then_inc(kt_stored[nk[m] % 2], 16)
                    else:
                        sp.dma_start(v_d[i, c0:c0 + cw, :, t].rearrange("c p a f -> p c (a f)"),
                                     f32(vs[:, nv[m] % 2, 0:cw]).rearrange("p c a f -> p c (a f)"))\
                            .then_inc(v_stored[nv[m] % 2], 16)

                def body(i, ahead):
                    for m, (u, t, kind, t0, w) in enumerate(PIECES):
                        if (m == 0 or PIECES[m - 1][0] != u) and (u + 3 < NU or ahead):
                            tile(i, u + 3)
                        cw, c0 = w // P, t0 // P
                        if kind in "qk":
                            a = nqk[m]
                            sp.wait_ge(piece_read, i * NPC + (m + 1 + 4))
                            sp.dma_start(qk_d[i, "qk".index(kind), t, :, c0:c0 + cw].rearrange("p c a t -> p (c a t)"),
                                         f32(qks[:, a % 2, 0:cw]).rearrange("p c a t -> p (c a t)"))\
                                .then_inc(qk_stored[a % 2], 16)
                        if kind in "ps":
                            a = npz[m]
                            sp.wait_ge(piece_read, i * NPC + (m + 1 + 4))
                            sp.dma_start((p_d if kind == "p" else zp_d)[i, :, t0 - CTX:t0 - CTX + w],
                                         pzs[:, a % 2, 0:w]).then_inc(pz_stored[a % 2], 16)
                        if m >= 1 and PIECES[m - 1][2] in "kv":
                            store_turned(i, m - 1)

                for u in range(3):
                    tile(0, u)
                heads(sp, body)
                for n in range(2):
                    sp.wait_ge(pz_stored[n], 16 * HEADS * npz[-1] // 2)
                    sp.wait_ge(qk_stored[n], 16 * HEADS * nqk[-1] // 2)
                    sp.wait_ge(kt_stored[n], 16 * HEADS * nk[-1] // 2)
                    sp.wait_ge(v_stored[n], 16 * HEADS * nv[-1] // 2)

            @block.gpsimd
            def _(pool):
                for part in range(2):
                    pool.dma_start(xe_d[part], f32(xearly[part][:, :, CTX:CTX + HALF])).then_inc(xe_stored, 16)
                pool.wait_ge(xe_stored, 32)

            @block.tensor
            def _(pe):
                pe.sem_inc(piece_done, NPC)
                pe.sem_inc(turned, 2)

                def turn(i, m):
                    u, t, kind, t0, w = PIECES[m]
                    r = ntr[m]
                    if kind == "k":
                        pe.wait_ge(y_copied, i * nk[-1] + (nk[m] + 1))
                    else:
                        pe.wait_ge(piece_read, i * NPC + (m + 1 + 4))
                    pe.wait_ge(turned_read, i * ntr[-1] + (r + 1))
                    for b in range(w // P):
                        mm = pe.transpose(bank[4 + r % 2][:, b * P:(b + 1) * P],
                                          ymaj[:, r % 2, b * P:(b + 1) * P], ident[:, :])
                    mm.then_inc(turned, 1)

                with pe.Fori(0, HEADS) as i:
                    for m, (u, t, kind, t0, w) in enumerate(PIECES):
                        if m == 0 or PIECES[m - 1][0] != u:
                            pe.wait_ge(w_hi, i * NU + (u + 1 + 2))
                            pe.wait_ge(w_lo, i * NU + (u + 1 + 2))
                        pe.wait_ge(piece_read, i * NPC + (m + 1))
                        for k in range(KT):
                            for n, (a, b) in enumerate(((wh, 0), (wh, 1), (wl, 0))):
                                mm = pe.matmul(bank[m % 4][:, 0:w], a[:, u % 2, k, :], xn(b, k, t0, w),
                                               start=(k == 0 and n == 0), stop=(k == KT - 1 and n == 2))
                        mm.then_inc(piece_done, 1)
                        if m >= 1 and PIECES[m - 1][2] in "kv":
                            turn(i, m - 1)

            @block.scalar
            def _(act):
                act.sem_inc(w_hi, 2)

                def turned_hi(i, m):
                    u, t, kind, t0, w = PIECES[m]
                    if kind == "v":
                        r, a, cw = ntr[m], nv[m], w // P
                        act.wait_ge(turned, i * ntr[-1] + (r + 1 + 2))
                        act.wait_ge(v_stored[a % 2], i * (16 * nv[-1] // 2) + 16 * (a // 2))
                        act.activation(vs[:, a % 2, 0:cw, 0, :],
                                       bank[4 + r % 2][:, 0:w].rearrange("p (c t) -> p c t", t=P),
                                       ACT.Copy).then_inc(v_hi, 1)

                def split_hi(i, u):
                    act.wait_ge(w_loaded[u % 2], i * (16 * NU // 2) + 16 * (u // 2 + 1))
                    if u >= 2:
                        act.wait_ge(piece_done, i * NPC + unit_end(u - 2))
                    act.activation(wh[:, u % 2], wraw[:, u % 2], ACT.Copy).then_inc(w_hi, 1)

                split_hi(0, 0)
                split_hi(0, 1)

                def body(i, ahead):
                    for m, (u, t, kind, t0, w) in enumerate(PIECES):
                        scale = HD ** -0.5 if kind == "k" else 1.0
                        if kind in "qk":
                            a, cw = nqk[m], w // P
                            act.wait_ge(piece_done, i * NPC + (NPC + m + 1))
                            if kind == "k":
                                act.wait_ge(turned, i * ntr[-1] + (ntr[m] + 1))
                                act.activation(ymaj[:, ntr[m] % 2, 0:w], bank[m % 4][:, 0:w], ACT.Copy,
                                               scale=scale).then_inc(y_copied, 1)
                            act.wait_ge(qk_stored[a % 2], i * (16 * nqk[-1] // 2) + 16 * (a // 2))
                            act.activation(qks[:, a % 2, 0:cw, 0, :],
                                           bank[m % 4][:, 0:w].rearrange("p (c t) -> p c t", t=P),
                                           ACT.Copy, scale=scale).then_inc(qk_hi, 1)
                        if kind == "s":
                            act.wait_ge(piece_done, i * NPC + (NPC + m + 1))
                            act.wait_ge(piece_read, i * NPC + (m + 4))
                            act.activation(tz[:, 0:w], bank[m % 4][:, 0:w], ACT.Tanh, scale=0.5).then_inc(tz_made, 1)
                        if m >= 1 and PIECES[m - 1][2] in "kv":
                            turned_hi(i, m - 1)
                        if (m + 1 == NPC or PIECES[m + 1][0] != u) and (u + 2 < NU or ahead):
                            split_hi(i, u + 2)

                heads(act, body)

            @block.vector
            def _(dve):
                dve.sem_inc(w_lo, 2)
                dve.sem_inc(piece_read, 4)
                dve.sem_inc(turned_read, 2)

                def turned_lo(i, m):
                    u, t, kind, t0, w = PIECES[m]
                    r, cw = ntr[m], w // P
                    src = bank[4 + r % 2][:, 0:w].rearrange("p (c t) -> p c t", t=P)
                    if kind == "k":
                        a = nk[m]
                        dve.wait_ge(turned, i * ntr[-1] + (r + 1 + 2))
                        dve.wait_ge(kt_stored[a % 2], i * (16 * nk[-1] // 2) + 16 * (a // 2))
                        dve.tensor_copy(kts[:, a % 2, 0:cw], src).then_inc(turned_read, 1)
                    else:
                        a = nv[m]
                        dve.wait_ge(v_hi, i * nv[-1] + (a + 1))
                        dve.tensor_tensor(vs[:, a % 2, 0:cw, 1, :], src, f32(vs[:, a % 2, 0:cw, 0, :]),
                                          ALU.subtract).then_inc(turned_read, 1)

                def split_lo(i, u):
                    dve.wait_ge(w_hi, i * NU + (u + 1 + 2))
                    dve.tensor_tensor(wl[:, u % 2], wraw[:, u % 2], f32(wh[:, u % 2]), ALU.subtract).then_inc(w_lo, 1)

                split_lo(0, 0)
                split_lo(0, 1)

                def body(i, ahead):
                    for m, (u, t, kind, t0, w) in enumerate(PIECES):
                        if kind in "qk":
                            a, cw = nqk[m], w // P
                            dve.wait_ge(qk_hi, i * nqk[-1] + (a + 1))
                            dve.scalar_tensor_tensor(
                                out=qks[:, a % 2, 0:cw, 1, :],
                                in0=bank[m % 4][:, 0:w].rearrange("p (c t) -> p c t", t=P),
                                scalar=HD ** -0.5 if kind == "k" else 1.0, in1=f32(qks[:, a % 2, 0:cw, 0, :]),
                                op0=ALU.mult, op1=ALU.subtract).then_inc(piece_read, 1)
                        elif kind in "ps":
                            a = npz[m]
                            dve.wait_ge(pz_stored[a % 2], i * (16 * npz[-1] // 2) + 16 * (a // 2))
                            if kind == "p":
                                dve.wait_ge(piece_done, i * NPC + (NPC + m + 1))
                                dve.tensor_copy(pzs[:, a % 2, 0:w], bank[m % 4][:, 0:w]).then_inc(piece_read, 1)
                            else:
                                dve.wait_ge(tz_made, i * NTQ + (a - NTQ + 1))
                                dve.scalar_tensor_tensor(out=pzs[:, a % 2, 0:w], in0=tz[:, 0:w], scalar=1.0,
                                                         in1=bank[m % 4][:, 0:w], op0=ALU.add,
                                                         op1=ALU.mult).then_inc(piece_read, 1)
                        else:
                            dve.wait_ge(piece_done, i * NPC + (NPC + m + 1))
                            dve.wait_ge(turned, i * ntr[-1] + (ntr[m] + 1))
                            dve.tensor_copy(ymaj[:, ntr[m] % 2, 0:w], bank[m % 4][:, 0:w]).then_inc(piece_read, 1)
                        if m >= 1 and PIECES[m - 1][2] in "kv":
                            turned_lo(i, m - 1)
                        if (m + 1 == NPC or PIECES[m + 1][0] != u) and (u + 2 < NU or ahead):
                            split_lo(i, u + 2)

                heads(dve, body)

        early.close()
        with ExitStack() as ph:
            def sb(name, shape, dt=FP32):
                return ph.enter_context(nc.sbuf_tensor(name, shape, dt))

            wraw = sb("wraw4", [P, 2, KT, P])
            wh = sb("wh4", [P, 2, KT, P], FP32R)
            wl = sb("wl4", [P, 2, KT, P], FP32R)
            tanh_o = sb("tanh_o", [P, 2, TQ])
            tanh_z = sb("tanh_z", [P, TQ])
            zgate = sb("zgate", [P, TQ])
            ustage = sb("ustage", [P, 2, TQ])
            gstage = sb("gstage", [P, 2, TQ])
            NCHAIN = 2 * HEADS
            state = sb("state", [P, NCHAIN, HB, VW])
            state_h = sb("state_h", [P, 2, HB, VW], FP32R)
            state_l = sb("state_l", [P, 2, HB, VW], FP32R)
            qk_t = sb("qk_t", [P, 2, 2, HB, 2, P], FP32R)
            v_t = sb("v_t", [P, 2, 2, VW], FP32R)
            kt_t = sb("kt_t", [P, 2, HD])
            nm = sb("nm", [P, 2, 2, HEADS, P])
            cmask = sb("cmask", [P, 2, P])
            cols = sb("cols", [P, 2, NCH, NQ * HEADS])
            ccol = sb("ccol", [P, 2, 2, NQ, HEADS])
            wexp = sb("wexp", [P, 2, P])
            pf = sb("pf", [P, 2, P])
            p_h = sb("p_h", [P, 2, P], FP32R)
            p_l = sb("p_l", [P, 2, P], FP32R)
            ek_h = sb("ek_h", [P, 2, HD], FP32R)
            ek_l = sb("ek_l", [P, 2, HD], FP32R)
            ysb = sb("ysb", [P, 2, VW])
            num = sb("num", [P, 2, VW])
            den = sb("den", [P, 2, 3])
            hout = sb("hout", [P, 2, HD])
            hother = sb("hother", [P, 2, HD])
            PADR = GRID_H + max(2, 16)
            pool_a = sb("pool_a", [P, PADR * GRID_W])
            pool_b = sb("pool_b", [P, PADR * GRID_W])
            icnt = sb("icnt", [P, 2, GRID_W])

            w_loaded = [sem(f"w4_loaded{n}") for n in range(2)]
            w_hi = sem("w4_hi"); w_lo = sem("w4_lo"); piece_done = sem("piece4_done")
            act_read = sem("act_read"); u_made = sem("u_made"); dz = sem("dz")
            u_stored = [sem(f"u_stored{n}") for n in range(2)]
            g_stored = [sem(f"g4_stored{n}") for n in range(2)]
            qk_loaded = [sem(f"qk_loaded{n}") for n in range(2)]
            vk_loaded = [sem(f"vk_loaded{n}") for n in range(2)]
            nm_loaded = [sem(f"nm_loaded{n}") for n in range(2)]
            cols_loaded = sem("cols_loaded"); x_back = [sem(f"x_back{n}") for n in range(2)]; setup = sem("setup"); state_zero = sem("state_zero"); mask_made = sem("mask_made")
            chunk_cols = sem("chunk_cols"); s_done = sem("s_done"); w_exp = sem("w_exp"); s_hi = sem("s_hi")
            ek_hi = sem("ek_hi"); prep = sem("prep"); ek_lo = sem("ek_lo"); step_done = sem("step_done")
            y_read = sem("y_read"); nm_masked = sem("nm_masked"); zg = sem("zg"); fin = sem("fin"); state_new = sem("state_new")
            h_stored = [sem(f"h_stored{n}") for n in range(2)]
            h_back = [sem(f"h_back{n}") for n in range(2)]
            p_loaded = sem("p_loaded"); box = sem("box"); mix_stored = sem("mix_stored")

            CTX_UBANK = [bank[0:2], bank[2:4]]
            UBANK, XBANK, YBANK, SBANK = bank[2:4], bank[4], bank[5], bank[6]

            STEPS = [(cc, h, d) for cc in range(2) for h in range(HEADS) for d in range(2)]
            NS = len(STEPS)
            TILES = [(k, e) for e in range(2) for k in ("o", "z")] + [(k, e) for e in range(2) for k in ("m", "p")]
            OFF4 = {"o": O0, "z": Z0, "m": GM0, "p": GP0}
            PIECES = [(u, kind, e, tq) for u, (kind, e) in enumerate(TILES) for tq in range(2)]
            NU, NPC = len(TILES), len(PIECES)
            nz = [sum(p[1] == "z" for p in PIECES[:m]) for m in range(NPC + 1)]
            na = [sum(p[1] != "z" for p in PIECES[:m]) for m in range(NPC + 1)]
            ng = [sum(p[1] in "mp" for p in PIECES[:m]) for m in range(NPC + 1)]
            assert NPC == NS and NPC % 4 == 0 and nz[-1] % 2 == 0 and ng[-1] % 2 == 0
            NTRIP = NX // 2
            NCS = NS

            HALFTRIPS = NTRIP // 2

            def trips(eng, body):
                with eng.Fori(0, HALFTRIPS - 1) as i:
                    body(i, True)
                body(HALFTRIPS - 1, True)
                with eng.Fori(HALFTRIPS, NTRIP - 1) as i:
                    body(i, True)
                body(NTRIP - 1, False)

            def half_of(i):
                return int((i if isinstance(i, int) else i.max_val) < HALFTRIPS)

            def row(i):
                return i if half_of(i) else i - HALFTRIPS

            def chunk(i, cc, d):
                return i * 2 + (NC + cc) if d == 0 else i * -2 + (NCH - 1 - cc)

            def ctx_chunk(cc, d):
                return cc if d == 0 else NC - 1 - cc

            def chain(h, d):
                return d * HEADS + h

            block = ph.enter_context(nc.Block())

            @block.sync
            def _(sp):
                sp.dma_start(cols[:, :, :, :], cols_d.rearrange("p d c q h -> p d c (q h)")).then_inc(cols_loaded, 16)

                def operands(s, L, h, c, latent):
                    sp.wait_ge(step_done, s + 1)
                    if latent:
                        sp.dma_start(f32(qk_t[:, L]).rearrange("p o b a t -> p (o b) (a t)"),
                                     qk_d[h, :, :, :, c].rearrange("o b p a t -> p (o b) (a t)"))\
                            .then_inc(qk_loaded[L], 16)
                    for a in range(2):
                        sp.dma_start(f32(v_t[:, L, a, 0:HD]).rearrange("p (b f) -> p b f", b=HB),
                                     v_d[h, c, :, :, a]).then_inc(vk_loaded[L], 16)
                    sp.dma_start(kt_t[:, L], kt_d[h, c]).then_inc(vk_loaded[L], 16)

                def tile(i, r, u):
                    kind, e = TILES[u]
                    sp.wait_ge(w_hi, i * NU + (u + 1))
                    sp.wait_ge(w_lo, i * NU + (u + 1))
                    sp.dma_start(wraw[:, u % 2], in_v[:, :, bass.ds(r * (2 * P) + (OFF4[kind] + e * P), P)])\
                        .then_inc(w_loaded[u % 2], 16)

                def store(i, st):
                    cc, h, d = STEPS[st]
                    u, kind, e, tq = PIECES[st]
                    r, half = row(i), half_of(i)
                    t0 = half * HALF + tq * TQ
                    if kind == "z":
                        sp.wait_ge(u_made, i * nz[-1] + (nz[-1] + nz[st] + 1))
                        sp.dma_start(u_d[r * 2 + e, :, t0:t0 + TQ], ustage[:, nz[st] % 2, :])\
                            .then_inc(u_stored[nz[st] % 2], 16)
                    elif kind in "mp":
                        sp.wait_ge(act_read, i * na[-1] + (na[-1] + na[st] + 1))
                        sp.dma_start((gm_d if kind == "m" else gp_d)[r * 2 + e, :, t0:t0 + TQ],
                                     gstage[:, ng[st] % 2, :]).then_inc(g_stored[ng[st] % 2], 16)
                    sp.wait_ge(fin, i * (5 * NS) + 5 * (st + 1))
                    dst = h_d if half_of(i) else hsum_d
                    sp.dma_start(dst[chunk(i, cc, d) - NC, :, h * HD:(h + 1) * HD], hout[:, st % 2, :])\
                        .then_inc(h_stored[st % 2], 16)

                def maxima(i, cc):
                    n, slot = cc + 1, (cc + 1) % 2
                    sp.wait_ge(w_exp, i * NS + NCHAIN * (cc + 1))
                    for dd in range(2):
                        sp.dma_start(nm[:, slot, dd], negm_d[dd, :, chunk(i, n, dd), :].partition_broadcast(P))\
                            .then_inc(nm_loaded[slot], 16)

                def latent_operands(i, st):
                    cc, h, d = STEPS[st % NS]
                    operands(i * NS + (NCS + st), st % 2, h, chunk(i, cc + 2 * (st // NS), d), True)

                def other_direction(i, st):
                    cc, h, d = STEPS[st % NS]
                    sp.wait_ge(h_stored[1 - d], 16 * (NS * HALFTRIPS // 2 - HEADS + h + 1))
                    sp.dma_start(hother[:, st % 2, :],
                                 h_d[chunk(i, cc + 2 * (st // NS), d) - NC, :, h * HD:(h + 1) * HD])\
                        .then_inc(h_back[st % 2], 16)

                def early_quarter(tq):
                    sp.wait_ge(piece_done, NPC * HALFTRIPS + NPC - 1 + tq)
                    for part in range(2):
                        sp.dma_start(f32(xlate[part][:, :, tq * TQ:(tq + 1) * TQ]),
                                     xe_d[part, :, :, tq * TQ:(tq + 1) * TQ]).then_inc(x_back[tq], 16)

                def body(i, ahead):
                    swap = isinstance(i, int) and i == HALFTRIPS - 1
                    for st, (cc, h, d) in enumerate(STEPS):
                        if st % NCHAIN == NCHAIN // 2 and (cc == 0 or ahead):
                            maxima(i, cc)
                        if st % 2 == 0:
                            u = st // 2 + 2
                            if u < NU:
                                tile(i, row(i), u)
                            elif ahead:
                                last = isinstance(i, int) and i == HALFTRIPS - 1
                                tile(i + 1, 0 if last else row(i) + 1, u - NU)
                        if swap and st == NS - 1:
                            early_quarter(0)
                        if st + 2 < NS or ahead:
                            latent_operands(i, st + 2)
                        if swap and st == NS - 1:
                            early_quarter(1)
                        store(i, st)
                        if (half_of(i) == 0 and (st + 2 < NS or ahead)) or (swap and st + 2 >= NS):
                            other_direction(i, st + 2)

                for st, (cc, h, d) in enumerate(STEPS):
                    if st == 2:
                        for u in range(2):
                            tile(0, 0, u)
                        maxima(0, -1)
                    operands(st, st % 2, h, ctx_chunk(cc, d), False)
                for st in range(2):
                    latent_operands(0, st)
                trips(sp, body)
                for n in range(2):
                    sp.wait_ge(u_stored[n], 16 * NTRIP * nz[-1] // 2)
                    sp.wait_ge(g_stored[n], 16 * NTRIP * ng[-1] // 2)
                    sp.wait_ge(h_stored[n], 16 * NTRIP * NS // 2)

            @block.tensor
            def _(pe):
                pe.sem_inc(piece_done, NPC)
                pe.sem_inc(step_done, 2)
                pe.wait_ge(setup, 2)

                def scores(l, i, st):
                    L = st % 2
                    pe.wait_ge(qk_loaded[L], i * (16 * NS // 2) + 16 * (st // 2 + 1))
                    pe.wait_ge(prep, l * 3)
                    for b in range(HB):
                        for n, (ka, qa) in enumerate(((0, 0), (0, 1), (1, 0))):
                            mm = pe.matmul(SBANK[:, 0:P], qk_t[:, L, 1, b, ka, :], qk_t[:, L, 0, b, qa, :],
                                           start=(b == 0 and n == 0), stop=(b == HB - 1 and n == 2))
                    mm.then_inc(s_done, 1)

                def step(s, l, L, vk):
                    ubank = UBANK if l is not None else CTX_UBANK[L]
                    pe.wait_ge(state_new, s + NCHAIN - (1 if l is None else 0))
                    pe.wait_ge(vk_loaded[L], vk)
                    if l is not None:
                        pe.wait_ge(s_hi, l + 1)
                        pe.wait_ge(prep, l * 3 + 3)
                        for b in range(HB):
                            for n, (qa, c_) in enumerate(((0, state_h), (0, state_l), (1, state_h))):
                                pe.matmul(XBANK[:, 0:VW], qk_t[:, L, 0, b, qa, :], c_[:, L, b, :],
                                          start=(b == 0 and n == 0), stop=(b == HB - 1 and n == 2))
                        for n, (p_, va) in enumerate(((p_h, 0), (p_h, 1), (p_l, 0))):
                            pe.matmul(YBANK[:, 0:VW], p_[:, L, :], v_t[:, L, va, :], start=(n == 0), stop=(n == 2))
                    pe.wait_ge(ek_hi, s + 1)
                    pe.wait_ge(ek_lo, s + 1)
                    for b in range(HB):
                        for n, (e_, va) in enumerate(((ek_h, 0), (ek_h, 1), (ek_l, 0))):
                            mm = pe.matmul(ubank[b][:, 0:VW], e_[:, L, b * P:(b + 1) * P],
                                           v_t[:, L, va, :], start=(n == 0), stop=(n == 2))
                    mm.then_inc(step_done, 1)

                def piece(i, m):
                    u, kind, e, tq = PIECES[m]
                    if tq == 0:
                        pe.wait_ge(w_hi, i * NU + (u + 1 + 2))
                        pe.wait_ge(w_lo, i * NU + (u + 1 + 2))
                    if half_of(i) == 0:
                        pe.wait_ge(x_back[tq], 32)
                    pm, trip = (m - 2) % NPC, (1 if m >= 2 else 0)
                    if PIECES[pm][1] == "z":
                        pe.wait_ge(u_made, i * nz[-1] + (nz[-1] * trip + nz[pm] + 1))
                    else:
                        pe.wait_ge(act_read, i * na[-1] + (na[-1] * trip + na[pm] + 1))
                    for k in range(KT):
                        for n, (a, part) in enumerate(((wh, 0), (wh, 1), (wl, 0))):
                            mm = pe.matmul(bank[m % 2][:, :], a[:, u % 2, k, :],
                                           xlate[part][:, k, tq * TQ:(tq + 1) * TQ],
                                           start=(k == 0 and n == 0), stop=(k == KT - 1 and n == 2))
                    mm.then_inc(piece_done, 1)

                for st in range(NCS):
                    step(st, None, st % 2, 48 * (st // 2 + 1))
                pe.wait_ge(state_new, NCS + NCHAIN)

                def body(i):
                    for st in range(NS):
                        l = i * NS + st
                        scores(l, i, st)
                        piece(i, st)
                        step(l + NCS, l, st % 2, i * (48 * NS // 2) + 48 * (NCS // 2 + st // 2 + 1))

                with pe.Fori(0, NTRIP // 2) as i:
                    body(i)
                with pe.Fori(NTRIP // 2, NTRIP) as i:
                    body(i)

            @block.scalar
            def _(act):
                act.sem_inc(w_hi, 2)
                act.sem_inc(act_read, na[-1])
                act.sem_inc(w_exp, NCHAIN)

                def keys(s, L, cc, h, d, vk):
                    act.wait_ge(vk_loaded[L], vk)
                    act.wait_ge(step_done, s + 1)
                    act.activation(ek_h[:, L, :], kt_t[:, L, :], ACT.Copy,
                                   scale=ccol[:, cc, d, 3, h:h + 1]).then_inc(ek_hi, 1)

                def split_hi(i, u):
                    act.wait_ge(w_loaded[u % 2], i * (16 * NU // 2) + 16 * (u // 2 + 1))
                    act.wait_ge(piece_done, i * NPC + (NPC + 2 * u - 2))
                    act.activation(wh[:, u % 2], wraw[:, u % 2], ACT.Copy).then_inc(w_hi, 1)

                def evacuate(i, m):
                    u, kind, e, tq = PIECES[m]
                    act.wait_ge(piece_done, i * NPC + (NPC + m + 1))
                    if kind == "o":
                        act.wait_ge(u_made, i * nz[-1] + (nz[-1] + nz[m]))
                        act.activation(tanh_o[:, tq, :], bank[m % 2][:, :], ACT.Tanh, scale=0.5).then_inc(act_read, 1)
                    elif kind == "z":
                        act.wait_ge(u_made, i * nz[-1] + (nz[-1] + nz[m]))
                        act.activation(tanh_z[:, :], bank[m % 2][:, :], ACT.Tanh, scale=0.5).then_inc(dz, 1)
                    else:
                        a = ng[m]
                        act.wait_ge(g_stored[a % 2], i * (16 * ng[-1] // 2) + 16 * (a // 2))
                        act.activation(gstage[:, a % 2, :], bank[m % 2][:, :], ACT.Tanh, scale=0.5).then_inc(act_read, 1)

                for st, (cc, h, d) in enumerate(STEPS):
                    act.wait_ge(chunk_cols, 2 * cc + 2)
                    keys(st, st % 2, cc, h, d, 48 * (st // 2 + 1))
                    if st in (6, 7):
                        split_hi(0, st - 6)

                def body(i, ahead):
                    for st, (cc, h, d) in enumerate(STEPS):
                        L, l = st % 2, i * NS + st
                        s = l + NCS
                        act.wait_ge(chunk_cols, i * 4 + (2 * cc + 6))
                        keys(s, L, cc, h, d, i * (48 * NS // 2) + 48 * (NCS // 2 + st // 2 + 1))
                        act.wait_ge(nm_masked, i * 4 + (2 * cc + 2))
                        act.activation(wexp[:, L, :], nm[:, cc, d, h, :], ACT.Exp,
                                       bias=ccol[:, cc, d, 0, h:h + 1]).then_inc(w_exp, 1)
                        act.wait_ge(state_new, s + 1)
                        act.activation(state_h[:, L], state[:, chain(h, d)], ACT.Copy).then_inc(s_hi, 1)
                        evacuate(i, st)
                        act.wait_ge(step_done, s + 3)
                        act.activation(ysb[:, L, :], YBANK[:, 0:VW], ACT.Copy).then_inc(y_read, 1)
                        if st % 2 == 1 and (st // 2 + 2 < NU or ahead):
                            split_hi(i, st // 2 + 2)

                trips(act, body)

            @block.vector
            def _(dve):
                dve.sem_inc(w_lo, 2)
                dve.sem_inc(u_made, nz[-1])
                dve.sem_inc(state_new, NCHAIN)
                dve.memset(f32(v_t[:, :, :, HD:VW]), 0.0).then_inc(setup, 1)
                dve.wait_ge(setup, 1)
                dve.memset(f32(v_t[:, :, 0, HD:HD + 1]), 1.0).then_inc(setup, 1)
                dve.wait_ge(cols_loaded, 16)

                def keys(s, L, cc, h, d):
                    dve.wait_ge(ek_hi, s + 1)
                    dve.scalar_tensor_tensor(out=ek_l[:, L, :], in0=kt_t[:, L, :], scalar=ccol[:, cc, d, 3, h:h + 1],
                                             in1=f32(ek_h[:, L, :]), op0=ALU.mult, op1=ALU.subtract).then_inc(ek_lo, 1)

                def update(s, cc, h, d, ubank=UBANK):
                    ch, decay = chain(h, d), ccol[:, cc, d, 4, h:h + 1]
                    dve.wait_ge(step_done, s + 3)
                    dve.wait_ge(state_new, s + 1)
                    for b in range(HB):
                        last = dve.scalar_tensor_tensor(out=state[:, ch, b, :], in0=state[:, ch, b, :], scalar=decay,
                                                        in1=ubank[b][:, 0:VW], op0=ALU.mult, op1=ALU.add)
                    last.then_inc(state_new, 1)

                def split_lo(i, u):
                    dve.wait_ge(w_hi, i * NU + (u + 1 + 2))
                    dve.tensor_tensor(wl[:, u % 2], wraw[:, u % 2], f32(wh[:, u % 2]), ALU.subtract).then_inc(w_lo, 1)

                for st, (cc, h, d) in enumerate(STEPS):
                    if st % NCHAIN == 0:
                        for dd in range(2):
                            dve.tensor_copy(ccol[:, cc, dd], cols[:, dd, ctx_chunk(cc, dd), :]
                                            .rearrange("p (q h) -> p q h", h=HEADS)).then_inc(chunk_cols, 1)
                        dve.wait_ge(chunk_cols, 2 * cc + 2)
                    keys(st, st % 2, cc, h, d)
                    if st == 0:
                        dve.wait_ge(state_zero, 1)
                    update(st, cc, h, d, CTX_UBANK[st % 2])
                    if st in (6, 7):
                        split_lo(0, st - 6)

                def evacuate(i, m):
                    u, kind, e, tq = PIECES[m]
                    if kind != "z":
                        return
                    a = nz[m]
                    dve.wait_ge(dz, i * nz[-1] + (a + 1))
                    dve.scalar_tensor_tensor(out=zgate[:, :], in0=tanh_z[:, :], scalar=1.0, in1=bank[m % 2][:, :],
                                             op0=ALU.add, op1=ALU.mult).then_inc(zg, 1)
                    dve.wait_ge(u_stored[a % 2], i * (16 * nz[-1] // 2) + 16 * (a // 2))
                    dve.wait_ge(zg, i * nz[-1] + (a + 1))
                    dve.scalar_tensor_tensor(out=ustage[:, a % 2, :], in0=tanh_o[:, tq, :], scalar=1.0,
                                             in1=zgate[:, :], op0=ALU.add, op1=ALU.mult).then_inc(u_made, 1)

                def prepare(i, cc):
                    n, slot = cc + 1, (cc + 1) % 2
                    dve.wait_ge(step_done, i * NS + (NCS + NCHAIN * cc + 2))
                    for dd in range(2):
                        dve.tensor_copy(ccol[:, slot, dd], cols[:, dd, bass.ds(chunk(i, n, dd), 1), :]
                                        .rearrange("p c (q h) -> p (c q) h", h=HEADS)).then_inc(chunk_cols, 1)
                    dve.wait_ge(nm_loaded[slot], i * 32 + 32 * (n // 2 + 1))
                    for dd in range(2):
                        dve.tensor_tensor(nm[:, slot, dd], nm[:, slot, dd],
                                          cmask[:, dd].unsqueeze(1).broadcast_to([P, HEADS, P]),
                                          ALU.add).then_inc(nm_masked, 1)

                def body(i, ahead):
                    for st, (cc, h, d) in enumerate(STEPS):
                        L, l = st % 2, i * NS + st
                        s = l + NCS
                        if st % NCHAIN == 0:
                            dve.wait_ge(chunk_cols, i * 4 + (2 * cc + 6))
                        keys(s, L, cc, h, d)
                        dve.wait_ge(s_done, l + 1)
                        dve.wait_ge(w_exp, l + (1 + NCHAIN))
                        dve.tensor_tensor(pf[:, L, :], SBANK[:, 0:P], wexp[:, L, :], ALU.mult).then_inc(prep, 1)
                        dve.wait_ge(s_hi, l + 1)
                        dve.tensor_tensor(state_l[:, L], state[:, chain(h, d)], f32(state_h[:, L]), ALU.subtract)
                        dve.wait_ge(prep, l * 3 + 1)
                        dve.tensor_copy(p_h[:, L, :], pf[:, L, :]).then_inc(prep, 1)
                        dve.wait_ge(prep, l * 3 + 2)
                        dve.tensor_tensor(p_l[:, L, :], pf[:, L, :], f32(p_h[:, L, :]), ALU.subtract).then_inc(prep, 1)
                        evacuate(i, st)
                        update(s, cc, h, d)
                        dve.wait_ge(y_read, l + 1)
                        dve.scalar_tensor_tensor(out=num[:, L, :], in0=XBANK[:, 0:VW], scalar=ccol[:, cc, d, 1, h:h + 1],
                                                 in1=ysb[:, L, :], op0=ALU.mult, op1=ALU.add).then_inc(fin, 1)
                        dve.wait_ge(fin, l * 5 + 1)
                        dve.tensor_scalar(den[:, L, 0:1], num[:, L, HD:HD + 1], -1.0, ccol[:, cc, d, 2, h:h + 1],
                                          ALU.mult, ALU.max).then_inc(fin, 1)
                        dve.wait_ge(fin, l * 5 + 2)
                        dve.tensor_tensor(den[:, L, 1:2], den[:, L, 0:1], num[:, L, HD:HD + 1], ALU.max).then_inc(fin, 1)
                        dve.wait_ge(fin, l * 5 + 3)
                        dve.reciprocal(den[:, L, 2:3], den[:, L, 1:2]).then_inc(fin, 1)
                        dve.wait_ge(h_stored[L], i * (16 * NS // 2) + 16 * (st // 2))
                        dve.wait_ge(fin, l * 5 + 4)
                        if half_of(i):
                            dve.tensor_scalar(hout[:, L, :], num[:, L, 0:HD], den[:, L, 2:3], None,
                                              ALU.mult).then_inc(fin, 1)
                        else:
                            dve.wait_ge(h_back[L], row(i) * (16 * NS // 2) + 16 * (st // 2 + 1))
                            dve.scalar_tensor_tensor(out=hout[:, L, :], in0=num[:, L, 0:HD], scalar=den[:, L, 2:3],
                                                     in1=hother[:, L, :], op0=ALU.mult, op1=ALU.add).then_inc(fin, 1)
                        if st % 2 == 1 and (st // 2 + 2 < NU or ahead):
                            split_lo(i, st // 2 + 2)
                        if st % NCHAIN == NCHAIN - 2 and (cc == 0 or ahead):
                            prepare(i, cc)

                dve.wait_ge(mask_made, 3)
                prepare(0, -1)
                trips(dve, body)

            @block.gpsimd
            def _(pool):
                made = [0]

                def link(ins):
                    made[0] += 1
                    ins.then_inc(box, 1)
                    pool.wait_ge(box, made[0])

                pool.memset(state[:, :, :, :], 0.0).then_inc(state_zero, 1)
                pool.memset(cmask[:, :, :], 0.0).then_inc(mask_made, 1)
                pool.wait_ge(mask_made, 1)
                for d in range(2):
                    sign = -1 if d == 0 else 1
                    nc.gpsimd.affine_select(out=cmask[:, d], in_=cmask[:, d], compare_op=ALU.is_ge, fill=M_INIT,
                                            base=0, pattern=[[-sign, P]], channel_multiplier=sign).then_inc(mask_made, 1)

                def inverse_counts(axis, length, w):
                    cnt = [min(n + w - w // 2, length) - max(n - w // 2, 0) for n in range(length)]
                    link(pool.memset(icnt[:, axis, 0:length], 1.0 / w))
                    for n in range(length):
                        if cnt[n] != w:
                            last = pool.memset(icnt[:, axis, n:n + 1], 1.0 / cnt[n])
                    link(last)

                def window_sums(views, length, w):
                    src, dst = views
                    step = 1
                    while step < w:
                        m = length - 2 * step + 1
                        link(pool.tensor_tensor(dst(0, m), src(0, m), src(step, m), ALU.add))
                        src, dst, step = dst, src, 2 * step
                    return src, dst

                PAD = 8
                RL, CL = GRID_H + 2 * PAD, GRID_W + 2 * PAD
                for g in range(PG):
                    w = 2 << g
                    start = PAD - w // 2
                    inverse_counts(0, GRID_H, w)
                    inverse_counts(1, GRID_W, w)
                    pool.memset(pool_a[:, 0:PAD * GRID_W], 0.0)
                    link(pool.memset(pool_a[:, (PAD + GRID_H) * GRID_W:RL * GRID_W], 0.0))
                    pool.dma_start(pool_a[:, PAD * GRID_W:(PAD + GRID_H) * GRID_W], p_d[g]).then_inc(p_loaded, 16)
                    pool.wait_ge(p_loaded, 32 * g + 16)
                    rows = [(lambda buf: lambda n, m: buf[:, n * GRID_W:(n + m) * GRID_W])(b) for b in (pool_a, pool_b)]
                    src, dst = window_sums(rows, RL, w)
                    other = pool_b if src is rows[0] else pool_a
                    this = pool_a if src is rows[0] else pool_b
                    wide = other[:, 0:GRID_H * CL].rearrange("p (r c) -> p r c", c=CL)
                    pool.memset(wide[:, :, 0:PAD], 0.0)
                    pool.memset(wide[:, :, PAD + GRID_W:CL], 0.0)
                    link(pool.tensor_tensor(wide[:, :, PAD:PAD + GRID_W],
                                            src(start, GRID_H).rearrange("p (r c) -> p r c", c=GRID_W),
                                            icnt[:, 0, 0:GRID_H].unsqueeze(2).broadcast_to([P, GRID_H, GRID_W]), ALU.mult))
                    cols_ = [(lambda buf: lambda n, m: buf[:, 0:GRID_H * CL]
                              .rearrange("p (r c) -> p r c", c=CL)[:, :, n:n + m])(b) for b in (other, this)]
                    src, dst = window_sums(cols_, CL, w)
                    end = other if src is cols_[0] else this
                    spare = this if src is cols_[0] else other
                    pool.dma_start(spare[:, 0:SEQ], p_d[g]).then_inc(p_loaded, 16)
                    res = src(start, GRID_W)
                    link(pool.tensor_tensor(res, res, icnt[:, 1, 0:GRID_W].unsqueeze(1)
                                            .broadcast_to([P, GRID_H, GRID_W]), ALU.mult))
                    pool.wait_ge(p_loaded, 32 * g + 32)
                    flat = spare[:, 0:SEQ].rearrange("p (r c) -> p r c", c=GRID_W)
                    link(pool.tensor_tensor(flat, res, flat, ALU.subtract))
                    pool.dma_start(mix_d[g], spare[:, 0:SEQ]).then_inc(mix_stored, 16)
                    pool.wait_ge(mix_stored, 16 * g + 16)

        late.close()
        with ExitStack() as ph:
            def sb(name, shape, dt=FP32):
                return ph.enter_context(nc.sbuf_tensor(name, shape, dt))

            QT = TQ // P
            WS = 3
            wraw = sb("wraw5", [P, 2, KT, P])
            wh = sb("wh5", [P, WS, KT, P], FP32R)
            wl = sb("wl5", [P, WS, KT, P], FP32R)
            pw = sb("pw", [P, PG, P])
            pw_h = sb("pw_h", [P, PG, P], FP32R)
            pw_l = sb("pw_l", [P, PG, P], FP32R)
            hw_row = sb("hw_row", [P, D])
            fn_row = sb("fn_row", [P, D])
            hsum = sb("hsum", [P, QT, D])
            ut = sb("ut", [P, 2, KT, P])
            yt = sb("yt", [P, KT, P])
            y_h = sb("y_h", [P, KT, TQ], FP32R)
            y_l = sb("y_l", [P, KT, TQ], FP32R)
            mixt = sb("mixt", [P, 2, TQ])
            mix_h = sb("mix_h", [P, 2, TQ], FP32R)
            mix_l = sb("mix_l", [P, 2, TQ], FP32R)
            zpt = sb("zpt", [P, 2, TQ])
            ypt = sb("ypt", [P, TQ])
            yp_h = sb("yp_h", [P, PG, TQ], FP32R)
            yp_l = sb("yp_l", [P, PG, TQ], FP32R)
            gmt = sb("gmt", [P, 2, TQ])
            gpt = sb("gpt", [P, 2, TQ])
            mm_ = sb("merged_m", [P, TQ])
            mp_ = sb("merged_p", [P, TQ])
            m_h = sb("m_h", [P, KT, TQ], FP32R)
            m_l = sb("m_l", [P, KT, TQ], FP32R)
            of = sb("of", [P, 2, TQ])
            xo = sb("xo", [P, QT, D])
            junk_h = sb("junk_h", [P, HD], mybir.dt.bfloat16)
            junk_o = sb("junk_o", [P, D], mybir.dt.bfloat16)
            hss = sb("hss", [P, 4, 2, HEADS])
            oss = sb("oss", [P, 4, QT])

            w_loaded = [sem(f"w5_loaded{n}") for n in range(2)]
            w_hi = sem("w5_hi"); w_lo = sem("w5_lo"); unit_done = sem("unit_done")
            rows_loaded = sem("rows_loaded"); rows_ready = sem("rows_ready")
            pw_hi = sem("pw_hi"); pw_lo = sem("pw_lo")
            h_loaded = [sem(f"h_loaded{n}") for n in range(QT)]
            u_loaded = [sem(f"u_loaded{n}") for n in range(2)]
            h_dve = sem("h_dve"); h_act = sem("h_act"); h_turned = sem("h_turned"); y_made = sem("y_made5")
            y_hi = sem("y_hi"); y_lo = sem("y_lo")
            mix_loaded = [sem(f"mix_loaded{n}") for n in range(2)]
            mix_hi = sem("mix_hi"); mix_lo = sem("mix_lo"); mix_done = sem("mix_done")
            yp_made = sem("yp_made"); yp_hi = sem("yp_hi"); yp_lo = sem("yp_lo")
            g_loaded = [sem(f"g5_loaded{n}") for n in range(2)]
            gated = sem("gated"); m_made = sem("m_made"); m_hi = sem("m_hi"); m_lo = sem("m_lo")
            of_made = sem("of_made"); o_turned = sem("o_turned"); x_loaded = sem("x5_loaded")
            x_added = sem("x_added"); o_act = sem("o_act"); o_dve = sem("o_dve"); o_ready = sem("o_ready")
            o_stored = sem("o_stored")

            UNITS = [(m, n, kt) for n in range(KT) for m, kt in (("m", KT), ("p", PG))] + [("o", n, KT) for n in range(KT)]
            NU = len(UNITS)
            SRC = {"m": branch_m_w[0].rearrange("(j p) n -> p j n", p=P),
                   "p": branch_p_w[0].rearrange("(j p) n -> p j n", p=P),
                   "o": out_w[0].rearrange("(j p) n -> p j n", p=P)}
            HSTEP = 2 + HEADS
            NORM = {1: 0, 2: 1, 4: 2, 5: 3}
            GATE = {2: 0, 3: 1, 5: 2, 6: 3}
            SPLIT = {2: 0, 3: 1, 5: 2, 6: 3}
            GROUP = {3: 0, 4: 1, 6: 2, 7: 3}
            block = ph.enter_context(nc.Block())

            def quarters(eng, out_proj, merge, last):
                with eng.Fori(0, NTQ - 1) as i:
                    out_proj(i, True)
                    merge(i + 1, True)
                out_proj(NTQ - 1, False)
                last(NTQ - 1)

            @block.sync
            def _(sp):
                sp.sem_inc(o_stored, 1)

                def tile(i, u):
                    m, n, kt = UNITS[u % NU]
                    sp.wait_ge(w_hi, i * NU + (u + 1))
                    sp.wait_ge(w_lo, i * NU + (u + 1))
                    sp.dma_start(wraw[:, u % 2, 0:kt], SRC[m][:, :, n * P:(n + 1) * P]).then_inc(w_loaded[u % 2], 16)

                def hidden(i, q):
                    if not isinstance(i, int):
                        sp.wait_ge(h_turned, i * QT + (q + 1 - QT))
                    sp.dma_start(hsum[:, q], hsum_d[i * QT + q]).then_inc(h_loaded[q], 16)

                def hidden_gate(i, q):
                    sp.wait_ge(y_made, i * QT + (q + 1))
                    sp.dma_start(ut[:, q % 2], u_d[:, :, bass.ds(i * TQ + q * P, P)].rearrange("j p t -> p j t"))\
                        .then_inc(u_loaded[q % 2], 16)

                def pooled(i, g):
                    sp.wait_ge(yp_made, i * PG + (g + 1))
                    sp.dma_start(mixt[:, g % 2], mix_d[g, :, bass.ds(i * TQ, TQ)]).then_inc(mix_loaded[g % 2], 16)
                    sp.dma_start(zpt[:, g % 2], zp_d[g, :, bass.ds(i * TQ, TQ)]).then_inc(mix_loaded[g % 2], 16)

                def gates(i, n):
                    sp.wait_ge(gated, i * (2 * KT) + (2 * n + 1))
                    sp.dma_start(gmt[:, n % 2], gm_d[n, :, bass.ds(i * TQ, TQ)]).then_inc(g_loaded[n % 2], 16)
                    sp.dma_start(gpt[:, n % 2], gp_d[n, :, bass.ds(i * TQ, TQ)]).then_inc(g_loaded[n % 2], 16)

                def store(i, q):
                    sp.wait_ge(o_ready, i * QT + (q + 1))
                    sp.dma_start(out[bass.ds(i * TQ + q * P, P), :], xo[:, q, :]).then_inc(o_stored, 16)

                def residual_x(i, q):
                    sp.dma_start(xo[:, q, :], x[bass.ds(i * TQ + q * P, P), :]).then_inc(x_loaded, 16)

                def merge(i, after):
                    for n in range(KT):
                        tile(i, 2 * n + 3)
                        tile(i, 2 * n + 4)
                        if n + 2 < KT:
                            gates(i, n + 2)
                        if n > KT - QT:
                            q = n - (KT - QT + 1)
                            if after:
                                sp.wait_ge(o_stored, (i - 1) * (16 * QT) + (16 * (q + 1) + 1))
                            residual_x(i, q)
                        if after and n >= KT - QT:
                            store(i - 1, n - (KT - QT))

                def out_proj(i, ahead):
                    for n in range(KT):
                        if n + 3 < KT or ahead:
                            tile(i, 2 * KT + n + 3)
                        if n == 0:
                            sp.wait_ge(o_stored, i * (16 * QT) + 1)
                            residual_x(i, QT - 1)
                        if ahead:
                            for q, at in enumerate((0, 1, 3, 4)):
                                if n == at:
                                    hidden(i + 1, q)
                                    hidden_gate(i + 1, q)
                            for g, at in enumerate((1, 2, 4, 5)):
                                if n == at:
                                    pooled(i + 1, g)
                            if n >= KT - 2:
                                gates(i + 1, n - (KT - 2))

                def last(i):
                    for q in range(QT):
                        store(i, q)

                hidden(0, 0)
                sp.dma_start(pw[:, :, :], pool_w[0].rearrange("g c n -> c g n")).then_inc(rows_loaded, 16)
                sp.dma_start(hw_row[:, :], head_norm_w[0].partition_broadcast(P)).then_inc(rows_loaded, 16)
                pooled(0, 0)
                hidden(0, 1)
                hidden_gate(0, 0)
                pooled(0, 1)
                hidden(0, 2)
                hidden_gate(0, 1)
                tile(0, 0)
                hidden(0, 3)
                for q in range(2, QT):
                    pooled(0, q)
                    hidden_gate(0, q)
                    if q == 2:
                        tile(0, 1)
                for n in range(2):
                    gates(0, n)
                tile(0, 2)
                sp.dma_start(fn_row[:, :], final_norm_w.partition_broadcast(P)).then_inc(rows_loaded, 16)
                merge(0, False)
                quarters(sp, out_proj, merge, last)
                sp.wait_ge(o_stored, 16 * QT * NTQ + 1)

            @block.tensor
            def _(pe):
                pe.sem_inc(unit_done, WS)
                pe.sem_inc(o_turned, 2)
                pe.sem_inc(mix_done, 2)

                def turn_hidden(i, q):
                    t = i * QT + q
                    pe.wait_ge(h_dve, t * HSTEP + HSTEP)
                    pe.wait_ge(y_made, t + 2)
                    for j in range(KT):
                        mm = pe.transpose(bank[4 + j // 4][:, (j % 4) * P:(j % 4 + 1) * P],
                                          hsum[:, q, j * P:(j + 1) * P], ident[:, :])
                    mm.then_inc(h_turned, 1)

                def group(i, g):
                    pe.wait_ge(mix_hi, i * PG + (g + 1))
                    pe.wait_ge(mix_lo, i * PG + (g + 1))
                    pe.wait_ge(yp_made, i * PG + (g + 1))
                    pe.wait_ge(gated, i * (2 * KT) + 3)
                    for n, (a, b) in enumerate(((pw_h, mix_h), (pw_h, mix_l), (pw_l, mix_h))):
                        mm = pe.matmul(bank[2 + g % 2][:, :], a[:, g, :], b[:, g % 2, :], start=(n == 0), stop=(n == 2))
                    mm.then_inc(mix_done, 1)

                def unit(i, u):
                    m, n, kt = UNITS[u]
                    pe.wait_ge(w_hi, i * NU + (u + 3))
                    pe.wait_ge(w_lo, i * NU + (u + 3))
                    if m == "m":
                        dst, (bh, bl) = bank[n % 2], (y_h, y_l)
                        if n == 0:
                            pe.wait_ge(y_hi, i * QT + QT)
                            pe.wait_ge(y_lo, i * QT + QT)
                        if n >= 2:
                            pe.wait_ge(gated, i * (2 * KT) + (2 * n - 3 + 3))
                        else:
                            pe.wait_ge(of_made, i * KT + (n - 1 + 2))
                    elif m == "p":
                        dst, (bh, bl) = bank[2 + n % 2], (yp_h, yp_l)
                        if n == 0:
                            pe.wait_ge(yp_hi, i * PG + PG)
                            pe.wait_ge(yp_lo, i * PG + PG)
                        if n >= 2:
                            pe.wait_ge(gated, i * (2 * KT) + (2 * n - 2 + 3))
                    else:
                        dst, (bh, bl) = bank[n % 2], (m_h, m_l)
                        if n == 0:
                            pe.wait_ge(m_hi, i * KT + KT - 1)
                            pe.wait_ge(m_lo, i * KT + KT - 1)
                        if n >= 2:
                            pe.wait_ge(of_made, i * KT + (n - 1 + 2))
                        else:
                            pe.wait_ge(gated, i * (2 * KT) + (2 * (KT - 2 + n) + 1 + 3))
                    for k in range(kt):
                        if m == "o" and n == 0 and k == kt - 1:
                            pe.wait_ge(m_hi, i * KT + KT)
                            pe.wait_ge(m_lo, i * KT + KT)
                        for r, (a, b) in enumerate(((wh, bh), (wh, bl), (wl, bh))):
                            mm = pe.matmul(dst[:, :], a[:, u % WS, k, :], b[:, k, :],
                                           start=(k == 0 and r == 0), stop=(k == kt - 1 and r == 2))
                    mm.then_inc(unit_done, 1)

                def turn_output(i, n):
                    pe.wait_ge(of_made, i * KT + (n + 1 + 2))
                    pe.wait_ge(x_added, i * KT + (n + 1))
                    for q in range(QT):
                        mm = pe.transpose(bank[6 + n % 2][:, q * P:(q + 1) * P], of[:, n % 2, q * P:(q + 1) * P], ident[:, :])
                    mm.then_inc(o_turned, 1)

                def merge(i, after):
                    for u in range(2 * KT):
                        unit(i, u)
                        if after and u == 0:
                            turn_output(i - 1, KT - 1)

                def out_proj(i, ahead):
                    for n in range(KT):
                        if ahead and n in GATE:
                            turn_hidden(i + 1, GATE[n])
                        if ahead and n in GROUP:
                            group(i + 1, GROUP[n])
                        unit(i, 2 * KT + n)
                        if n >= 1:
                            turn_output(i, n - 1)

                pe.wait_ge(pw_lo, 1)
                for q in range(QT):
                    group(0, q)
                    turn_hidden(0, q)
                merge(0, False)
                quarters(pe, out_proj, merge, lambda i: turn_output(i, KT - 1))

            @block.scalar
            def _(act):
                act.sem_inc(w_hi, 2)
                act.sem_inc(of_made, 2)
                act.sem_inc(o_act, 1)

                def split_hi(i, u):
                    m, n, kt = UNITS[u % NU]
                    act.wait_ge(w_loaded[u % 2], i * (16 * NU // 2) + 16 * (u // 2 + 1))
                    act.wait_ge(unit_done, i * NU + (u - WS + 1 + WS))
                    act.activation(wh[:, u % WS, 0:kt], wraw[:, u % 2, 0:kt], ACT.Copy).then_inc(w_hi, 1)

                def squares(i, q):
                    t = i * QT + q
                    act.wait_ge(h_loaded[q], i * 16 + 16)
                    for h in range(HEADS):
                        if not (isinstance(t, int) and t == 0 and h == 0):
                            act.wait_ge(h_act, t * (HEADS + 1) + h)
                        act.activation(junk_h[:, :], hsum[:, q, h * HD:(h + 1) * HD], ACT.Square,
                                       accum_out=hss[:, 0, q % 2, h:h + 1]).then_inc(h_act, 1)
                    act.wait_ge(h_dve, t * HSTEP + 1)
                    act.activation(hss[:, 2, q % 2], hss[:, 1, q % 2], ACT.Sqrt).then_inc(h_act, 1)

                def branches_done(i):
                    if not isinstance(i, int):
                        act.wait_ge(unit_done, i * NU - (NU - 2 * KT - WS))

                def hidden_hi(i, q):
                    t = i * QT + q
                    act.wait_ge(y_made, t + 3)
                    branches_done(i)
                    act.activation(y_h[:, :, q * P:(q + 1) * P], yt[:, :, :], ACT.Copy).then_inc(y_hi, 1)

                def pooled_hi(i, g):
                    act.wait_ge(mix_loaded[g % 2], i * (32 * PG // 2) + 32 * (g // 2 + 1))
                    act.wait_ge(mix_done, i * PG + (g + 1))
                    act.activation(mix_h[:, g % 2], mixt[:, g % 2], ACT.Copy).then_inc(mix_hi, 1)

                def branch_hi(i, g):
                    act.wait_ge(yp_made, i * PG + (g + 1 + 2))
                    branches_done(i)
                    act.activation(yp_h[:, g], ypt[:, :], ACT.Copy).then_inc(yp_hi, 1)

                def output(i, n):
                    act.wait_ge(unit_done, i * NU + (2 * KT + n + 1 + WS))
                    act.wait_ge(o_turned, i * KT + (n + 1))
                    act.activation(of[:, n % 2], bank[n % 2][:, :], ACT.Copy,
                                   scale=mgate[:, n:n + 1]).then_inc(of_made, 1)

                def out_square(i, q):
                    act.wait_ge(x_added, i * KT + (KT + 2))
                    act.wait_ge(o_act, i * (QT + 1) + (q + 1))
                    act.activation(junk_o[:, :], xo[:, q], ACT.Square, accum_out=oss[:, 0, q:q + 1]).then_inc(o_act, 1)

                def out_root(i):
                    act.wait_ge(o_dve, i * 2 + 1)
                    act.activation(oss[:, 2], oss[:, 1], ACT.Sqrt).then_inc(o_act, 1)

                def merge(i, after):
                    for n in range(KT):
                        if after and n == 0:
                            output(i - 1, KT - 1)
                        split_hi(i, 2 * n + 2)
                        split_hi(i, 2 * n + 3)
                        if after and n in (1, 2):
                            out_square(i - 1, 2 * n - 2)
                            out_square(i - 1, 2 * n - 1)
                        if after and n == 3:
                            out_root(i - 1)
                        act.wait_ge(m_made, i * KT + (n + 1))
                        act.activation(m_h[:, n], mm_[:, :], ACT.Copy).then_inc(m_hi, 1)

                def out_proj(i, ahead):
                    for n in range(KT):
                        if n + 2 < KT or ahead:
                            split_hi(i, 2 * KT + n + 2)
                        if n >= 1:
                            output(i, n - 1)
                        if ahead:
                            if n in GATE:
                                hidden_hi(i + 1, GATE[n])
                            if n in SPLIT:
                                pooled_hi(i + 1, SPLIT[n])
                            if n in GROUP:
                                branch_hi(i + 1, GROUP[n])
                            if n in NORM:
                                squares(i + 1, NORM[n])

                def last(i):
                    output(i, KT - 1)
                    for q in range(QT):
                        out_square(i, q)
                    out_root(i)

                act.wait_ge(rows_loaded, 32)
                act.activation(pw_h[:, :, :], pw[:, :, :], ACT.Copy).then_inc(pw_hi, 1)
                for q in range(QT + 1):
                    if q < QT:
                        squares(0, q)
                        pooled_hi(0, q)
                    if q > 0:
                        branch_hi(0, q - 1)
                        hidden_hi(0, q - 1)
                    if q in (1, 2):
                        split_hi(0, q - 1)
                merge(0, False)
                quarters(act, out_proj, merge, last)

            @block.vector
            def _(dve):
                dve.sem_inc(w_lo, 2)
                dve.sem_inc(y_made, 2)
                dve.sem_inc(yp_made, 2)
                dve.sem_inc(gated, 3)
                dve.sem_inc(x_added, 2)

                def split_lo(i, u):
                    m, n, kt = UNITS[u % NU]
                    dve.wait_ge(w_hi, i * NU + (u + 3))
                    dve.tensor_tensor(wl[:, u % WS, 0:kt], wraw[:, u % 2, 0:kt], f32(wh[:, u % WS, 0:kt]),
                                      ALU.subtract).then_inc(w_lo, 1)

                def norms(i, q):
                    t, L = i * QT + q, q % 2
                    dve.wait_ge(h_act, t * (HEADS + 1) + HEADS)
                    dve.tensor_scalar(hss[:, 1, L], hss[:, 0, L], 1.0 / HD, EPS, ALU.mult, ALU.add).then_inc(h_dve, 1)
                    dve.wait_ge(h_act, t * (HEADS + 1) + HEADS + 1)
                    dve.reciprocal(hss[:, 3, L], hss[:, 2, L]).then_inc(h_dve, 1)
                    dve.wait_ge(h_dve, t * HSTEP + 2)
                    for h in range(HEADS):
                        s = slice(h * HD, (h + 1) * HD)
                        dve.scalar_tensor_tensor(out=hsum[:, q, s], in0=hsum[:, q, s], scalar=hss[:, 3, L, h:h + 1],
                                                 in1=hw_row[:, s], op0=ALU.mult, op1=ALU.mult).then_inc(h_dve, 1)

                def gate_hidden(i, q):
                    t = i * QT + q
                    dve.wait_ge(h_turned, t + 1)
                    dve.wait_ge(u_loaded[q % 2], i * (16 * QT // 2) + 16 * (q // 2 + 1))
                    if not (isinstance(t, int) and t == 0):
                        dve.wait_ge(y_hi, t)
                        dve.wait_ge(y_lo, t)
                    for b in range(2):
                        half = dve.tensor_tensor(yt[:, 4 * b:4 * b + 4], bank[4 + b][:, :].rearrange("p (j t) -> p j t", t=P),
                                                 ut[:, q % 2, 4 * b:4 * b + 4], ALU.mult)
                    half.then_inc(y_made, 1)

                def branch(i, g):
                    dve.wait_ge(mix_done, i * PG + (g + 1 + 2))
                    if not (isinstance(i, int) and i == 0 and g == 0):
                        dve.wait_ge(yp_hi, i * PG + g)
                        dve.wait_ge(yp_lo, i * PG + g)
                    dve.scalar_tensor_tensor(out=ypt[:, :], in0=bank[2 + g % 2][:, :],
                                             scalar=vcol[:, VR["pool"] + g:VR["pool"] + g + 1], in1=zpt[:, g % 2],
                                             op0=ALU.mult, op1=ALU.mult).then_inc(yp_made, 1)

                def residual(i, n):
                    dve.wait_ge(o_turned, i * KT + (n + 1 + 2))
                    if n == 0:
                        dve.wait_ge(x_loaded, i * (16 * QT) + 16 * QT)
                    s = slice(n * P, (n + 1) * P)
                    dve.tensor_tensor(xo[:, :, s], bank[6 + n % 2][:, :].rearrange("p (q f) -> p q f", f=P),
                                      xo[:, :, s], ALU.add).then_inc(x_added, 1)

                def out_stats(i):
                    dve.wait_ge(o_act, i * (QT + 1) + (QT + 1))
                    dve.tensor_scalar(oss[:, 1], oss[:, 0], 1.0 / D, EPS, ALU.mult, ALU.add).then_inc(o_dve, 1)
                    dve.wait_ge(o_act, i * (QT + 1) + (QT + 1 + 1))
                    dve.reciprocal(oss[:, 3], oss[:, 2]).then_inc(o_dve, 1)
                    dve.wait_ge(o_dve, i * 2 + 2)

                def out_norm(i, q):
                    dve.scalar_tensor_tensor(out=xo[:, q], in0=xo[:, q], scalar=oss[:, 3, q:q + 1], in1=fn_row[:, :],
                                             op0=ALU.mult, op1=ALU.mult).then_inc(o_ready, 1)

                def merge(i, after):
                    first = isinstance(i, int)
                    for n in range(KT):
                        split_lo(i, 2 * n + 2)
                        if after and n == 0:
                            residual(i - 1, KT - 2)
                        dve.wait_ge(g_loaded[n % 2], i * (32 * KT // 2) + 32 * (n // 2 + 1))
                        dve.wait_ge(unit_done, i * NU + (2 * n + 1 + WS))
                        if not (first and n == 0):
                            dve.wait_ge(m_hi, i * KT + n)
                            dve.wait_ge(m_lo, i * KT + n)
                        dve.scalar_tensor_tensor(out=mm_[:, :], in0=gmt[:, n % 2], scalar=1.0, in1=bank[n % 2][:, :],
                                                 op0=ALU.add, op1=ALU.mult).then_inc(gated, 1)
                        if after and n == 0:
                            residual(i - 1, KT - 1)
                        split_lo(i, 2 * n + 3)
                        if after and n == 3:
                            out_stats(i - 1)
                        if after and 3 <= n < 3 + QT:
                            out_norm(i - 1, n - 3)
                        dve.wait_ge(unit_done, i * NU + (2 * n + 2 + WS))
                        dve.scalar_tensor_tensor(out=mp_[:, :], in0=gpt[:, n % 2], scalar=1.0, in1=bank[2 + n % 2][:, :],
                                                 op0=ALU.add, op1=ALU.mult).then_inc(gated, 1)
                        dve.wait_ge(gated, i * (2 * KT) + (2 * n + 2 + 3))
                        dve.tensor_tensor(mm_[:, :], mm_[:, :], mp_[:, :], ALU.add).then_inc(m_made, 1)
                        dve.wait_ge(m_hi, i * KT + (n + 1))
                        dve.wait_ge(m_made, i * KT + (n + 1))
                        dve.tensor_tensor(m_l[:, n], mm_[:, :], f32(m_h[:, n]), ALU.subtract).then_inc(m_lo, 1)

                def out_proj(i, ahead):
                    for n in range(KT):
                        if n + 2 < KT or ahead:
                            split_lo(i, 2 * KT + n + 2)
                        if n >= 2:
                            residual(i, n - 2)
                        if ahead:
                            if n in GATE:
                                gate_hidden(i + 1, GATE[n])
                            if n in GROUP:
                                branch(i + 1, GROUP[n])
                            if n in NORM:
                                norms(i + 1, NORM[n])

                def last(i):
                    residual(i, KT - 2)
                    residual(i, KT - 1)
                    out_stats(i)
                    for q in range(QT):
                        out_norm(i, q)

                dve.wait_ge(rows_loaded, 32)
                dve.tensor_scalar(hw_row[:, :], hw_row[:, :], 0.25, None, ALU.mult).then_inc(rows_ready, 1)
                dve.wait_ge(pw_hi, 1)
                dve.tensor_tensor(pw_l[:, :, :], pw[:, :, :], f32(pw_h[:, :, :]), ALU.subtract).then_inc(pw_lo, 1)
                dve.wait_ge(rows_ready, 1)
                for q in range(QT + 1):
                    if q < QT:
                        norms(0, q)
                    if q > 0:
                        branch(0, q - 1)
                        gate_hidden(0, q - 1)
                    if q in (1, 2):
                        split_lo(0, q - 1)
                dve.wait_ge(rows_loaded, 48)
                merge(0, False)
                quarters(dve, out_proj, merge, last)

            @block.gpsimd
            def _(pool):
                def hidden_lo(i, q):
                    t = i * QT + q
                    pool.wait_ge(y_hi, t + 1)
                    pool.tensor_tensor(y_l[:, :, q * P:(q + 1) * P], yt[:, :, :], f32(y_h[:, :, q * P:(q + 1) * P]),
                                       ALU.subtract).then_inc(y_lo, 1)

                def pooled_lo(i, g):
                    pool.wait_ge(mix_hi, i * PG + (g + 1))
                    pool.tensor_tensor(mix_l[:, g % 2], mixt[:, g % 2], f32(mix_h[:, g % 2]), ALU.subtract).then_inc(mix_lo, 1)

                def branch_lo(i, g):
                    pool.wait_ge(yp_hi, i * PG + (g + 1))
                    pool.tensor_tensor(yp_l[:, g], ypt[:, :], f32(yp_h[:, g]), ALU.subtract).then_inc(yp_lo, 1)

                for q in range(QT + 1):
                    if q < QT:
                        pooled_lo(0, q)
                    if q > 0:
                        branch_lo(0, q - 1)
                        hidden_lo(0, q - 1)
                with pool.Fori(0, NTQ - 1) as i:
                    for n in range(KT):
                        if n in GATE:
                            hidden_lo(i + 1, GATE[n])
                        if n in SPLIT:
                            pooled_lo(i + 1, SPLIT[n])
                        if n in GROUP:
                            branch_lo(i + 1, GROUP[n])


_INS = ['x', 'c', 'ctx', 'c_ctx', 'norm_w', 'ada_w', 'ada_b', 'in_w', 'gate_b', 'head_norm_w', 'pool_w',
        'pool_scale', 'branch_m_w', 'branch_p_w', 'out_w', 'final_norm_w']
_OUTS = [((1, SEQ, D), 'float32')]


def kernel(**inputs):
    import numpy as _np
    import concourse.bacc as _bacc
    from concourse import mybir as _mybir
    from concourse.bass_utils import run_bass_kernel_spmd as _run

    nc = _bacc.Bacc("TRN2", target_bir_lowering=False, num_devices=1)
    arrays, args = {}, []
    for name in _INS:
        a = _np.ascontiguousarray(inputs[name])
        arrays[f"in_{name}_dram"] = a
        args.append(nc.dram_tensor(f"in_{name}_dram", a.shape, _mybir.dt.from_np(a.dtype), kind="ExternalInput").ap())
    for i, (shape, dtype) in enumerate(_OUTS):
        dt = _mybir.dt.from_np(_np.dtype(dtype))
        args.append(nc.dram_tensor(f"out_{i}_dram", shape, dt, kind="ExternalOutput").ap())
    hybrid_block(nc, *args)
    r = _run(nc, [arrays], core_ids=[0])
    return r.results[0]["out_0_dram"]
```

```python
import numpy as np
from contextlib import ExitStack

import concourse.bass as bass
from concourse import mybir
from concourse.alu_op_type import AluOpType as ALU

FP32 = mybir.dt.float32
FP32R = mybir.dt.float32r
ACT = mybir.ActivationFunctionType

P = 128
D = 1024
KT = D // P
SEQ, CTX = 2048, 256
TOK = CTX + SEQ
NX, NC = SEQ // P, CTX // P
NCH = NX + NC
GRID_W = 64
GRID_H = SEQ // GRID_W
HEADS = 4
HD = D // HEADS
HB = HD // P
PW = D // 2
PG = 4
EPS = 1e-6
M_INIT = -1e30
Q0, K0, V0, O0, Z0 = (D * n for n in range(5))
GATE0 = 5 * D
NGATE = 16
POOL0 = GATE0 + NGATE
ZP0 = POOL0 + PW
GM0 = ZP0 + PW
GP0 = GM0 + D
TQ = 512
NTQ = SEQ // TQ
VW = HD + 2
NQ = 5


def f32(ap):
    return ap.bitcast(FP32)


def hybrid_block(nc, x, c, ctx, c_ctx, norm_w, ada_w, ada_b, in_w, gate_b, head_norm_w, pool_w,
                 pool_scale, branch_m_w, branch_p_w, out_w, final_norm_w, out):
    x, ctx, out = x[0], ctx[0], out[0]

    def scratch(name, shape):
        return nc.dram_tensor(name, shape, FP32, kind="Internal").ap()

    gates_d = scratch("gates_d", (NGATE, TOK))
    qk_d = scratch("qk_d", (HEADS, 2, HB, P, NCH, 2, P))
    kt_d = scratch("kt_d", (HEADS, NCH, P, HD))
    v_d = scratch("v_d", (HEADS, NCH, P, HB, 2, P))
    ends_d = scratch("ends_d", (2, 2, HEADS * NCH))
    mprev_d = scratch("mprev_d", (2, HEADS * NCH))
    negm_d = scratch("negm_d", (2, HEADS, NCH, P))
    cols_d = scratch("cols_d", (P, 2, NCH, NQ, HEADS))
    u_d = scratch("u_d", (KT, P, SEQ))
    gm_d = scratch("gm_d", (KT, P, SEQ))
    gp_d = scratch("gp_d", (KT, P, SEQ))
    xe_d = scratch("xe_d", (2, P, KT, SEQ // 2))
    p_d = scratch("p_d", (PG, P, SEQ))
    zp_d = scratch("zp_d", (PG, P, SEQ))
    mix_d = scratch("mix_d", (PG, P, SEQ))
    h_d = scratch("h_d", (NX, P, D))
    hsum_d = scratch("hsum_d", (NX, P, D))

    in_v = in_w[0].rearrange("(j p) n -> p j n", p=P)
    ada_v = ada_w[0].rearrange("(j p) n -> p j n", p=P)

    with ExitStack() as top:
        def sem(name):
            return top.enter_context(nc.semaphore(name))

        def keep(name, shape, dt=FP32):
            return top.enter_context(nc.sbuf_tensor(name, shape, dt))

        ident = keep("ident", [P, P])
        vcol = keep("vcol", [P, 64])
        mgate = keep("mgate", [P, KT])
        bank = [top.enter_context(nc.psum_tensor(f"bank{n}", [P, TQ], FP32)) for n in range(8)]
        HALF = SEQ // 2
        late = top.enter_context(ExitStack())
        early = top.enter_context(ExitStack())
        xlate = [late.enter_context(nc.sbuf_tensor(f"xlate{n}", [P, KT, HALF], FP32R)) for n in range(2)]
        xearly = [early.enter_context(nc.sbuf_tensor(f"xearly{n}", [P, KT, CTX + HALF], FP32R)) for n in range(2)]

        wgh = early.enter_context(nc.sbuf_tensor("wgh", [P, KT, NGATE], FP32R))
        wgl = early.enter_context(nc.sbuf_tensor("wgl", [P, KT, NGATE], FP32R))
        gbias = early.enter_context(nc.sbuf_tensor("gbias", [NGATE, 1], FP32))
        g_loaded = sem("g_loaded"); g_hi = sem("g_hi"); g_lo = sem("g_lo")

        def xn(part, k, t0, w):
            if t0 >= CTX + HALF:
                return xlate[part][:, k, t0 - CTX - HALF:t0 - CTX - HALF + w]
            return xearly[part][:, k, t0:t0 + w]


        VR = {"norm": 0, "ada": 8, "head": 32, "pool": 40, "c": 44, "cc": 52}
        NV = 60
        AS = 128
        NAS, TS = 3 * D // AS, AS // P
        NEARLY = 2 * NAS // 3

        def later(g):
            n = NEARLY + 2 * (g - 1)
            return range(n, n + 2) if g >= 1 else ()

        groups = [(CTX // P, 0, 1, ctx)] + [(TQ // P, CTX + TQ * n, 0, x) for n in range(NTQ)]
        tiles = [(g, r) for g, (w, *_) in enumerate(groups) for r in range(w)]
        first = [sum(w for w, *_ in groups[:g]) for g in range(len(groups) + 1)]
        with ExitStack() as ph:
            def sb(name, shape, dt=FP32):
                return ph.enter_context(nc.sbuf_tensor(name, shape, dt))

            XS, YS, GS = 9, 2, 8
            WS1 = 3
            vrow = sb("vrow", [NV, P])
            aw = sb("aw", [P, WS1, KT, AS])
            xt = sb("xt", [P, XS, D])
            junk = sb("junk1", [P, D], mybir.dt.bfloat16)
            mrow = sb("mrow", [2, 2, AS])
            diag = sb("diag", [P, GS, P])
            y = sb("y", [P, YS, TQ])
            ss = sb("ss", [P, NCH])
            ms = sb("ms", [P, NCH])
            rt = sb("rt", [P, NCH])
            rstd = sb("rstd", [P, NCH])
            newton = sb("newton", [P, 3, NCH])
            wg = sb("wg", [P, KT, NGATE])
            th = sb("th", [P, 2 * KT])
            s1 = sb("s1", [P, 2 * KT])
            sc = sb("sc", [P, KT, 2])
            modA = sb("modA", [P, KT, 2])
            modB = sb("modB", [P, KT, 2])
            sc1 = sb("sc1", [P, KT, 2])

            v_loaded = sem("v_loaded"); aw_loaded = [sem(f"aw_loaded{n}") for n in range(WS1)]
            x_loaded = [sem(f"x_loaded{n}") for n in range(XS)]
            ident_made = sem("ident_made"); v_turned = sem("v_turned"); vcol_made = sem("vcol_made")
            c_tanh = sem("c_tanh"); c_ready = sem("c_ready"); aw_used = sem("aw_used")
            mod_dve = sem("mod_dve"); squared = sem("squared"); rooted = sem("rooted")
            norm_dve = sem("norm_dve"); diag_made = sem("diag_made"); row_made = sem("row_made")
            row_turned = sem("row_turned"); x_turned = sem("x_turned")
            y_made = sem("y_made"); y_split = sem("y_split")
            GSTEP = 6
            block = ph.enter_context(nc.Block())

            @block.sync
            def _(sp):
                for key, src in (("norm", norm_w[0]), ("ada", ada_b[0]), ("head", head_norm_w[0]),
                                 ("pool", pool_scale[0]), ("c", c[0]), ("cc", c_ctx)):
                    rows = src.shape[0] // P
                    sp.dma_start(vrow[VR[key]:VR[key] + rows, :],
                                 src.rearrange("(a b) -> a b", b=P)).then_inc(v_loaded, 16)
                for n in range(NAS):
                    if n == NEARLY:
                        sp.dma_start(wg[:, :, :], in_v[:, :, GATE0:GATE0 + NGATE]).then_inc(g_loaded, 16)
                        sp.dma_start(gbias[:, :], gate_b[0].rearrange("(a b) -> a b", b=1)).then_inc(g_loaded, 16)
                    if n >= WS1:
                        sp.wait_ge(aw_used, n - WS1 + 1)
                    sp.dma_start(aw[:, n % WS1], ada_v[:, :, n * AS:(n + 1) * AS]).then_inc(aw_loaded[n % WS1], 16)

            @block.gpsimd
            def _(pool):
                nc.gpsimd.memset(ident[:, :], 0.0).then_inc(ident_made, 1)
                pool.wait_ge(ident_made, 1)
                nc.gpsimd.affine_select(out=ident[:, :], in_=ident[:, :], compare_op=ALU.not_equal, fill=1.0,
                                        base=0, pattern=[[-1, P]], channel_multiplier=1).then_inc(ident_made, 1)
                for n, (g, r) in enumerate(tiles):
                    if 2 <= n < XS:
                        pool.wait_ge(aw_used, n - 1)
                    if n >= XS:
                        back = tiles[n - XS][0]
                        pool.wait_ge(x_turned, KT * (back + 1))
                    src = groups[g][3]
                    row = (n - first[g]) * P + (0 if g == 0 else groups[g][1] - CTX)
                    pool.dma_start(xt[:, n % XS, :], src[row:row + P, :]).then_inc(x_loaded[n % XS], 16)

            @block.tensor
            def _(pe):
                pe.wait_ge(ident_made, 2)
                pe.wait_ge(v_loaded, 16 * 6)
                pe.transpose(bank[0][:, 0:NV], vrow[:, :], ident[0:NV, 0:NV]).then_inc(v_turned, 1)
                pe.wait_ge(c_ready, 1)

                def modulation(n):
                    pe.wait_ge(aw_loaded[n % WS1], 16 * (n // WS1 + 1))
                    if n >= 2:
                        pe.wait_ge(row_made, n - 1)
                    for k in range(KT):
                        mm = pe.matmul(bank[6 + n % 2][0:2, 0:AS], sc[:, k, :], aw[:, n % WS1, k, :],
                                       start=(k == 0), stop=(k == KT - 1))
                    mm.then_inc(aw_used, 1)

                def turn_row(n):
                    pe.wait_ge(row_made, n + 1)
                    for t in range(TS):
                        f = n * TS + t
                        mm = pe.transpose(bank[1][:, 2 * f:2 * f + 2], mrow[:, n % 2, t * P:(t + 1) * P], ident[0:2, 0:2])
                    mm.then_inc(row_turned, 1)

                for n in range(NEARLY):
                    modulation(n)
                    if n >= 1:
                        turn_row(n - 1)
                turn_row(NEARLY - 1)
                for g, (w, t0, kind, _) in enumerate(groups):
                    for j in range(KT):
                        m = KT * g + j
                        pe.wait_ge(diag_made, first[g + 1])
                        if m >= 2:
                            pe.wait_ge(y_made, m - 1)
                        for r in range(w):
                            n = first[g] + r
                            mm = pe.matmul(bank[2 + m % 2][:, r * P:(r + 1) * P], xt[:, n % XS, j * P:(j + 1) * P],
                                           diag[:, n % GS, :], start=True, stop=True)
                        mm.then_inc(x_turned, 1)
                        for r, n in enumerate(later(g)):
                            if j == 2 * r + 3:
                                modulation(n)
                            if j == 2 * r + 5:
                                turn_row(n)

            @block.scalar
            def _(act):
                act.wait_ge(vcol_made, 1)
                act.activation(th[:, :], vcol[:, VR["c"]:VR["c"] + 2 * KT], ACT.Tanh, scale=0.5).then_inc(c_tanh, 1)

                def squares(*tiles_):
                    for n in tiles_:
                        act.wait_ge(x_loaded[n % XS], 16 * (n // XS + 1))
                        if n >= 1:
                            act.wait_ge(squared, n)
                        act.activation(junk[:, :], xt[:, n % XS, :], ACT.Square,
                                       accum_out=ss[:, n:n + 1]).then_inc(squared, 1)

                def root(g):
                    act.wait_ge(norm_dve, GSTEP * g + 1)
                    a, b = first[g], first[g + 1]
                    act.activation(rt[:, a:b], ms[:, a:b], ACT.Sqrt).then_inc(rooted, 1)

                for g in range(2):
                    squares(*range(first[g], first[g + 1]))
                    root(g)
                for g, (w, t0, kind, _) in enumerate(groups):
                    for j in range(KT):
                        m = KT * g + j
                        act.wait_ge(x_turned, m + 1)
                        if g == 0 and j == 0:
                            act.wait_ge(mod_dve, 3)
                        if m >= YS:
                            act.wait_ge(y_split, 2 * (m - YS + 1))
                        act.activation(y[:, m % YS, 0:w * P], bank[2 + m % 2][:, 0:w * P], ACT.Identity,
                                       bias=modB[:, j, kind:kind + 1], scale=modA[:, j, kind:kind + 1]).then_inc(y_made, 1)
                        if g >= 1 and g + 1 < len(groups):
                            if j < TQ // P:
                                squares(first[g + 1] + j)
                            elif j == TQ // P:
                                root(g + 1)
                act.wait_ge(g_loaded, 32)
                act.activation(wgh[:, :, :], wg[:, :, :], ACT.Copy).then_inc(g_hi, 1)

            @block.vector
            def _(dve):
                dve.wait_ge(v_turned, 1)
                dve.tensor_copy(vcol[:, 0:NV], bank[0][:, 0:NV]).then_inc(vcol_made, 1)
                dve.wait_ge(vcol_made, 1)
                dve.wait_ge(c_tanh, 1)
                dve.scalar_tensor_tensor(out=s1[:, :], in0=th[:, :], scalar=1.0,
                                         in1=vcol[:, VR["c"]:VR["c"] + 2 * KT], op0=ALU.add,
                                         op1=ALU.mult).then_inc(vcol_made, 1)
                dve.wait_ge(vcol_made, 2)
                dve.tensor_scalar(sc[:, :, :], s1[:, :].rearrange("p (a j) -> p j a", a=2), 0.5, None,
                                  ALU.mult).then_inc(c_ready, 1)

                def scales(g):
                    a, b = first[g], first[g + 1]
                    dve.wait_ge(squared, b)
                    dve.tensor_scalar(ms[:, a:b], ss[:, a:b], 1.0 / D, EPS, ALU.mult, ALU.add).then_inc(norm_dve, 1)
                    dve.wait_ge(rooted, g + 1)
                    dve.reciprocal(rstd[:, a:b], rt[:, a:b]).then_inc(norm_dve, 1)
                    for n, (dst, in0, in1) in enumerate(((newton[:, 0], rstd, ms), (newton[:, 1], newton[:, 0], rstd))):
                        dve.wait_ge(norm_dve, GSTEP * g + 2 + n)
                        dve.tensor_tensor(dst[:, a:b], in0[:, a:b], in1[:, a:b], ALU.mult).then_inc(norm_dve, 1)
                    dve.wait_ge(norm_dve, GSTEP * g + 4)
                    dve.tensor_scalar(newton[:, 2, a:b], newton[:, 1, a:b], -0.5, 1.5, ALU.mult, ALU.add).then_inc(norm_dve, 1)
                    dve.wait_ge(norm_dve, GSTEP * g + 5)
                    dve.tensor_tensor(rstd[:, a:b], rstd[:, a:b], newton[:, 2, a:b], ALU.mult).then_inc(norm_dve, 1)
                    dve.wait_ge(norm_dve, GSTEP * g + 6)
                    if g >= 2:
                        dve.wait_ge(x_turned, KT * (g - 1))
                    for n in range(a, b):
                        dve.tensor_scalar(diag[:, n % GS, :], ident[:, :], rstd[:, n:n + 1], None,
                                          ALU.mult).then_inc(diag_made, 1)

                def copy_row(n):
                    dve.wait_ge(aw_used, n + 1)
                    if n >= 2:
                        dve.wait_ge(row_turned, n - 1)
                    dve.tensor_copy(mrow[:, n % 2, :], bank[6 + n % 2][0:2, 0:AS]).then_inc(row_made, 1)

                copy_row(0)
                copy_row(1)
                scales(0)
                for n in range(2, 10):
                    copy_row(n)
                scales(1)
                for n in range(10, NEARLY):
                    copy_row(n)
                dve.wait_ge(row_turned, NEARLY)
                mod = bank[1][:, 0:6 * KT].rearrange("p (f a) -> p f a", a=2)
                for a in range(2):
                    dve.tensor_tensor(modB[:, :, a], mod[:, 0:KT, a], vcol[:, VR["ada"]:VR["ada"] + KT],
                                      ALU.add)
                    last = dve.tensor_tensor(sc1[:, :, a], mod[:, KT:2 * KT, a],
                                             vcol[:, VR["ada"] + KT:VR["ada"] + 2 * KT], ALU.add)
                last.then_inc(mod_dve, 1)
                dve.wait_ge(mod_dve, 1)
                for a in range(2):
                    dve.scalar_tensor_tensor(out=modA[:, :, a], in0=sc1[:, :, a], scalar=1.0,
                                             in1=vcol[:, VR["norm"]:VR["norm"] + KT], op0=ALU.add,
                                             op1=ALU.mult).then_inc(mod_dve, 1)
                for g, (w, t0, kind, _) in enumerate(groups):
                    for j in range(KT):
                        if g >= 1 and g + 1 < len(groups) and j == TQ // P + 1:
                            scales(g + 1)
                        m = KT * g + j
                        dve.wait_ge(y_made, m + 1)
                        n = w * P
                        dve.tensor_copy(xn(0, j, t0, n), y[:, m % YS, 0:n]).then_inc(y_split, 1)
                        dve.wait_ge(y_split, 2 * m + 1)
                        dve.tensor_tensor(xn(1, j, t0, n), y[:, m % YS, 0:n], f32(xn(0, j, t0, n)),
                                          ALU.subtract).then_inc(y_split, 1)
                        for r, n in enumerate(later(g)):
                            if j == 2 * r + 3:
                                copy_row(n)
                dve.wait_ge(g_hi, 1)
                dve.tensor_tensor(wgl[:, :, :], wg[:, :, :], f32(wgh[:, :, :]), ALU.subtract).then_inc(g_lo, 1)
                dve.wait_ge(row_turned, NAS)
                dve.tensor_tensor(mgate[:, :], mod[:, 2 * KT:3 * KT, 0],
                                  vcol[:, VR["ada"] + 2 * KT:VR["ada"] + 3 * KT], ALU.add).then_inc(mod_dve, 1)
                dve.wait_ge(mod_dve, 4)
                dve.tensor_scalar(mgate[:, :], mgate[:, :], 0.5, None, ALU.mult).then_inc(mod_dve, 1)
                dve.tensor_scalar(vcol[:, VR["pool"]:VR["pool"] + PG], vcol[:, VR["pool"]:VR["pool"] + PG],
                                  0.5, None, ALU.mult)



        HC = HEADS * NCH
        with ExitStack() as ph:
            def sb(name, shape, dt=FP32):
                return ph.enter_context(nc.sbuf_tensor(name, shape, dt))

            wraw = sb("wraw", [P, 2, KT, P])
            wh = sb("wh", [P, 2, KT, P], FP32R)
            wl = sb("wl", [P, 2, KT, P], FP32R)
            qks = sb("qks", [P, 2, 4, 2, P], FP32R)
            ymaj = sb("ymaj", [P, 2, TQ])
            kts = sb("kts", [P, 2, 4, P])
            vs = sb("vs", [P, 2, 4, 2, P], FP32R)
            pz = sb("pz", [P, 3 * TQ])
            pzs, tz = pz[:, 0:2 * TQ].rearrange("p (a t) -> p a t", a=2), pz[:, 2 * TQ:3 * TQ]

            grow = pz[0:NGATE, 0:TQ]
            gi = [sb(f"gi{d}", [HC, P]) for d in range(2)]
            gf = [sb(f"gf{d}", [HC, P]) for d in range(2)]
            gb = [sb(f"gb{d}", [HC, P]) for d in range(2)]
            gt = [sb(f"gt{d}", [HC, P]) for d in range(2)]
            gm = [sb(f"gm{d}", [HC, P]) for d in range(2)]
            gq = [pz[0:HC, d * NQ * P:(d + 1) * NQ * P].rearrange("p (q t) -> p q t", q=NQ) for d in range(2)]
            zeros = sb("zeros", [HC, P])
            ce = [sb(f"ce{d}", [HEADS, 2, NCH]) for d in range(2)]
            cm = [sb(f"cm{d}", [HEADS, NCH]) for d in range(2)]
            mprev = [sb(f"mprev{d}", [HC, 1]) for d in range(2)]
            nmend = [sb(f"nmend{d}", [HC, 1]) for d in range(2)]
            colst = sb("colst", [P, NCH, NQ, HEADS])
            dexp = [sb(f"dexp{d}", [HC, 1]) for d in range(2)]
            R_LF, R_CUM, R_A, R_ENDS = 3, 5, 7, 9
            R_CARRY = R_ENDS + 6
            R_M = R_CARRY + 2
            R_NEGM = R_M + 4
            R_QUANT = R_NEGM + 8

            g_done = sem("g_done")
            g_row = sem("g_row"); g_stored = sem("g_stored"); g_back = sem("g_back"); r_act = sem("r_act")
            r_dve = sem("r_dve"); ends_st = sem("ends_st"); ends_ld = sem("ends_ld"); mp_st = sem("mp_st")
            mp_ld = sem("mp_ld"); negm_st = sem("negm_st"); q_turned = sem("q_turned"); q_cols = sem("q_cols")
            cols_st = sem("cols_st")
            gpieces = [(0, CTX)] + [(CTX + TQ * n, TQ) for n in range(NTQ)]
            AT = {"decay": 1, "carry": 3, "weights": 5, "columns": 7}
            w_loaded = [sem(f"w_loaded{n}") for n in range(2)]
            w_hi = sem("w_hi"); w_lo = sem("w_lo")
            piece_done = sem("piece_done"); piece_read = sem("piece_read")
            qk_hi = sem("qk_hi"); qk_stored = [sem(f"qk_stored{n}") for n in range(2)]
            y_copied = sem("y_copied"); turned = sem("turned")
            turned_read = sem("turned_read"); v_hi = sem("v_hi")
            kt_stored = [sem(f"kt_stored{n}") for n in range(2)]
            v_stored = [sem(f"v_stored{n}") for n in range(2)]
            pz_stored = [sem(f"pz_stored{n}") for n in range(2)]
            tz_made = sem("tz_made"); xe_stored = sem("xe_stored")

            UNITS = [(t, kind) for t in range(HB) for kind in "qkv"] + [(0, "p"), (0, "s")]
            OFF = {"q": (Q0, HD), "k": (K0, HD), "v": (V0, HD), "p": (POOL0, P), "s": (ZP0, P)}
            cpiece, xpieces = (0, CTX), [(CTX + TQ * n, TQ) for n in range(NTQ)]
            PIECES = [(u, t, kind, t0, w) for u, (t, kind) in enumerate(UNITS)
                      for t0, w in ([cpiece] if kind in "kv" else []) + xpieces]
            NU, NPC = len(UNITS), len(PIECES)
            nqk = [sum(p[2] in "qk" for p in PIECES[:m]) for m in range(NPC + 1)]
            ntr = [sum(p[2] in "kv" for p in PIECES[:m]) for m in range(NPC + 1)]
            nk = [sum(p[2] == "k" for p in PIECES[:m]) for m in range(NPC + 1)]
            nv = [sum(p[2] == "v" for p in PIECES[:m]) for m in range(NPC + 1)]
            def unit_end(u):
                return NPC + 1 + max(m for m in range(NPC) if PIECES[m][0] == u)

            npz = [sum(p[2] in "ps" for p in PIECES[:m]) for m in range(NPC + 1)]
            assert NU % 2 == 0 and NPC % 4 == 0 and nqk[-1] % 2 == 0 and ntr[-1] % 2 == 0 and nk[-1] % 2 == 0
            block = ph.enter_context(nc.Block())

            def heads(eng, body):
                body(0, True)
                with eng.Fori(1, HEADS - 1) as i:
                    body(i, True)
                body(HEADS - 1, False)

            @block.sync
            def _(sp):
                def tile(i, u):
                    t, kind = UNITS[u % NU]
                    first_col, per_head = OFF[kind]
                    sp.wait_ge(w_hi, i * NU + (u + 1))
                    sp.wait_ge(w_lo, i * NU + (u + 1))
                    sp.dma_start(wraw[:, u % 2],
                                 in_v[:, :, bass.ds(i * per_head + (first_col + t * P + (u // NU) * per_head), P)])\
                        .then_inc(w_loaded[u % 2], 16)

                def store_turned(i, m):
                    u, t, kind, t0, w = PIECES[m]
                    r, cw, c0 = ntr[m], w // P, t0 // P
                    sp.wait_ge(turned_read, i * ntr[-1] + (r + 1 + 2))
                    if kind == "k":
                        sp.dma_start(kt_d[i, c0:c0 + cw, :, t * P:(t + 1) * P].rearrange("c p f -> p c f"),
                                     kts[:, nk[m] % 2, 0:cw]).then_inc(kt_stored[nk[m] % 2], 16)
                    else:
                        sp.dma_start(v_d[i, c0:c0 + cw, :, t].rearrange("c p a f -> p c (a f)"),
                                     f32(vs[:, nv[m] % 2, 0:cw]).rearrange("p c a f -> p c (a f)"))\
                            .then_inc(v_stored[nv[m] % 2], 16)

                def body(i, ahead):
                    for m, (u, t, kind, t0, w) in enumerate(PIECES):
                        if (m == 0 or PIECES[m - 1][0] != u) and (u + 3 < NU or ahead):
                            tile(i, u + 3)
                        cw, c0 = w // P, t0 // P
                        if kind in "qk":
                            a = nqk[m]
                            sp.wait_ge(piece_read, i * NPC + (m + 1 + 4))
                            sp.dma_start(qk_d[i, "qk".index(kind), t, :, c0:c0 + cw].rearrange("p c a t -> p (c a t)"),
                                         f32(qks[:, a % 2, 0:cw]).rearrange("p c a t -> p (c a t)"))\
                                .then_inc(qk_stored[a % 2], 16)
                        if kind in "ps":
                            a = npz[m]
                            sp.wait_ge(piece_read, i * NPC + (m + 1 + 4))
                            sp.dma_start((p_d if kind == "p" else zp_d)[i, :, t0 - CTX:t0 - CTX + w],
                                         pzs[:, a % 2, 0:w]).then_inc(pz_stored[a % 2], 16)
                        if m >= 1 and PIECES[m - 1][2] in "kv":
                            store_turned(i, m - 1)

                for u in range(3):
                    tile(0, u)
                heads(sp, body)
                for n in range(2):
                    sp.wait_ge(pz_stored[n], 16 * HEADS * npz[-1] // 2)
                    sp.wait_ge(qk_stored[n], 16 * HEADS * nqk[-1] // 2)
                    sp.wait_ge(kt_stored[n], 16 * HEADS * nk[-1] // 2)
                    sp.wait_ge(v_stored[n], 16 * HEADS * nv[-1] // 2)

            @block.gpsimd
            def _(pool):
                for n, (t0, w) in enumerate(gpieces):
                    pool.wait_ge(g_row, n + 1)
                    pool.dma_start(gates_d[:, t0:t0 + w], grow[:, 0:w]).then_inc(g_stored, 16)
                pool.wait_ge(g_stored, 16 * len(gpieces))
                for d in range(2):
                    for k, dst in ((0, gi[d]), (1, gf[d])):
                        r = 2 * HEADS * d + HEADS * k
                        pool.dma_start(dst[:, :], gates_d[r:r + HEADS, :].rearrange("h (c t) -> (h c) t", t=P))\
                            .then_inc(g_back, 16)
                pool.wait_ge(r_dve, R_ENDS)
                for d in range(2):
                    e = P - 1 if d == 0 else 0
                    pool.dma_start(ends_d[d, 0].rearrange("(a b) -> a b", b=1), gm[d][:, e:e + 1]).then_inc(ends_st, 16)
                    pool.dma_start(ends_d[d, 1].rearrange("(a b) -> a b", b=1), gb[d][:, e:e + 1]).then_inc(ends_st, 16)
                pool.wait_ge(ends_st, 64)
                for d in range(2):
                    pool.dma_start(ce[d][:, :, :], ends_d[d].rearrange("q (h c) -> h q c", h=HEADS)).then_inc(ends_ld, 16)
                pool.wait_ge(r_dve, R_CARRY)
                for d in range(2):
                    pool.dma_start(mprev_d[d].rearrange("(h c) -> h c", h=HEADS), cm[d][:, :]).then_inc(mp_st, 16)
                pool.wait_ge(mp_st, 32)
                for d in range(2):
                    pool.dma_start(mprev[d][:, :], mprev_d[d].rearrange("(a b) -> a b", b=1)).then_inc(mp_ld, 16)
                pool.wait_ge(r_dve, R_NEGM)
                for d in range(2):
                    pool.dma_start(negm_d[d].rearrange("h c t -> (h c) t"), gt[d][:, :]).then_inc(negm_st, 16)
                for d in range(2):
                    pool.wait_ge(q_cols, d + 1)
                    pool.dma_start(cols_d[:, d], colst[:, :, :, :]).then_inc(cols_st, 16)
                for part in range(2):
                    pool.dma_start(xe_d[part], f32(xearly[part][:, :, CTX:CTX + HALF])).then_inc(xe_stored, 16)
                pool.wait_ge(negm_st, 32)
                pool.wait_ge(cols_st, 32)
                pool.wait_ge(xe_stored, 32)

            @block.tensor
            def _(pe):
                pe.sem_inc(piece_done, NPC)
                pe.sem_inc(turned, 2)

                def turn(i, m):
                    u, t, kind, t0, w = PIECES[m]
                    r = ntr[m]
                    if kind == "k":
                        pe.wait_ge(y_copied, i * nk[-1] + (nk[m] + 1))
                    else:
                        pe.wait_ge(piece_read, i * NPC + (m + 1 + 4))
                    pe.wait_ge(turned_read, i * ntr[-1] + (r + 1))
                    for b in range(w // P):
                        mm = pe.transpose(bank[4 + r % 2][:, b * P:(b + 1) * P],
                                          ymaj[:, r % 2, b * P:(b + 1) * P], ident[:, :])
                    mm.then_inc(turned, 1)

                def turn_rows():
                    pe.wait_ge(r_act, 8)
                    for d in range(2):
                        for q in range(NQ):
                            mm = pe.transpose(bank[6 + d][:, q * HC:(q + 1) * HC], gq[d][:, q, :], ident[0:HC, 0:HC])
                        mm.then_inc(q_turned, 1)

                pe.wait_ge(g_lo, 1)
                for n, (t0, w) in enumerate(gpieces):
                    if n >= 2:
                        pe.wait_ge(g_row, n - 1)
                    for k in range(KT):
                        for n3, (a, b) in enumerate(((wgh, 0), (wgh, 1), (wgl, 0))):
                            mm = pe.matmul(bank[6 + n % 2][0:NGATE, 0:w], a[:, k, :], xn(b, k, t0, w),
                                           start=(k == 0 and n3 == 0), stop=(k == KT - 1 and n3 == 2))
                    mm.then_inc(g_done, 1)
                def body(i, ahead):
                    for m, (u, t, kind, t0, w) in enumerate(PIECES):
                        if m == 0 or PIECES[m - 1][0] != u:
                            pe.wait_ge(w_hi, i * NU + (u + 1 + 2))
                            pe.wait_ge(w_lo, i * NU + (u + 1 + 2))
                        pe.wait_ge(piece_read, i * NPC + (m + 1))
                        for k in range(KT):
                            for n, (a, b) in enumerate(((wh, 0), (wh, 1), (wl, 0))):
                                mm = pe.matmul(bank[m % 4][:, 0:w], a[:, u % 2, k, :], xn(b, k, t0, w),
                                               start=(k == 0 and n == 0), stop=(k == KT - 1 and n == 2))
                        mm.then_inc(piece_done, 1)
                        if m >= 1 and PIECES[m - 1][2] in "kv":
                            turn(i, m - 1)
                        if isinstance(i, int) and i == 0 and m == AT["columns"]:
                            turn_rows()

                heads(pe, body)

            @block.scalar
            def _(act):
                act.sem_inc(w_hi, 2)

                def turned_hi(i, m):
                    u, t, kind, t0, w = PIECES[m]
                    if kind == "v":
                        r, a, cw = ntr[m], nv[m], w // P
                        act.wait_ge(turned, i * ntr[-1] + (r + 1 + 2))
                        act.wait_ge(v_stored[a % 2], i * (16 * nv[-1] // 2) + 16 * (a // 2))
                        act.activation(vs[:, a % 2, 0:cw, 0, :],
                                       bank[4 + r % 2][:, 0:w].rearrange("p (c t) -> p c t", t=P),
                                       ACT.Copy).then_inc(v_hi, 1)

                def split_hi(i, u):
                    act.wait_ge(w_loaded[u % 2], i * (16 * NU // 2) + 16 * (u // 2 + 1))
                    if u >= 2:
                        act.wait_ge(piece_done, i * NPC + unit_end(u - 2))
                    act.activation(wh[:, u % 2], wraw[:, u % 2], ACT.Copy).then_inc(w_hi, 1)

                def decay_logs():
                    act.wait_ge(g_back, 64)
                    for d in range(2):
                        act.activation(gt[d][:, :], gf[d][:, :], ACT.Abs).then_inc(r_act, 1)
                    act.wait_ge(r_act, 2)
                    for d in range(2):
                        act.activation(gm[d][:, :], gt[d][:, :], ACT.Exp, scale=-1.0).then_inc(r_act, 1)
                    act.wait_ge(r_act, 4)
                    for d in range(2):
                        act.activation(gb[d][:, :], gm[d][:, :], ACT.Ln, bias=1.0).then_inc(r_act, 1)
                def weights():
                    act.wait_ge(r_dve, R_QUANT)
                    for d in range(2):
                        act.activation(gq[d][:, 1, :], gm[d][:, :], ACT.Exp, bias=mprev[d][:, 0:1], scale=-1.0)
                        act.activation(gq[d][:, 2, :], gf[d][:, :], ACT.Exp, scale=-1.0)
                        act.activation(gq[d][:, 3, :], gi[d][:, :], ACT.Exp, bias=nmend[d][:, 0:1])
                        act.activation(gq[d][:, 4, :], zeros[:, :], ACT.Exp, bias=dexp[d][:, 0:1]).then_inc(r_act, 1)

                split_hi(0, 0)
                split_hi(0, 1)
                for n, (t0, w) in enumerate(gpieces):
                    act.wait_ge(g_done, n + 1)
                    if n >= 1:
                        act.wait_ge(g_stored, 16 * n)
                    act.activation(grow[:, 0:w], bank[6 + n % 2][0:NGATE, 0:w], ACT.Identity,
                                   bias=gbias[:, 0:1]).then_inc(g_row, 1)

                def body(i, ahead):
                    for m, (u, t, kind, t0, w) in enumerate(PIECES):
                        scale = HD ** -0.5 if kind == "k" else 1.0
                        if kind in "qk":
                            a, cw = nqk[m], w // P
                            act.wait_ge(piece_done, i * NPC + (NPC + m + 1))
                            if kind == "k":
                                act.wait_ge(turned, i * ntr[-1] + (ntr[m] + 1))
                                act.activation(ymaj[:, ntr[m] % 2, 0:w], bank[m % 4][:, 0:w], ACT.Copy,
                                               scale=scale).then_inc(y_copied, 1)
                            act.wait_ge(qk_stored[a % 2], i * (16 * nqk[-1] // 2) + 16 * (a // 2))
                            act.activation(qks[:, a % 2, 0:cw, 0, :],
                                           bank[m % 4][:, 0:w].rearrange("p (c t) -> p c t", t=P),
                                           ACT.Copy, scale=scale).then_inc(qk_hi, 1)
                        if kind == "s":
                            act.wait_ge(piece_done, i * NPC + (NPC + m + 1))
                            act.wait_ge(piece_read, i * NPC + (m + 4))
                            act.activation(tz[:, 0:w], bank[m % 4][:, 0:w], ACT.Tanh, scale=0.5).then_inc(tz_made, 1)
                        if m >= 1 and PIECES[m - 1][2] in "kv":
                            turned_hi(i, m - 1)
                        if (m + 1 == NPC or PIECES[m + 1][0] != u) and (u + 2 < NU or ahead):
                            split_hi(i, u + 2)
                        if isinstance(i, int) and i == 0:
                            if m == AT["decay"]:
                                decay_logs()
                            elif m == AT["weights"]:
                                weights()

                heads(act, body)

            @block.vector
            def _(dve):
                dve.sem_inc(w_lo, 2)
                dve.sem_inc(piece_read, 4)
                dve.sem_inc(turned_read, 2)

                def turned_lo(i, m):
                    u, t, kind, t0, w = PIECES[m]
                    r, cw = ntr[m], w // P
                    src = bank[4 + r % 2][:, 0:w].rearrange("p (c t) -> p c t", t=P)
                    if kind == "k":
                        a = nk[m]
                        dve.wait_ge(turned, i * ntr[-1] + (r + 1 + 2))
                        dve.wait_ge(kt_stored[a % 2], i * (16 * nk[-1] // 2) + 16 * (a // 2))
                        dve.tensor_copy(kts[:, a % 2, 0:cw], src).then_inc(turned_read, 1)
                    else:
                        a = nv[m]
                        dve.wait_ge(v_hi, i * nv[-1] + (a + 1))
                        dve.tensor_tensor(vs[:, a % 2, 0:cw, 1, :], src, f32(vs[:, a % 2, 0:cw, 0, :]),
                                          ALU.subtract).then_inc(turned_read, 1)

                def split_lo(i, u):
                    dve.wait_ge(w_hi, i * NU + (u + 1 + 2))
                    dve.tensor_tensor(wl[:, u % 2], wraw[:, u % 2], f32(wh[:, u % 2]), ALU.subtract).then_inc(w_lo, 1)

                def decays():
                    dve.wait_ge(r_act, 6)
                    for d in range(2):
                        dve.scalar_tensor_tensor(out=gf[d][:, :], in0=gf[d][:, :], scalar=0.0, in1=gb[d][:, :],
                                                 op0=ALU.min, op1=ALU.subtract).then_inc(r_dve, 1)
                    dve.wait_ge(r_dve, R_LF)
                    fwd = [slice(None), slice(None, None, -1)]
                    for d in range(2):
                        s = fwd[d]
                        dve.tensor_tensor_scan(gb[d][:, s], zeros[:, :], gf[d][:, s], 0.0, ALU.add,
                                               ALU.add).then_inc(r_dve, 1)
                    dve.wait_ge(r_dve, R_CUM)
                    for d in range(2):
                        dve.tensor_tensor(gi[d][:, :], gi[d][:, :], gb[d][:, :], ALU.subtract).then_inc(r_dve, 1)
                    dve.wait_ge(r_dve, R_A)
                    for d in range(2):
                        s = fwd[d]
                        dve.tensor_tensor_scan(gm[d][:, s], zeros[:, :], gi[d][:, s], -3e38, ALU.add,
                                               ALU.max).then_inc(r_dve, 1)

                def carry():
                    dve.wait_ge(ends_ld, 32)
                    for d in range(2):
                        order = list(range(NCH)) if d == 0 else list(range(NC - 1, -1, -1)) + list(range(NCH - 1, NC - 1, -1))
                        dve.memset(cm[d][:, order[0]:order[0] + 1], M_INIT).then_inc(r_dve, 1)
                        if d == 0:
                            dve.wait_ge(r_dve, R_ENDS + 1)
                            dve.tensor_tensor_scan(cm[0][:, 1:NCH], ce[0][:, 0, 0:NCH - 1], ce[0][:, 1, 0:NCH - 1],
                                                   M_INIT, ALU.max, ALU.add).then_inc(r_dve, 1)
                        else:
                            dve.wait_ge(r_dve, R_ENDS + 3)
                            dve.tensor_tensor_scan(cm[1][:, 0:1], ce[1][:, 0, 1:2], ce[1][:, 1, 1:2],
                                                   M_INIT, ALU.max, ALU.add).then_inc(r_dve, 1)
                            dve.wait_ge(r_dve, R_ENDS + 4)
                            dve.tensor_tensor_scan(cm[1][:, NCH - 1:NCH], ce[1][:, 0, 0:1], ce[1][:, 1, 0:1],
                                                   cm[1][:, 0:1], ALU.max, ALU.add).then_inc(r_dve, 1)
                            dve.wait_ge(r_dve, R_ENDS + 5)
                            dve.tensor_tensor_scan(cm[1][:, NCH - 2:NC - 1:-1], ce[1][:, 0, NCH - 1:NC:-1],
                                                   ce[1][:, 1, NCH - 1:NC:-1], cm[1][:, NCH - 1:NCH],
                                                   ALU.max, ALU.add).then_inc(r_dve, 1)

                def exponents():
                    dve.wait_ge(mp_ld, 32)
                    for d in range(2):
                        dve.tensor_scalar(gm[d][:, :], gm[d][:, :], mprev[d][:, 0:1], None, ALU.max).then_inc(r_dve, 1)
                    dve.wait_ge(r_dve, R_M)
                    for d in range(2):
                        e = P - 1 if d == 0 else 0
                        dve.tensor_scalar(gt[d][:, :], gm[d][:, :], -1.0, None, ALU.mult).then_inc(r_dve, 1)
                        dve.tensor_scalar(nmend[d][:, :], gm[d][:, e:e + 1], -1.0, None, ALU.mult).then_inc(r_dve, 1)
                    for d in range(2):
                        dve.tensor_tensor(gf[d][:, :], gb[d][:, :], gm[d][:, :], ALU.add).then_inc(r_dve, 1)
                        dve.tensor_copy(gq[d][:, 0, :], gi[d][:, :]).then_inc(r_dve, 1)
                    dve.wait_ge(r_dve, R_NEGM + 4)
                    for d in range(2):
                        dve.tensor_scalar(gf[d][:, :], gf[d][:, :], -88.0, None, ALU.max).then_inc(r_dve, 1)
                        dve.tensor_tensor(dexp[d][:, :], mprev[d][:, :], nmend[d][:, :], ALU.add).then_inc(r_dve, 1)

                def columns():
                    for d in range(2):
                        dve.wait_ge(q_turned, d + 1)
                        if d == 1:
                            dve.wait_ge(cols_st, 16)
                        dve.tensor_copy(colst[:, :, :, :], bank[6 + d][:, 0:NQ * HC]
                                        .rearrange("p (q h c) -> p c q h", q=NQ, h=HEADS)).then_inc(q_cols, 1)

                dve.memset(zeros[:, :], 0.0).then_inc(r_dve, 1)
                dve.wait_ge(r_dve, 1)
                split_lo(0, 0)
                split_lo(0, 1)

                def body(i, ahead):
                    for m, (u, t, kind, t0, w) in enumerate(PIECES):
                        if kind in "qk":
                            a, cw = nqk[m], w // P
                            dve.wait_ge(qk_hi, i * nqk[-1] + (a + 1))
                            dve.scalar_tensor_tensor(
                                out=qks[:, a % 2, 0:cw, 1, :],
                                in0=bank[m % 4][:, 0:w].rearrange("p (c t) -> p c t", t=P),
                                scalar=HD ** -0.5 if kind == "k" else 1.0, in1=f32(qks[:, a % 2, 0:cw, 0, :]),
                                op0=ALU.mult, op1=ALU.subtract).then_inc(piece_read, 1)
                        elif kind in "ps":
                            a = npz[m]
                            dve.wait_ge(pz_stored[a % 2], i * (16 * npz[-1] // 2) + 16 * (a // 2))
                            if kind == "p":
                                dve.wait_ge(piece_done, i * NPC + (NPC + m + 1))
                                dve.tensor_copy(pzs[:, a % 2, 0:w], bank[m % 4][:, 0:w]).then_inc(piece_read, 1)
                            else:
                                dve.wait_ge(tz_made, i * NTQ + (a - NTQ + 1))
                                dve.scalar_tensor_tensor(out=pzs[:, a % 2, 0:w], in0=tz[:, 0:w], scalar=1.0,
                                                         in1=bank[m % 4][:, 0:w], op0=ALU.add,
                                                         op1=ALU.mult).then_inc(piece_read, 1)
                        else:
                            dve.wait_ge(piece_done, i * NPC + (NPC + m + 1))
                            dve.wait_ge(turned, i * ntr[-1] + (ntr[m] + 1))
                            dve.tensor_copy(ymaj[:, ntr[m] % 2, 0:w], bank[m % 4][:, 0:w]).then_inc(piece_read, 1)
                        if m >= 1 and PIECES[m - 1][2] in "kv":
                            turned_lo(i, m - 1)
                        if (m + 1 == NPC or PIECES[m + 1][0] != u) and (u + 2 < NU or ahead):
                            split_lo(i, u + 2)
                        if isinstance(i, int) and i == 0:
                            if m == AT["decay"]:
                                decays()
                            elif m == AT["carry"]:
                                carry()
                            elif m == AT["weights"]:
                                exponents()
                            elif m == AT["columns"]:
                                columns()

                heads(dve, body)

        early.close()
        with ExitStack() as ph:
            def sb(name, shape, dt=FP32):
                return ph.enter_context(nc.sbuf_tensor(name, shape, dt))

            wraw = sb("wraw4", [P, 2, KT, P])
            wh = sb("wh4", [P, 2, KT, P], FP32R)
            wl = sb("wl4", [P, 2, KT, P], FP32R)
            tanh_o = sb("tanh_o", [P, 2, TQ])
            tanh_z = sb("tanh_z", [P, TQ])
            zgate = sb("zgate", [P, TQ])
            ustage = sb("ustage", [P, 2, TQ])
            gstage = sb("gstage", [P, 2, TQ])
            NCHAIN = 2 * HEADS
            PREP = 4
            VS = 4
            state = sb("state", [P, NCHAIN, HB, VW])
            state_h = sb("state_h", [P, 2, HB, VW], FP32R)
            state_l = sb("state_l", [P, 2, HB, VW], FP32R)
            qk_t = sb("qk_t", [P, 2, 2, HB, 2, P], FP32R)
            v_t = sb("v_t", [P, VS, 2, VW], FP32R)
            kt_t = sb("kt_t", [P, VS, HD])
            nm = sb("nm", [P, 2, 2, HEADS, P])
            cmask = sb("cmask", [P, 2, P])
            cols = sb("cols", [P, 2, NCH, NQ * HEADS])
            ccol = sb("ccol", [P, 2, 2, NQ, HEADS])
            wexp = sb("wexp", [P, 2, P])
            pf = sb("pf", [P, 2, P])
            s_lo = sb("s_lo", [P, 2, P])
            p_h = sb("p_h", [P, 2, P], FP32R)
            p_l = sb("p_l", [P, 2, P], FP32R)
            ek_h = sb("ek_h", [P, 2, HD], FP32R)
            ek_l = sb("ek_l", [P, 2, HD], FP32R)
            ysb = sb("ysb", [P, 2, VW])
            num = sb("num", [P, 2, VW])
            den = sb("den", [P, 2, 3])
            hout = sb("hout", [P, 2, HD])
            hother = sb("hother", [P, 2, HD])
            PADR = GRID_H + max(2, 16)
            pool_a = sb("pool_a", [P, PADR * GRID_W])
            pool_b = sb("pool_b", [P, PADR * GRID_W])
            icnt = sb("icnt", [P, 2, GRID_W])

            w_loaded = [sem(f"w4_loaded{n}") for n in range(2)]
            w_hi = sem("w4_hi"); w_lo = sem("w4_lo"); piece_done = sem("piece4_done")
            act_read = sem("act_read"); u_made = sem("u_made"); dz = sem("dz")
            u_stored = [sem(f"u_stored{n}") for n in range(2)]
            g_stored = [sem(f"g4_stored{n}") for n in range(2)]
            qk_loaded = [sem(f"qk_loaded{n}") for n in range(2)]
            vk_loaded = [sem(f"vk_loaded{n}") for n in range(VS)]
            nm_loaded = [sem(f"nm_loaded{n}") for n in range(2)]
            cols_loaded = sem("cols_loaded"); x_back = [sem(f"x_back{n}") for n in range(2)]; setup = sem("setup"); state_zero = sem("state_zero"); mask_made = sem("mask_made")
            chunk_cols = sem("chunk_cols"); s_done = sem("s_done"); w_exp = sem("w_exp"); s_hi = sem("s_hi"); s_copied = sem("s_copied")
            ek_hi = sem("ek_hi"); prep = sem("prep"); ek_lo = sem("ek_lo"); step_done = sem("step_done")
            y_read = sem("y_read"); nm_masked = sem("nm_masked"); zg = sem("zg"); fin = sem("fin"); state_new = sem("state_new")
            h_stored = [sem(f"h_stored{n}") for n in range(2)]
            h_back = [sem(f"h_back{n}") for n in range(2)]
            p_loaded = sem("p_loaded"); box = sem("box"); mix_stored = sem("mix_stored")

            CTX_UBANK = [bank[0:2], bank[2:4]]
            UBANK, XBANK, YBANK, SBANK = bank[2:4], bank[4], bank[5], bank[6]

            STEPS = [(cc, h, d) for cc in range(2) for h in range(HEADS) for d in range(2)]
            NS = len(STEPS)
            TILES = [(k, e) for e in range(2) for k in ("o", "z")] + [(k, e) for e in range(2) for k in ("m", "p")]
            OFF4 = {"o": O0, "z": Z0, "m": GM0, "p": GP0}
            PIECES = [(u, kind, e, tq) for u, (kind, e) in enumerate(TILES) for tq in range(2)]
            NU, NPC = len(TILES), len(PIECES)
            nz = [sum(p[1] == "z" for p in PIECES[:m]) for m in range(NPC + 1)]
            na = [sum(p[1] != "z" for p in PIECES[:m]) for m in range(NPC + 1)]
            ng = [sum(p[1] in "mp" for p in PIECES[:m]) for m in range(NPC + 1)]
            assert NPC == NS and NPC % 4 == 0 and nz[-1] % 2 == 0 and ng[-1] % 2 == 0
            NTRIP = NX // 2
            NCS = NS

            HALFTRIPS = NTRIP // 2

            def trips(eng, body):
                with eng.Fori(0, HALFTRIPS - 1) as i:
                    body(i, True)
                body(HALFTRIPS - 1, True)
                with eng.Fori(HALFTRIPS, NTRIP - 1) as i:
                    body(i, True)
                body(NTRIP - 1, False)

            def half_of(i):
                return int((i if isinstance(i, int) else i.max_val) < HALFTRIPS)

            def row(i):
                return i if half_of(i) else i - HALFTRIPS

            def chunk(i, cc, d):
                return i * 2 + (NC + cc) if d == 0 else i * -2 + (NCH - 1 - cc)

            def ctx_chunk(cc, d):
                return cc if d == 0 else NC - 1 - cc

            def chain(h, d):
                return d * HEADS + h

            block = ph.enter_context(nc.Block())

            @block.sync
            def _(sp):
                for stored in (u_stored, g_stored, h_stored):
                    for n in range(2):
                        sp.sem_inc(stored[n], 1)
                sp.dma_start(cols[:, :, :, :], cols_d.rearrange("p d c q h -> p d c (q h)")).then_inc(cols_loaded, 16)

                def operands(s, L, V, h, c, latent):
                    if latent:
                        sp.wait_ge(step_done, s + 1)
                    elif s >= VS:
                        sp.wait_ge(step_done, s + 1 - (VS - 2))
                    if latent:
                        sp.dma_start(f32(qk_t[:, L]).rearrange("p o b a t -> p (o b) (a t)"),
                                     qk_d[h, :, :, :, c].rearrange("o b p a t -> p (o b) (a t)"))\
                            .then_inc(qk_loaded[L], 16)
                    for a in range(2):
                        sp.dma_start(f32(v_t[:, V, a, 0:HD]).rearrange("p (b f) -> p b f", b=HB),
                                     v_d[h, c, :, :, a]).then_inc(vk_loaded[V], 16)
                    sp.dma_start(kt_t[:, V], kt_d[h, c]).then_inc(vk_loaded[V], 16)

                def tile(i, r, u):
                    kind, e = TILES[u]
                    sp.wait_ge(w_hi, i * NU + (u + 1))
                    sp.wait_ge(w_lo, i * NU + (u + 1))
                    sp.dma_start(wraw[:, u % 2], in_v[:, :, bass.ds(r * (2 * P) + (OFF4[kind] + e * P), P)])\
                        .then_inc(w_loaded[u % 2], 16)

                def store(i, st):
                    cc, h, d = STEPS[st]
                    u, kind, e, tq = PIECES[st]
                    r, half = row(i), half_of(i)
                    t0 = half * HALF + tq * TQ
                    if kind == "z":
                        sp.wait_ge(u_made, i * nz[-1] + (nz[-1] + nz[st] + 1))
                        sp.dma_start(u_d[r * 2 + e, :, t0:t0 + TQ], ustage[:, nz[st] % 2, :])\
                            .then_inc(u_stored[nz[st] % 2], 16)
                    elif kind in "mp":
                        sp.wait_ge(act_read, i * na[-1] + (na[-1] + na[st] + 1))
                        sp.dma_start((gm_d if kind == "m" else gp_d)[r * 2 + e, :, t0:t0 + TQ],
                                     gstage[:, ng[st] % 2, :]).then_inc(g_stored[ng[st] % 2], 16)
                    sp.wait_ge(fin, i * (5 * NS) + 5 * (st + 1))
                    dst = h_d if half_of(i) else hsum_d
                    sp.dma_start(dst[chunk(i, cc, d) - NC, :, h * HD:(h + 1) * HD], hout[:, st % 2, :])\
                        .then_inc(h_stored[st % 2], 16)

                def maxima(i, cc):
                    n, slot = cc + 1, (cc + 1) % 2
                    sp.wait_ge(w_exp, i * NS + NCHAIN * (cc + 1))
                    for dd in range(2):
                        sp.dma_start(nm[:, slot, dd], negm_d[dd, :, chunk(i, n, dd), :].partition_broadcast(P))\
                            .then_inc(nm_loaded[slot], 16)

                def latent_operands(i, st):
                    cc, h, d = STEPS[st % NS]
                    operands(i * NS + (NCS + st), st % 2, st % VS, h, chunk(i, cc + 2 * (st // NS), d), True)

                def other_direction(i, st):
                    cc, h, d = STEPS[st % NS]
                    sp.wait_ge(h_stored[1 - d], 16 * (NS * HALFTRIPS // 2 - HEADS + h + 1) + 1)
                    sp.dma_start(hother[:, st % 2, :],
                                 h_d[chunk(i, cc + 2 * (st // NS), d) - NC, :, h * HD:(h + 1) * HD])\
                        .then_inc(h_back[st % 2], 16)

                def early_quarter(tq):
                    sp.wait_ge(piece_done, NPC * HALFTRIPS + NPC - 1 + tq)
                    for part in range(2):
                        sp.dma_start(f32(xlate[part][:, :, tq * TQ:(tq + 1) * TQ]),
                                     xe_d[part, :, :, tq * TQ:(tq + 1) * TQ]).then_inc(x_back[tq], 16)

                def body(i, ahead):
                    swap = isinstance(i, int) and i == HALFTRIPS - 1
                    for st, (cc, h, d) in enumerate(STEPS):
                        if st % NCHAIN == NCHAIN // 2 and (cc == 0 or ahead):
                            maxima(i, cc)
                        if st % 2 == 0:
                            u = st // 2 + 2
                            if u < NU:
                                tile(i, row(i), u)
                            elif ahead:
                                last = isinstance(i, int) and i == HALFTRIPS - 1
                                tile(i + 1, 0 if last else row(i) + 1, u - NU)
                        if swap and st == NS - 1:
                            early_quarter(0)
                        if st + 2 < NS or ahead:
                            latent_operands(i, st + 2)
                        if swap and st == NS - 1:
                            early_quarter(1)
                        store(i, st)
                        if (half_of(i) == 0 and (st + 2 < NS or ahead)) or (swap and st + 2 >= NS):
                            other_direction(i, st + 2)

                for st, (cc, h, d) in enumerate(STEPS):
                    if st == VS:
                        for u in range(2):
                            tile(0, 0, u)
                        maxima(0, -1)
                    operands(st, st % 2, st % VS, h, ctx_chunk(cc, d), False)
                for st in range(2):
                    latent_operands(0, st)
                trips(sp, body)
                for n in range(2):
                    sp.wait_ge(u_stored[n], 16 * NTRIP * nz[-1] // 2 + 1)
                    sp.wait_ge(g_stored[n], 16 * NTRIP * ng[-1] // 2 + 1)
                    sp.wait_ge(h_stored[n], 16 * NTRIP * NS // 2 + 1)

            @block.tensor
            def _(pe):
                pe.sem_inc(piece_done, NPC)
                pe.sem_inc(step_done, 2)
                pe.wait_ge(setup, 2)

                def scores(l, i, st):
                    L = st % 2
                    pe.wait_ge(qk_loaded[L], i * (16 * NS // 2) + 16 * (st // 2 + 1))
                    pe.wait_ge(prep, l * PREP + 1)
                    def wide(b):
                        return pe.matmul(SBANK[:, 0:2 * P], qk_t[:, L, 1, b, 0, :],
                                         qk_t[:, L, 0, b, :, :].rearrange("p a t -> p (a t)"),
                                         start=(b == 0), stop=(b == HB - 1))

                    for b in range(HB - 1):
                        wide(b)
                    for b in range(HB):
                        pe.matmul(SBANK[:, 0:P], qk_t[:, L, 1, b, 1, :], qk_t[:, L, 0, b, 0, :], start=False, stop=False)
                    wide(HB - 1).then_inc(s_done, 1)

                def step(s, l, L, V, vk):
                    ubank = UBANK if l is not None else CTX_UBANK[L]
                    pe.wait_ge(state_new, s + NCHAIN - (1 if l is None else 0))
                    pe.wait_ge(vk_loaded[V], vk)
                    if l is not None:
                        pe.wait_ge(s_hi, l + 1)
                        pe.wait_ge(prep, l * PREP + (PREP + 1))
                        for b in range(HB):
                            for n, (qa, c_) in enumerate(((0, state_h), (0, state_l), (1, state_h))):
                                pe.matmul(XBANK[:, 0:VW], qk_t[:, L, 0, b, qa, :], c_[:, L, b, :],
                                          start=(b == 0 and n == 0), stop=(b == HB - 1 and n == 2))
                        for n, (p_, va) in enumerate(((p_h, 0), (p_h, 1), (p_l, 0))):
                            pe.matmul(YBANK[:, 0:VW], p_[:, L, :], v_t[:, V, va, :], start=(n == 0), stop=(n == 2))
                    pe.wait_ge(ek_hi, s + 1)
                    pe.wait_ge(ek_lo, s + 1)
                    for b in range(HB):
                        for n, (e_, va) in enumerate(((ek_h, 0), (ek_h, 1), (ek_l, 0))):
                            mm = pe.matmul(ubank[b][:, 0:VW], e_[:, L, b * P:(b + 1) * P],
                                           v_t[:, V, va, :], start=(n == 0), stop=(n == 2))
                    mm.then_inc(step_done, 1)

                def piece(i, m):
                    u, kind, e, tq = PIECES[m]
                    if tq == 0:
                        pe.wait_ge(w_hi, i * NU + (u + 1 + 2))
                        pe.wait_ge(w_lo, i * NU + (u + 1 + 2))
                    pm, trip = (m - 2) % NPC, (1 if m >= 2 else 0)
                    if PIECES[pm][1] == "z":
                        pe.wait_ge(u_made, i * nz[-1] + (nz[-1] * trip + nz[pm] + 1))
                    else:
                        pe.wait_ge(act_read, i * na[-1] + (na[-1] * trip + na[pm] + 1))
                    if half_of(i) == 0:
                        pe.wait_ge(x_back[tq], 32)
                    for k in range(KT):
                        for n, (a, part) in enumerate(((wh, 0), (wh, 1), (wl, 0))):
                            mm = pe.matmul(bank[m % 2][:, :], a[:, u % 2, k, :],
                                           xlate[part][:, k, tq * TQ:(tq + 1) * TQ],
                                           start=(k == 0 and n == 0), stop=(k == KT - 1 and n == 2))
                    mm.then_inc(piece_done, 1)

                for st in range(NCS):
                    step(st, None, st % 2, st % VS, 48 * (st // VS + 1))
                pe.wait_ge(state_new, NCS + NCHAIN)

                def body(i):
                    for st in range(NS):
                        l = i * NS + st
                        scores(l, i, st)
                        piece(i, st)
                        step(l + NCS, l, st % 2, st % VS, i * (48 * NS // VS) + 48 * (NCS // VS + st // VS + 1))

                with pe.Fori(0, NTRIP // 2) as i:
                    body(i)
                with pe.Fori(NTRIP // 2, NTRIP) as i:
                    body(i)

            @block.scalar
            def _(act):
                act.sem_inc(w_hi, 2)
                act.sem_inc(act_read, na[-1])
                act.sem_inc(w_exp, NCHAIN)

                def keys(s, L, V, cc, h, d, vk):
                    act.wait_ge(vk_loaded[V], vk)
                    act.wait_ge(step_done, s + 1)
                    act.activation(ek_h[:, L, :], kt_t[:, V, :], ACT.Copy,
                                   scale=ccol[:, cc, d, 3, h:h + 1]).then_inc(ek_hi, 1)

                def split_hi(i, u):
                    act.wait_ge(w_loaded[u % 2], i * (16 * NU // 2) + 16 * (u // 2 + 1))
                    act.wait_ge(piece_done, i * NPC + (NPC + 2 * u - 2))
                    act.activation(wh[:, u % 2], wraw[:, u % 2], ACT.Copy).then_inc(w_hi, 1)

                def evacuate(i, m):
                    u, kind, e, tq = PIECES[m]
                    act.wait_ge(piece_done, i * NPC + (NPC + m + 1))
                    if kind == "o":
                        act.wait_ge(u_made, i * nz[-1] + (nz[-1] + nz[m]))
                        act.activation(tanh_o[:, tq, :], bank[m % 2][:, :], ACT.Tanh, scale=0.5).then_inc(act_read, 1)
                    elif kind == "z":
                        act.wait_ge(u_made, i * nz[-1] + (nz[-1] + nz[m]))
                        act.activation(tanh_z[:, :], bank[m % 2][:, :], ACT.Tanh, scale=0.5).then_inc(dz, 1)
                    else:
                        a = ng[m]
                        act.wait_ge(g_stored[a % 2], i * (16 * ng[-1] // 2) + (16 * (a // 2) + 1))
                        act.activation(gstage[:, a % 2, :], bank[m % 2][:, :], ACT.Tanh, scale=0.5).then_inc(act_read, 1)

                for st, (cc, h, d) in enumerate(STEPS):
                    act.wait_ge(chunk_cols, 2 * cc + 2)
                    keys(st, st % 2, st % VS, cc, h, d, 48 * (st // VS + 1))
                    if st in (6, 7):
                        split_hi(0, st - 6)

                def body(i, ahead):
                    for st, (cc, h, d) in enumerate(STEPS):
                        L, l = st % 2, i * NS + st
                        s = l + NCS
                        act.wait_ge(chunk_cols, i * 4 + (2 * cc + 6))
                        keys(s, L, st % VS, cc, h, d, i * (48 * NS // VS) + 48 * (NCS // VS + st // VS + 1))
                        act.wait_ge(nm_masked, i * 4 + (2 * cc + 2))
                        act.activation(wexp[:, L, :], nm[:, cc, d, h, :], ACT.Exp,
                                       bias=ccol[:, cc, d, 0, h:h + 1]).then_inc(w_exp, 1)
                        act.wait_ge(s_done, l + 1)
                        act.activation(s_lo[:, L, :], SBANK[:, P:2 * P], ACT.Copy).then_inc(s_copied, 1)
                        act.wait_ge(state_new, s + 1)
                        act.activation(state_h[:, L], state[:, chain(h, d)], ACT.Copy).then_inc(s_hi, 1)
                        evacuate(i, st)
                        act.wait_ge(step_done, s + 3)
                        act.activation(ysb[:, L, :], YBANK[:, 0:VW], ACT.Copy).then_inc(y_read, 1)
                        if st % 2 == 1 and (st // 2 + 2 < NU or ahead):
                            split_hi(i, st // 2 + 2)

                trips(act, body)

            @block.vector
            def _(dve):
                dve.sem_inc(w_lo, 2)
                dve.sem_inc(u_made, nz[-1])
                dve.sem_inc(state_new, NCHAIN)
                dve.sem_inc(prep, 1)
                dve.memset(f32(v_t[:, :, :, HD:VW]), 0.0).then_inc(setup, 1)
                dve.wait_ge(setup, 1)
                dve.memset(f32(v_t[:, :, 0, HD:HD + 1]), 1.0).then_inc(setup, 1)
                dve.wait_ge(cols_loaded, 16)

                def keys(s, L, V, cc, h, d):
                    dve.wait_ge(ek_hi, s + 1)
                    dve.scalar_tensor_tensor(out=ek_l[:, L, :], in0=kt_t[:, V, :], scalar=ccol[:, cc, d, 3, h:h + 1],
                                             in1=f32(ek_h[:, L, :]), op0=ALU.mult, op1=ALU.subtract).then_inc(ek_lo, 1)

                def update(s, cc, h, d, ubank=UBANK):
                    ch, decay = chain(h, d), ccol[:, cc, d, 4, h:h + 1]
                    dve.wait_ge(step_done, s + 3)
                    dve.wait_ge(state_new, s + 1)
                    for b in range(HB):
                        last = dve.scalar_tensor_tensor(out=state[:, ch, b, :], in0=state[:, ch, b, :], scalar=decay,
                                                        in1=ubank[b][:, 0:VW], op0=ALU.mult, op1=ALU.add)
                    last.then_inc(state_new, 1)

                def split_lo(i, u):
                    dve.wait_ge(w_hi, i * NU + (u + 1 + 2))
                    dve.tensor_tensor(wl[:, u % 2], wraw[:, u % 2], f32(wh[:, u % 2]), ALU.subtract).then_inc(w_lo, 1)

                def context_keys(st):
                    cc, h, d = STEPS[st]
                    if st % NCHAIN == 0:
                        for dd in range(2):
                            dve.tensor_copy(ccol[:, cc, dd], cols[:, dd, ctx_chunk(cc, dd), :]
                                            .rearrange("p (q h) -> p q h", h=HEADS)).then_inc(chunk_cols, 1)
                        dve.wait_ge(chunk_cols, 2 * cc + 2)
                    keys(st, st % 2, st % VS, cc, h, d)

                context_keys(0)
                for st, (cc, h, d) in enumerate(STEPS):
                    if st + 1 < NCS:
                        context_keys(st + 1)
                    if st == 0:
                        dve.wait_ge(state_zero, 1)
                    update(st, cc, h, d, CTX_UBANK[st % 2])
                    if st in (6, 7):
                        split_lo(0, st - 6)

                def evacuate(i, m):
                    u, kind, e, tq = PIECES[m]
                    if kind != "z":
                        return
                    a = nz[m]
                    dve.wait_ge(dz, i * nz[-1] + (a + 1))
                    dve.scalar_tensor_tensor(out=zgate[:, :], in0=tanh_z[:, :], scalar=1.0, in1=bank[m % 2][:, :],
                                             op0=ALU.add, op1=ALU.mult).then_inc(zg, 1)
                    dve.wait_ge(u_stored[a % 2], i * (16 * nz[-1] // 2) + (16 * (a // 2) + 1))
                    dve.wait_ge(zg, i * nz[-1] + (a + 1))
                    dve.scalar_tensor_tensor(out=ustage[:, a % 2, :], in0=tanh_o[:, tq, :], scalar=1.0,
                                             in1=zgate[:, :], op0=ALU.add, op1=ALU.mult).then_inc(u_made, 1)

                def prepare(i, cc):
                    n, slot = cc + 1, (cc + 1) % 2
                    dve.wait_ge(step_done, i * NS + (NCS + NCHAIN * cc + 2))
                    for dd in range(2):
                        dve.tensor_copy(ccol[:, slot, dd], cols[:, dd, bass.ds(chunk(i, n, dd), 1), :]
                                        .rearrange("p c (q h) -> p (c q) h", h=HEADS)).then_inc(chunk_cols, 1)
                    dve.wait_ge(nm_loaded[slot], i * 32 + 32 * (n // 2 + 1))
                    for dd in range(2):
                        dve.tensor_tensor(nm[:, slot, dd], nm[:, slot, dd],
                                          cmask[:, dd].unsqueeze(1).broadcast_to([P, HEADS, P]),
                                          ALU.add).then_inc(nm_masked, 1)

                def body(i, ahead):
                    for st, (cc, h, d) in enumerate(STEPS):
                        L, l = st % 2, i * NS + st
                        s = l + NCS
                        if st % NCHAIN == 0:
                            dve.wait_ge(chunk_cols, i * 4 + (2 * cc + 6))
                        keys(s, L, st % VS, cc, h, d)
                        dve.wait_ge(s_done, l + 1)
                        dve.wait_ge(w_exp, l + (1 + NCHAIN))
                        dve.wait_ge(s_copied, l + 1)
                        dve.tensor_tensor(pf[:, L, :], SBANK[:, 0:P], s_lo[:, L, :], ALU.add).then_inc(prep, 1)
                        dve.wait_ge(prep, l * PREP + 2)
                        dve.tensor_tensor(pf[:, L, :], pf[:, L, :], wexp[:, L, :], ALU.mult).then_inc(prep, 1)
                        dve.wait_ge(s_hi, l + 1)
                        dve.tensor_tensor(state_l[:, L], state[:, chain(h, d)], f32(state_h[:, L]), ALU.subtract)
                        dve.wait_ge(prep, l * PREP + 3)
                        dve.tensor_copy(p_h[:, L, :], pf[:, L, :]).then_inc(prep, 1)
                        dve.wait_ge(prep, l * PREP + 4)
                        dve.tensor_tensor(p_l[:, L, :], pf[:, L, :], f32(p_h[:, L, :]), ALU.subtract).then_inc(prep, 1)
                        if st % 2 == 0 and st > 0 and (st // 2 + 1 < NU or ahead):
                            split_lo(i, st // 2 + 1)
                        if st % NCHAIN == NCHAIN - 2 and (cc == 0 or ahead):
                            prepare(i, cc)
                        evacuate(i, st)
                        update(s, cc, h, d)
                        dve.wait_ge(y_read, l + 1)
                        dve.scalar_tensor_tensor(out=num[:, L, :], in0=XBANK[:, 0:VW], scalar=ccol[:, cc, d, 1, h:h + 1],
                                                 in1=ysb[:, L, :], op0=ALU.mult, op1=ALU.add).then_inc(fin, 1)
                        dve.wait_ge(fin, l * 5 + 1)
                        dve.tensor_scalar(den[:, L, 0:1], num[:, L, HD:HD + 1], -1.0, ccol[:, cc, d, 2, h:h + 1],
                                          ALU.mult, ALU.max).then_inc(fin, 1)
                        dve.wait_ge(fin, l * 5 + 2)
                        dve.tensor_tensor(den[:, L, 1:2], den[:, L, 0:1], num[:, L, HD:HD + 1], ALU.max).then_inc(fin, 1)
                        dve.wait_ge(fin, l * 5 + 3)
                        dve.reciprocal(den[:, L, 2:3], den[:, L, 1:2]).then_inc(fin, 1)
                        dve.wait_ge(h_stored[L], i * (16 * NS // 2) + (16 * (st // 2) + 1))
                        dve.wait_ge(fin, l * 5 + 4)
                        if half_of(i):
                            dve.tensor_scalar(hout[:, L, :], num[:, L, 0:HD], den[:, L, 2:3], None,
                                              ALU.mult).then_inc(fin, 1)
                        else:
                            dve.wait_ge(h_back[L], row(i) * (16 * NS // 2) + 16 * (st // 2 + 1))
                            dve.scalar_tensor_tensor(out=hout[:, L, :], in0=num[:, L, 0:HD], scalar=den[:, L, 2:3],
                                                     in1=hother[:, L, :], op0=ALU.mult, op1=ALU.add).then_inc(fin, 1)
                        if st == NS - 1 and ahead:
                            split_lo(i, NU + 1)

                dve.wait_ge(mask_made, 3)
                prepare(0, -1)
                trips(dve, body)

            @block.gpsimd
            def _(pool):
                made = [0]

                def link(ins):
                    made[0] += 1
                    ins.then_inc(box, 1)
                    pool.wait_ge(box, made[0])

                pool.memset(state[:, :, :, :], 0.0).then_inc(state_zero, 1)
                pool.memset(cmask[:, :, :], 0.0).then_inc(mask_made, 1)
                pool.wait_ge(mask_made, 1)
                for d in range(2):
                    sign = -1 if d == 0 else 1
                    nc.gpsimd.affine_select(out=cmask[:, d], in_=cmask[:, d], compare_op=ALU.is_ge, fill=M_INIT,
                                            base=0, pattern=[[-sign, P]], channel_multiplier=sign).then_inc(mask_made, 1)

                def inverse_counts(axis, length, w):
                    cnt = [min(n + w - w // 2, length) - max(n - w // 2, 0) for n in range(length)]
                    link(pool.memset(icnt[:, axis, 0:length], 1.0 / w))
                    for n in range(length):
                        if cnt[n] != w:
                            last = pool.memset(icnt[:, axis, n:n + 1], 1.0 / cnt[n])
                    link(last)

                def window_sums(views, length, w):
                    src, dst = views
                    step = 1
                    while step < w:
                        m = length - 2 * step + 1
                        link(pool.tensor_tensor(dst(0, m), src(0, m), src(step, m), ALU.add))
                        src, dst, step = dst, src, 2 * step
                    return src, dst

                PAD = 8
                RL, CL = GRID_H + 2 * PAD, GRID_W + 2 * PAD
                for g in range(PG):
                    w = 2 << g
                    start = PAD - w // 2
                    inverse_counts(0, GRID_H, w)
                    inverse_counts(1, GRID_W, w)
                    pool.memset(pool_a[:, 0:PAD * GRID_W], 0.0)
                    link(pool.memset(pool_a[:, (PAD + GRID_H) * GRID_W:RL * GRID_W], 0.0))
                    pool.dma_start(pool_a[:, PAD * GRID_W:(PAD + GRID_H) * GRID_W], p_d[g]).then_inc(p_loaded, 16)
                    pool.wait_ge(p_loaded, 32 * g + 16)
                    rows = [(lambda buf: lambda n, m: buf[:, n * GRID_W:(n + m) * GRID_W])(b) for b in (pool_a, pool_b)]
                    src, dst = window_sums(rows, RL, w)
                    other = pool_b if src is rows[0] else pool_a
                    this = pool_a if src is rows[0] else pool_b
                    wide = other[:, 0:GRID_H * CL].rearrange("p (r c) -> p r c", c=CL)
                    pool.memset(wide[:, :, 0:PAD], 0.0)
                    pool.memset(wide[:, :, PAD + GRID_W:CL], 0.0)
                    link(pool.tensor_tensor(wide[:, :, PAD:PAD + GRID_W],
                                            src(start, GRID_H).rearrange("p (r c) -> p r c", c=GRID_W),
                                            icnt[:, 0, 0:GRID_H].unsqueeze(2).broadcast_to([P, GRID_H, GRID_W]), ALU.mult))
                    cols_ = [(lambda buf: lambda n, m: buf[:, 0:GRID_H * CL]
                              .rearrange("p (r c) -> p r c", c=CL)[:, :, n:n + m])(b) for b in (other, this)]
                    src, dst = window_sums(cols_, CL, w)
                    end = other if src is cols_[0] else this
                    spare = this if src is cols_[0] else other
                    pool.dma_start(spare[:, 0:SEQ], p_d[g]).then_inc(p_loaded, 16)
                    res = src(start, GRID_W)
                    link(pool.tensor_tensor(res, res, icnt[:, 1, 0:GRID_W].unsqueeze(1)
                                            .broadcast_to([P, GRID_H, GRID_W]), ALU.mult))
                    pool.wait_ge(p_loaded, 32 * g + 32)
                    flat = spare[:, 0:SEQ].rearrange("p (r c) -> p r c", c=GRID_W)
                    link(pool.tensor_tensor(flat, res, flat, ALU.subtract))
                    pool.dma_start(mix_d[g], spare[:, 0:SEQ]).then_inc(mix_stored, 16)
                    pool.wait_ge(mix_stored, 16 * g + 16)

        late.close()
        with ExitStack() as ph:
            def sb(name, shape, dt=FP32):
                return ph.enter_context(nc.sbuf_tensor(name, shape, dt))

            QT = TQ // P
            WS = 3
            wraw = sb("wraw5", [P, 2, KT, P])
            wh = sb("wh5", [P, WS, KT, P], FP32R)
            wl = sb("wl5", [P, WS, KT, P], FP32R)
            pw = sb("pw", [P, PG, P])
            pw_h = sb("pw_h", [P, PG, P], FP32R)
            pw_l = sb("pw_l", [P, PG, P], FP32R)
            hw_row = sb("hw_row", [P, D])
            fn_row = sb("fn_row", [P, D])
            hsum = sb("hsum", [P, QT, D])
            ut = sb("ut", [P, 2, KT, P])
            yt = sb("yt", [P, KT, P])
            y_h = sb("y_h", [P, KT, TQ], FP32R)
            y_l = sb("y_l", [P, KT, TQ], FP32R)
            mixt = sb("mixt", [P, 2, TQ])
            mix_h = sb("mix_h", [P, 2, TQ], FP32R)
            mix_l = sb("mix_l", [P, 2, TQ], FP32R)
            zpt = sb("zpt", [P, 2, TQ])
            ypt = sb("ypt", [P, TQ])
            yp_h = sb("yp_h", [P, PG, TQ], FP32R)
            yp_l = sb("yp_l", [P, PG, TQ], FP32R)
            gmt = sb("gmt", [P, 2, TQ])
            gpt = sb("gpt", [P, 2, TQ])
            mm_ = sb("merged_m", [P, TQ])
            mp_ = sb("merged_p", [P, TQ])
            m_h = sb("m_h", [P, KT, TQ], FP32R)
            m_l = sb("m_l", [P, KT, TQ], FP32R)
            of = sb("of", [P, 2, TQ])
            xo = sb("xo", [P, QT, D])
            junk_h = sb("junk_h", [P, HD], mybir.dt.bfloat16)
            junk_o = sb("junk_o", [P, D], mybir.dt.bfloat16)
            hss = sb("hss", [P, 4, 2, HEADS])
            oss = sb("oss", [P, 4, QT])

            w_loaded = [sem(f"w5_loaded{n}") for n in range(2)]
            w_hi = sem("w5_hi"); w_lo = sem("w5_lo"); unit_done = sem("unit_done")
            rows_loaded = sem("rows_loaded"); rows_ready = sem("rows_ready")
            pw_hi = sem("pw_hi"); pw_lo = sem("pw_lo")
            h_loaded = [sem(f"h_loaded{n}") for n in range(QT)]
            u_loaded = [sem(f"u_loaded{n}") for n in range(2)]
            h_dve = sem("h_dve"); h_act = sem("h_act"); h_turned = sem("h_turned"); y_made = sem("y_made5")
            y_hi = sem("y_hi"); y_lo = sem("y_lo")
            mix_loaded = [sem(f"mix_loaded{n}") for n in range(2)]
            mix_hi = sem("mix_hi"); mix_lo = sem("mix_lo"); mix_done = sem("mix_done")
            yp_made = sem("yp_made"); yp_hi = sem("yp_hi"); yp_lo = sem("yp_lo")
            g_loaded = [sem(f"g5_loaded{n}") for n in range(2)]
            gated = sem("gated"); m_made = sem("m_made"); m_hi = sem("m_hi"); m_lo = sem("m_lo")
            of_made = sem("of_made"); o_turned = sem("o_turned"); x_loaded = sem("x5_loaded")
            x_added = sem("x_added"); o_act = sem("o_act"); o_dve = sem("o_dve"); o_ready = sem("o_ready")
            o_stored = sem("o_stored")

            UNITS = [(m, n, kt) for n in range(KT) for m, kt in (("m", KT), ("p", PG))] + [("o", n, KT) for n in range(KT)]
            NU = len(UNITS)
            SRC = {"m": branch_m_w[0].rearrange("(j p) n -> p j n", p=P),
                   "p": branch_p_w[0].rearrange("(j p) n -> p j n", p=P),
                   "o": out_w[0].rearrange("(j p) n -> p j n", p=P)}
            HSTEP = 2 + HEADS
            NORM = {1: 0, 2: 1, 3: 2, 4: 3}
            GATE = {3: 0, 4: 1, 5: 2, 6: 3}
            SPLIT = {1: 0, 3: 1, 4: 2, 6: 3}
            GROUP = {2: 0, 4: 1, 5: 2, 7: 3}
            block = ph.enter_context(nc.Block())

            def quarters(eng, out_proj, merge, last):
                with eng.Fori(0, NTQ - 1) as i:
                    out_proj(i, True)
                    merge(i + 1, True)
                out_proj(NTQ - 1, False)
                last(NTQ - 1)

            @block.sync
            def _(sp):
                sp.sem_inc(o_stored, 1)

                def tile(i, u):
                    m, n, kt = UNITS[u % NU]
                    sp.wait_ge(w_hi, i * NU + (u + 1))
                    sp.wait_ge(w_lo, i * NU + (u + 1))
                    sp.dma_start(wraw[:, u % 2, 0:kt], SRC[m][:, :, n * P:(n + 1) * P]).then_inc(w_loaded[u % 2], 16)

                def hidden(i, q):
                    if not isinstance(i, int):
                        sp.wait_ge(h_turned, i * QT + (q + 1 - QT))
                    sp.dma_start(hsum[:, q], hsum_d[i * QT + q]).then_inc(h_loaded[q], 16)

                def hidden_gate(i, q):
                    sp.wait_ge(y_made, i * QT + (q + 1))
                    sp.dma_start(ut[:, q % 2], u_d[:, :, bass.ds(i * TQ + q * P, P)].rearrange("j p t -> p j t"))\
                        .then_inc(u_loaded[q % 2], 16)

                def pooled(i, g):
                    sp.wait_ge(yp_made, i * PG + (g + 1))
                    sp.dma_start(mixt[:, g % 2], mix_d[g, :, bass.ds(i * TQ, TQ)]).then_inc(mix_loaded[g % 2], 16)
                    sp.dma_start(zpt[:, g % 2], zp_d[g, :, bass.ds(i * TQ, TQ)]).then_inc(mix_loaded[g % 2], 16)

                def gates(i, n):
                    sp.wait_ge(gated, i * (2 * KT) + (2 * n + 1))
                    sp.dma_start(gmt[:, n % 2], gm_d[n, :, bass.ds(i * TQ, TQ)]).then_inc(g_loaded[n % 2], 16)
                    sp.dma_start(gpt[:, n % 2], gp_d[n, :, bass.ds(i * TQ, TQ)]).then_inc(g_loaded[n % 2], 16)

                def store(i, q):
                    sp.wait_ge(o_ready, i * QT + (q + 1))
                    sp.dma_start(out[bass.ds(i * TQ + q * P, P), :], xo[:, q, :]).then_inc(o_stored, 16)

                def residual_x(i, q):
                    sp.dma_start(xo[:, q, :], x[bass.ds(i * TQ + q * P, P), :]).then_inc(x_loaded, 16)

                def merge(i, after):
                    for n in range(KT):
                        tile(i, 2 * n + 3)
                        tile(i, 2 * n + 4)
                        if n + 2 < KT:
                            gates(i, n + 2)
                        if n > KT - QT:
                            q = n - (KT - QT + 1)
                            if after:
                                sp.wait_ge(o_stored, (i - 1) * (16 * QT) + (16 * (q + 1) + 1))
                            residual_x(i, q)
                        if after and n >= KT - QT:
                            store(i - 1, n - (KT - QT))

                def out_proj(i, ahead):
                    for n in range(KT):
                        if n + 3 < KT or ahead:
                            tile(i, 2 * KT + n + 3)
                        if ahead:
                            for q, at in enumerate((0, 1, 2, 3)):
                                if n == at:
                                    hidden(i + 1, q)
                            for q, at in enumerate((1, 2, 4, 5)):
                                if n == at:
                                    hidden_gate(i + 1, q)
                            for g, at in enumerate((0, 1, 3, 5)):
                                if n == at:
                                    pooled(i + 1, g)
                            if n >= KT - 2:
                                gates(i + 1, n - (KT - 2))
                        if n == 0:
                            sp.wait_ge(o_stored, i * (16 * QT) + 1)
                            residual_x(i, QT - 1)

                def last(i):
                    for q in range(QT):
                        store(i, q)

                hidden(0, 0)
                sp.dma_start(pw[:, :, :], pool_w[0].rearrange("g c n -> c g n")).then_inc(rows_loaded, 16)
                sp.dma_start(hw_row[:, :], head_norm_w[0].partition_broadcast(P)).then_inc(rows_loaded, 16)
                pooled(0, 0)
                hidden(0, 1)
                hidden_gate(0, 0)
                pooled(0, 1)
                hidden(0, 2)
                hidden_gate(0, 1)
                tile(0, 0)
                hidden(0, 3)
                for q in range(2, QT):
                    pooled(0, q)
                    hidden_gate(0, q)
                    if q == 2:
                        tile(0, 1)
                for n in range(2):
                    gates(0, n)
                tile(0, 2)
                sp.dma_start(fn_row[:, :], final_norm_w.partition_broadcast(P)).then_inc(rows_loaded, 16)
                merge(0, False)
                quarters(sp, out_proj, merge, last)
                sp.wait_ge(o_stored, 16 * QT * NTQ + 1)

            @block.tensor
            def _(pe):
                pe.sem_inc(unit_done, WS)
                pe.sem_inc(o_turned, 2)
                pe.sem_inc(mix_done, 2)

                def turn_hidden(i, q):
                    t = i * QT + q
                    pe.wait_ge(h_dve, t * HSTEP + HSTEP)
                    pe.wait_ge(y_made, t + 2)
                    for j in range(KT):
                        mm = pe.transpose(bank[4 + j // 4][:, (j % 4) * P:(j % 4 + 1) * P],
                                          hsum[:, q, j * P:(j + 1) * P], ident[:, :])
                    mm.then_inc(h_turned, 1)

                def group(i, g):
                    pe.wait_ge(mix_hi, i * PG + (g + 1))
                    pe.wait_ge(mix_lo, i * PG + (g + 1))
                    pe.wait_ge(yp_made, i * PG + (g + 1))
                    pe.wait_ge(gated, i * (2 * KT) + 3)
                    for n, (a, b) in enumerate(((pw_h, mix_h), (pw_h, mix_l), (pw_l, mix_h))):
                        mm = pe.matmul(bank[2 + g % 2][:, :], a[:, g, :], b[:, g % 2, :], start=(n == 0), stop=(n == 2))
                    mm.then_inc(mix_done, 1)

                def unit(i, u):
                    m, n, kt = UNITS[u]
                    pe.wait_ge(w_hi, i * NU + (u + 3))
                    pe.wait_ge(w_lo, i * NU + (u + 3))
                    if m == "m":
                        dst, (bh, bl) = bank[n % 2], (y_h, y_l)
                        if n == 0:
                            pe.wait_ge(y_hi, i * QT + QT)
                            pe.wait_ge(y_lo, i * QT + QT)
                        if n >= 2:
                            pe.wait_ge(gated, i * (2 * KT) + (2 * n - 3 + 3))
                        else:
                            pe.wait_ge(of_made, i * KT + (n - 1 + 2))
                    elif m == "p":
                        dst, (bh, bl) = bank[2 + n % 2], (yp_h, yp_l)
                        if n == 0:
                            pe.wait_ge(yp_hi, i * PG + PG)
                            pe.wait_ge(yp_lo, i * PG + PG)
                        if n >= 2:
                            pe.wait_ge(gated, i * (2 * KT) + (2 * n - 2 + 3))
                    else:
                        dst, (bh, bl) = bank[n % 2], (m_h, m_l)
                        if n == 0:
                            pe.wait_ge(m_hi, i * KT + KT - 1)
                            pe.wait_ge(m_lo, i * KT + KT - 1)
                        if n >= 2:
                            pe.wait_ge(of_made, i * KT + (n - 1 + 2))
                        else:
                            pe.wait_ge(gated, i * (2 * KT) + (2 * (KT - 2 + n) + 1 + 3))
                    for k in range(kt):
                        if m == "o" and n == 0 and k == kt - 1:
                            pe.wait_ge(m_hi, i * KT + KT)
                            pe.wait_ge(m_lo, i * KT + KT)
                        for r, (a, b) in enumerate(((wh, bh), (wh, bl), (wl, bh))):
                            mm = pe.matmul(dst[:, :], a[:, u % WS, k, :], b[:, k, :],
                                           start=(k == 0 and r == 0), stop=(k == kt - 1 and r == 2))
                    mm.then_inc(unit_done, 1)

                def turn_output(i, n):
                    pe.wait_ge(of_made, i * KT + (n + 1 + 2))
                    pe.wait_ge(x_added, i * KT + (n + 1))
                    for q in range(QT):
                        mm = pe.transpose(bank[6 + n % 2][:, q * P:(q + 1) * P], of[:, n % 2, q * P:(q + 1) * P], ident[:, :])
                    mm.then_inc(o_turned, 1)

                def merge(i, after):
                    for u in range(2 * KT):
                        unit(i, u)
                        if after and u == 0:
                            turn_output(i - 1, KT - 1)

                def out_proj(i, ahead):
                    for n in range(KT):
                        if ahead and n in GATE:
                            turn_hidden(i + 1, GATE[n])
                        if ahead and n in GROUP:
                            group(i + 1, GROUP[n])
                        unit(i, 2 * KT + n)
                        if n >= 1:
                            turn_output(i, n - 1)

                pe.wait_ge(pw_lo, 1)
                for q in range(QT):
                    group(0, q)
                    turn_hidden(0, q)
                merge(0, False)
                quarters(pe, out_proj, merge, lambda i: turn_output(i, KT - 1))

            @block.scalar
            def _(act):
                act.sem_inc(w_hi, 2)
                act.sem_inc(of_made, 2)
                act.sem_inc(o_act, 1)

                def split_hi(i, u):
                    m, n, kt = UNITS[u % NU]
                    act.wait_ge(w_loaded[u % 2], i * (16 * NU // 2) + 16 * (u // 2 + 1))
                    act.wait_ge(unit_done, i * NU + (u - WS + 1 + WS))
                    act.activation(wh[:, u % WS, 0:kt], wraw[:, u % 2, 0:kt], ACT.Copy).then_inc(w_hi, 1)

                def squares(i, q):
                    t = i * QT + q
                    act.wait_ge(h_loaded[q], i * 16 + 16)
                    for h in range(HEADS):
                        if not (isinstance(t, int) and t == 0 and h == 0):
                            act.wait_ge(h_act, t * (HEADS + 1) + h)
                        act.activation(junk_h[:, :], hsum[:, q, h * HD:(h + 1) * HD], ACT.Square,
                                       accum_out=hss[:, 0, q % 2, h:h + 1]).then_inc(h_act, 1)
                    act.wait_ge(h_dve, t * HSTEP + 1)
                    act.activation(hss[:, 2, q % 2], hss[:, 1, q % 2], ACT.Sqrt).then_inc(h_act, 1)

                def branches_done(i):
                    if not isinstance(i, int):
                        act.wait_ge(unit_done, i * NU - (NU - 2 * KT - WS))

                def hidden_hi(i, q):
                    t = i * QT + q
                    act.wait_ge(y_made, t + 3)
                    branches_done(i)
                    act.activation(y_h[:, :, q * P:(q + 1) * P], yt[:, :, :], ACT.Copy).then_inc(y_hi, 1)

                def pooled_hi(i, g):
                    act.wait_ge(mix_loaded[g % 2], i * (32 * PG // 2) + 32 * (g // 2 + 1))
                    act.wait_ge(mix_done, i * PG + (g + 1))
                    act.activation(mix_h[:, g % 2], mixt[:, g % 2], ACT.Copy).then_inc(mix_hi, 1)

                def branch_hi(i, g):
                    act.wait_ge(yp_made, i * PG + (g + 1 + 2))
                    branches_done(i)
                    act.activation(yp_h[:, g], ypt[:, :], ACT.Copy).then_inc(yp_hi, 1)

                def output(i, n):
                    act.wait_ge(unit_done, i * NU + (2 * KT + n + 1 + WS))
                    act.wait_ge(o_turned, i * KT + (n + 1))
                    act.activation(of[:, n % 2], bank[n % 2][:, :], ACT.Copy,
                                   scale=mgate[:, n:n + 1]).then_inc(of_made, 1)

                def out_square(i, q):
                    act.wait_ge(x_added, i * KT + (KT + 2))
                    act.wait_ge(o_act, i * (QT + 1) + (q + 1))
                    act.activation(junk_o[:, :], xo[:, q], ACT.Square, accum_out=oss[:, 0, q:q + 1]).then_inc(o_act, 1)

                def out_root(i):
                    act.wait_ge(o_dve, i * 2 + 1)
                    act.activation(oss[:, 2], oss[:, 1], ACT.Sqrt).then_inc(o_act, 1)

                def merge(i, after):
                    for n in range(KT):
                        if after and n == 0:
                            output(i - 1, KT - 1)
                        split_hi(i, 2 * n + 2)
                        split_hi(i, 2 * n + 3)
                        if after and n in (1, 2):
                            out_square(i - 1, 2 * n - 2)
                            out_square(i - 1, 2 * n - 1)
                        if after and n == 3:
                            out_root(i - 1)
                        act.wait_ge(m_made, i * KT + (n + 1))
                        act.activation(m_h[:, n], mm_[:, :], ACT.Copy).then_inc(m_hi, 1)

                def out_proj(i, ahead):
                    for n in range(KT):
                        if n + 2 < KT or ahead:
                            split_hi(i, 2 * KT + n + 2)
                        if n >= 1:
                            output(i, n - 1)
                        if ahead:
                            if n in GATE:
                                hidden_hi(i + 1, GATE[n])
                            if n in SPLIT:
                                pooled_hi(i + 1, SPLIT[n])
                            if n in GROUP:
                                branch_hi(i + 1, GROUP[n])
                            if n in NORM:
                                squares(i + 1, NORM[n])

                def last(i):
                    output(i, KT - 1)
                    for q in range(QT):
                        out_square(i, q)
                    out_root(i)

                act.wait_ge(rows_loaded, 32)
                act.activation(pw_h[:, :, :], pw[:, :, :], ACT.Copy).then_inc(pw_hi, 1)
                for q in range(QT + 1):
                    if q < QT:
                        squares(0, q)
                        pooled_hi(0, q)
                    if q > 0:
                        branch_hi(0, q - 1)
                        hidden_hi(0, q - 1)
                    if q in (1, 2):
                        split_hi(0, q - 1)
                merge(0, False)
                quarters(act, out_proj, merge, last)

            @block.vector
            def _(dve):
                dve.sem_inc(w_lo, 2)
                dve.sem_inc(y_made, 2)
                dve.sem_inc(yp_made, 2)
                dve.sem_inc(gated, 3)
                dve.sem_inc(x_added, 2)

                def split_lo(i, u):
                    m, n, kt = UNITS[u % NU]
                    dve.wait_ge(w_hi, i * NU + (u + 3))
                    dve.tensor_tensor(wl[:, u % WS, 0:kt], wraw[:, u % 2, 0:kt], f32(wh[:, u % WS, 0:kt]),
                                      ALU.subtract).then_inc(w_lo, 1)

                def norms(i, q):
                    t, L = i * QT + q, q % 2
                    dve.wait_ge(h_act, t * (HEADS + 1) + HEADS)
                    dve.tensor_scalar(hss[:, 1, L], hss[:, 0, L], 1.0 / HD, EPS, ALU.mult, ALU.add).then_inc(h_dve, 1)
                    dve.wait_ge(h_act, t * (HEADS + 1) + HEADS + 1)
                    dve.reciprocal(hss[:, 3, L], hss[:, 2, L]).then_inc(h_dve, 1)
                    dve.wait_ge(h_dve, t * HSTEP + 2)
                    for h in range(HEADS):
                        s = slice(h * HD, (h + 1) * HD)
                        dve.scalar_tensor_tensor(out=hsum[:, q, s], in0=hsum[:, q, s], scalar=hss[:, 3, L, h:h + 1],
                                                 in1=hw_row[:, s], op0=ALU.mult, op1=ALU.mult).then_inc(h_dve, 1)

                def gate_hidden(i, q):
                    t = i * QT + q
                    dve.wait_ge(h_turned, t + 1)
                    dve.wait_ge(u_loaded[q % 2], i * (16 * QT // 2) + 16 * (q // 2 + 1))
                    if not (isinstance(t, int) and t == 0):
                        dve.wait_ge(y_hi, t)
                        dve.wait_ge(y_lo, t)
                    for b in range(2):
                        half = dve.tensor_tensor(yt[:, 4 * b:4 * b + 4], bank[4 + b][:, :].rearrange("p (j t) -> p j t", t=P),
                                                 ut[:, q % 2, 4 * b:4 * b + 4], ALU.mult)
                    half.then_inc(y_made, 1)

                def branch(i, g):
                    dve.wait_ge(mix_done, i * PG + (g + 1 + 2))
                    if not (isinstance(i, int) and i == 0 and g == 0):
                        dve.wait_ge(yp_hi, i * PG + g)
                        dve.wait_ge(yp_lo, i * PG + g)
                    dve.scalar_tensor_tensor(out=ypt[:, :], in0=bank[2 + g % 2][:, :],
                                             scalar=vcol[:, VR["pool"] + g:VR["pool"] + g + 1], in1=zpt[:, g % 2],
                                             op0=ALU.mult, op1=ALU.mult).then_inc(yp_made, 1)

                def residual(i, n):
                    dve.wait_ge(o_turned, i * KT + (n + 1 + 2))
                    if n == 0:
                        dve.wait_ge(x_loaded, i * (16 * QT) + 16 * QT)
                    s = slice(n * P, (n + 1) * P)
                    dve.tensor_tensor(xo[:, :, s], bank[6 + n % 2][:, :].rearrange("p (q f) -> p q f", f=P),
                                      xo[:, :, s], ALU.add).then_inc(x_added, 1)

                def out_stats(i):
                    dve.wait_ge(o_act, i * (QT + 1) + (QT + 1))
                    dve.tensor_scalar(oss[:, 1], oss[:, 0], 1.0 / D, EPS, ALU.mult, ALU.add).then_inc(o_dve, 1)
                    dve.wait_ge(o_act, i * (QT + 1) + (QT + 1 + 1))
                    dve.reciprocal(oss[:, 3], oss[:, 2]).then_inc(o_dve, 1)
                    dve.wait_ge(o_dve, i * 2 + 2)

                def out_norm(i, q):
                    dve.scalar_tensor_tensor(out=xo[:, q], in0=xo[:, q], scalar=oss[:, 3, q:q + 1], in1=fn_row[:, :],
                                             op0=ALU.mult, op1=ALU.mult).then_inc(o_ready, 1)

                def merge(i, after):
                    first = isinstance(i, int)
                    for n in range(KT):
                        split_lo(i, 2 * n + 2)
                        if after and n == 0:
                            residual(i - 1, KT - 2)
                        dve.wait_ge(g_loaded[n % 2], i * (32 * KT // 2) + 32 * (n // 2 + 1))
                        dve.wait_ge(unit_done, i * NU + (2 * n + 1 + WS))
                        if not (first and n == 0):
                            dve.wait_ge(m_hi, i * KT + n)
                            dve.wait_ge(m_lo, i * KT + n)
                        dve.scalar_tensor_tensor(out=mm_[:, :], in0=gmt[:, n % 2], scalar=1.0, in1=bank[n % 2][:, :],
                                                 op0=ALU.add, op1=ALU.mult).then_inc(gated, 1)
                        if after and n == 0:
                            residual(i - 1, KT - 1)
                        split_lo(i, 2 * n + 3)
                        if after and n == 3:
                            out_stats(i - 1)
                        if after and 3 <= n < 3 + QT:
                            out_norm(i - 1, n - 3)
                        dve.wait_ge(unit_done, i * NU + (2 * n + 2 + WS))
                        dve.scalar_tensor_tensor(out=mp_[:, :], in0=gpt[:, n % 2], scalar=1.0, in1=bank[2 + n % 2][:, :],
                                                 op0=ALU.add, op1=ALU.mult).then_inc(gated, 1)
                        dve.wait_ge(gated, i * (2 * KT) + (2 * n + 2 + 3))
                        dve.tensor_tensor(mm_[:, :], mm_[:, :], mp_[:, :], ALU.add).then_inc(m_made, 1)
                        dve.wait_ge(m_hi, i * KT + (n + 1))
                        dve.wait_ge(m_made, i * KT + (n + 1))
                        dve.tensor_tensor(m_l[:, n], mm_[:, :], f32(m_h[:, n]), ALU.subtract).then_inc(m_lo, 1)

                def out_proj(i, ahead):
                    for n in range(KT):
                        if n + 2 < KT or ahead:
                            split_lo(i, 2 * KT + n + 2)
                        if n >= 2:
                            residual(i, n - 2)
                        if ahead:
                            if n in GATE:
                                gate_hidden(i + 1, GATE[n])
                            if n in GROUP:
                                branch(i + 1, GROUP[n])
                            if n in NORM:
                                norms(i + 1, NORM[n])

                def last(i):
                    residual(i, KT - 2)
                    residual(i, KT - 1)
                    out_stats(i)
                    for q in range(QT):
                        out_norm(i, q)

                dve.wait_ge(rows_loaded, 32)
                dve.tensor_scalar(hw_row[:, :], hw_row[:, :], 0.25, None, ALU.mult).then_inc(rows_ready, 1)
                dve.wait_ge(pw_hi, 1)
                dve.tensor_tensor(pw_l[:, :, :], pw[:, :, :], f32(pw_h[:, :, :]), ALU.subtract).then_inc(pw_lo, 1)
                dve.wait_ge(rows_ready, 1)
                for q in range(QT + 1):
                    if q < QT:
                        norms(0, q)
                    if q > 0:
                        branch(0, q - 1)
                        gate_hidden(0, q - 1)
                    if q in (1, 2):
                        split_lo(0, q - 1)
                dve.wait_ge(rows_loaded, 48)
                merge(0, False)
                quarters(dve, out_proj, merge, last)

            @block.gpsimd
            def _(pool):
                def hidden_lo(i, q):
                    t = i * QT + q
                    pool.wait_ge(y_hi, t + 1)
                    pool.tensor_tensor(y_l[:, :, q * P:(q + 1) * P], yt[:, :, :], f32(y_h[:, :, q * P:(q + 1) * P]),
                                       ALU.subtract).then_inc(y_lo, 1)

                def pooled_lo(i, g):
                    pool.wait_ge(mix_hi, i * PG + (g + 1))
                    pool.tensor_tensor(mix_l[:, g % 2], mixt[:, g % 2], f32(mix_h[:, g % 2]), ALU.subtract).then_inc(mix_lo, 1)

                def branch_lo(i, g):
                    pool.wait_ge(yp_hi, i * PG + (g + 1))
                    pool.tensor_tensor(yp_l[:, g], ypt[:, :], f32(yp_h[:, g]), ALU.subtract).then_inc(yp_lo, 1)

                for q in range(QT + 1):
                    if q < QT:
                        pooled_lo(0, q)
                    if q > 0:
                        branch_lo(0, q - 1)
                        hidden_lo(0, q - 1)
                with pool.Fori(0, NTQ - 1) as i:
                    for n in range(KT):
                        if n in GATE:
                            hidden_lo(i + 1, GATE[n])
                        if n in SPLIT:
                            pooled_lo(i + 1, SPLIT[n])
                        if n in GROUP:
                            branch_lo(i + 1, GROUP[n])


_INS = ['x', 'c', 'ctx', 'c_ctx', 'norm_w', 'ada_w', 'ada_b', 'in_w', 'gate_b', 'head_norm_w', 'pool_w',
        'pool_scale', 'branch_m_w', 'branch_p_w', 'out_w', 'final_norm_w']
_OUTS = [((1, SEQ, D), 'float32')]


def kernel(**inputs):
    import numpy as _np
    import concourse.bacc as _bacc
    from concourse import mybir as _mybir
    from concourse.bass_utils import run_bass_kernel_spmd as _run

    nc = _bacc.Bacc("TRN2", target_bir_lowering=False, num_devices=1)
    arrays, args = {}, []
    for name in _INS:
        a = _np.ascontiguousarray(inputs[name])
        arrays[f"in_{name}_dram"] = a
        args.append(nc.dram_tensor(f"in_{name}_dram", a.shape, _mybir.dt.from_np(a.dtype), kind="ExternalInput").ap())
    for i, (shape, dtype) in enumerate(_OUTS):
        dt = _mybir.dt.from_np(_np.dtype(dtype))
        args.append(nc.dram_tensor(f"out_{i}_dram", shape, dt, kind="ExternalOutput").ap())
    hybrid_block(nc, *args)
    r = _run(nc, [arrays], core_ids=[0])
    return r.results[0]["out_0_dram"]
```
